# Optimizing a Trainium2 kernel written in Bass

```python
import jax, jax.numpy as jnp
from jax import lax
import numpy as np
import math

D_MODEL = 1024
BATCH = 1
SEQ = 256
DEPTH = 1

D_MIX = D_MODEL
N_MIXERS = 4
GROUP_W = D_MIX // N_MIXERS
HEAD_DIM = 64
N_HEADS_GROUP = GROUP_W // HEAD_DIM
QK_SCALE = HEAD_DIM ** -0.5
POOL_WINDOWS = (2, 4, 8, 16)
POOL_CH = GROUP_W // len(POOL_WINDOWS)
MAX_WINDOW = 16
RWKV_DECAY_LORA = 64
RWKV_A_LORA = 64
RWKV_GATE_LORA = 128
RWKV_COLS = 3 * GROUP_W + RWKV_DECAY_LORA + RWKV_A_LORA + RWKV_GATE_LORA
RWKV_GN_EPS = 64e-5
GLA_GATE_LORA = 16
GLA_GATE_TAU = 16.0
GLA_COLS = 4 * GROUP_W + GLA_GATE_LORA
CHUNK = 64
D_IN = GROUP_W + 4 * GROUP_W + RWKV_COLS + GLA_COLS
D_FF = 2816
NORM_EPS = 1e-6
GATE_FLOOR = 1e-30


def rms_norm(x, g, eps=NORM_EPS):
    xf = x.astype(jnp.float32)
    y = xf * lax.rsqrt(jnp.mean(xf * xf, axis=-1, keepdims=True) + eps)
    return (y * g.astype(jnp.float32)).astype(x.dtype)

def swiglu_ffn(x, w_in, w_out):
    gate, up = jnp.split(x @ w_in, 2, axis=-1)
    return (jax.nn.silu(gate) * up) @ w_out

def split_heads(t):
    return t.reshape(t.shape[:-1] + (N_HEADS_GROUP, HEAD_DIM))

def causal_multiscale_pool(p, w_pool, b_pool, scale):
    B, T, _ = p.shape
    cs = jnp.pad(jnp.cumsum(p, axis=1), ((0, 0), (MAX_WINDOW, 0), (0, 0)))
    pos = jnp.arange(T)
    pooled = []
    for gi, w in enumerate(POOL_WINDOWS):
        lo, hi = gi * POOL_CH, (gi + 1) * POOL_CH
        win_sum = cs[:, MAX_WINDOW:, lo:hi] - cs[:, MAX_WINDOW - w:MAX_WINDOW - w + T, lo:hi]
        count = jnp.minimum(pos + 1, w).astype(jnp.float32)[None, :, None]
        pooled.append(win_sum / count)
    pooled = jnp.stack(pooled, axis=2) - p.reshape(B, T, len(POOL_WINDOWS), POOL_CH)
    y = jnp.einsum('btgc,gcd->btgd', pooled, w_pool).reshape(B, T, GROUP_W) + b_pool
    return y * scale

def chunked_gated_linear_attention(q, k, v, log_a):
    B, T, H, K = q.shape
    V = v.shape[-1]
    n = T // CHUNK

    def to_chunks(t):
        return t.reshape(B, n, CHUNK, H, t.shape[-1]).transpose(1, 0, 3, 2, 4)

    causal = jnp.tril(jnp.ones((CHUNK, CHUNK), dtype=bool))[:, :, None]

    def step(S, inp):
        qc, kc, vc, gc = inp
        b = jnp.cumsum(gc, axis=-2)
        diff = b[:, :, :, None, :] - b[:, :, None, :, :]
        decay = jnp.where(causal, jnp.exp(jnp.where(causal, diff, 0.0)), 0.0)
        scores = jnp.einsum('bhtk,bhsk,bhtsk->bhts', qc, kc, decay)
        o = jnp.einsum('bhts,bhsv->bhtv', scores, vc) + jnp.einsum('bhtk,bhkv->bhtv', qc * jnp.exp(b), S)
        b_last = b[:, :, -1:, :]
        S_new = jnp.exp(b_last[:, :, 0, :])[..., None] * S + jnp.einsum('bhsk,bhsv->bhkv', kc * jnp.exp(b_last - b), vc)
        return S_new, o

    S0 = jnp.zeros((B, H, K, V), jnp.float32)
    _, o = lax.scan(step, S0, (to_chunks(q), to_chunks(k), to_chunks(v), to_chunks(log_a)))
    return o.transpose(1, 0, 3, 2, 4).reshape(B, T, H, V)

def rwkv7_scan(r, w, k, v, kk, a):
    B, T, H, N = r.shape

    def step(S, inp):
        r_t, w_t, k_t, v_t, kk_t, a_t = inp
        s_kk = jnp.einsum('bhvk,bhk->bhv', S, kk_t)
        S = (S * w_t[:, :, None, :] - s_kk[..., None] * (kk_t * a_t)[:, :, None, :]
             + v_t[..., :, None] * k_t[:, :, None, :])
        return S, jnp.einsum('bhvk,bhk->bhv', S, r_t)

    xs = tuple(jnp.moveaxis(t, 1, 0) for t in (r, w, k, v, kk, a))
    S0 = jnp.zeros((B, H, N, N), jnp.float32)
    _, out = lax.scan(step, S0, xs)
    return jnp.moveaxis(out, 0, 1)

def token_mixer(u, w_in, w_out, pool_w, pool_b, pool_scale, lb, hgrn_norm,
                rwkv_mu, rwkv_w0, rwkv_w2, rwkv_a0, rwkv_a2, rwkv_g2, rwkv_k_k, rwkv_k_a,
                rwkv_r_k, rwkv_ln_w, rwkv_ln_b, gla_w2, gla_b, gla_norm):
    B, T, _ = u.shape
    G = GROUP_W
    p = (u @ w_in).astype(jnp.float32)
    p_pool, p_hg, p_rw, p_gla = jnp.split(p, [G, 5 * G, 5 * G + RWKV_COLS], axis=-1)

    y_pool = causal_multiscale_pool(p_pool, pool_w, pool_b, pool_scale)

    hq, hf, hi, hg = jnp.split(p_hg, 4, axis=-1)
    f = lb + (1.0 - lb) * jax.nn.sigmoid(hf)
    log_f = jnp.log(jnp.maximum(f, GATE_FLOOR))
    o_h = chunked_gated_linear_attention(split_heads(jax.nn.silu(hq) * QK_SCALE),
                                         split_heads(1.0 - f),
                                         split_heads(hi), split_heads(log_f)).reshape(B, T, G)
    y_hgrn = rms_norm(o_h, hgrn_norm) * jax.nn.sigmoid(hg)

    prev = jnp.pad(p_rw, ((0, 0), (1, 0), (0, 0)))[:, :T]
    p_rw = p_rw + (prev - p_rw) * rwkv_mu
    rr, rk, rv, xw, xa, xg = jnp.split(
        p_rw, [G, 2 * G, 3 * G, 3 * G + RWKV_DECAY_LORA, 3 * G + RWKV_DECAY_LORA + RWKV_A_LORA], axis=-1)
    w_log = -jax.nn.softplus(-(rwkv_w0 + jnp.tanh(xw) @ rwkv_w2)) - 0.5
    decay = jnp.exp(-jnp.exp(w_log))
    a = jax.nn.sigmoid(rwkv_a0 + xa @ rwkv_a2)
    g_r = jax.nn.sigmoid(xg) @ rwkv_g2
    kk = split_heads(rk * rwkv_k_k)
    kk = kk / jnp.maximum(jnp.sqrt(jnp.sum(kk * kk, axis=-1, keepdims=True)), 1e-12)
    rk = rk * (1.0 + (a - 1.0) * rwkv_k_a)
    r_h, k_h, v_h = split_heads(rr), split_heads(rk), split_heads(rv)
    o_r = rwkv7_scan(r_h, split_heads(decay), k_h, v_h, kk, split_heads(a))
    mu = jnp.mean(o_r, axis=-1, keepdims=True)
    var = jnp.mean(jnp.square(o_r - mu), axis=-1, keepdims=True)
    gn = ((o_r - mu) * lax.rsqrt(var + RWKV_GN_EPS)).reshape(B, T, G) * rwkv_ln_w + rwkv_ln_b
    bonus = (jnp.sum(r_h * k_h * split_heads(rwkv_r_k), axis=-1, keepdims=True) * v_h).reshape(B, T, G)
    y_rwkv = (gn + bonus) * g_r

    gq, gk, gv, gg, ga = jnp.split(p_gla, [G, 2 * G, 3 * G, 4 * G], axis=-1)
    log_a = jax.nn.log_sigmoid(ga @ gla_w2 + gla_b) / GLA_GATE_TAU
    o_g = chunked_gated_linear_attention(split_heads(gq * QK_SCALE), split_heads(gk),
                                         split_heads(gv), split_heads(log_a))
    o_g = (o_g * lax.rsqrt(jnp.mean(o_g * o_g, axis=-1, keepdims=True) + NORM_EPS)).reshape(B, T, G)
    y_gla = o_g * gla_norm * jax.nn.silu(gg)

    y = jnp.concatenate([y_pool, y_hgrn, y_rwkv, y_gla], axis=-1).astype(u.dtype)
    return y @ w_out

def first_inputs(seed: int = 0) -> dict:
    key = jax.random.key(seed)
    ks = jax.random.split(key, 32)
    f32 = jnp.float32
    L, D, G = DEPTH, D_MODEL, GROUP_W

    def dense(k, shape, fan_in):
        return jax.random.normal(k, shape, f32) * fan_in ** -0.5

    def gain(k, shape):
        return 1.0 + 0.1 * jax.random.normal(k, shape, f32)

    def small(k, shape, s):
        return s * jax.random.normal(k, shape, f32)

    return {
        'x': jax.random.normal(ks[0], (BATCH, SEQ, D), f32),
        'norm_ffn1': gain(ks[1], (L, D)),
        'ffn1_w_in': dense(ks[2], (L, D, 2 * D_FF), D),
        'ffn1_w_out': dense(ks[3], (L, D_FF, D), D_FF),
        'norm_mix': gain(ks[4], (L, D)),
        'w_in': dense(ks[5], (L, D, D_IN), D),
        'w_out': dense(ks[6], (L, D_MIX, D), D_MIX),
        'pool_w': dense(ks[7], (L, len(POOL_WINDOWS), POOL_CH, POOL_CH), POOL_CH),
        'pool_b': small(ks[8], (L, G), 0.01),
        'pool_scale': gain(ks[9], (L, G)),
        'hgrn_lb_logits': small(ks[10], (L, G), 0.5),
        'hgrn_norm': gain(ks[11], (L, G)),
        'rwkv_mu': jax.random.uniform(ks[12], (L, RWKV_COLS), f32),
        'rwkv_w0': jax.random.uniform(ks[13], (L, G), f32, -4.0, 0.0),
        'rwkv_w2': dense(ks[14], (L, RWKV_DECAY_LORA, G), RWKV_DECAY_LORA),
        'rwkv_a0': small(ks[15], (L, G), 0.5),
        'rwkv_a2': dense(ks[16], (L, RWKV_A_LORA, G), RWKV_A_LORA),
        'rwkv_g2': dense(ks[17], (L, RWKV_GATE_LORA, G), RWKV_GATE_LORA),
        'rwkv_k_k': 0.85 + small(ks[18], (L, G), 0.1),
        'rwkv_k_a': gain(ks[19], (L, G)),
        'rwkv_r_k': small(ks[20], (L, G), 0.1),
        'rwkv_ln_w': gain(ks[21], (L, G)),
        'rwkv_ln_b': small(ks[22], (L, G), 0.01),
        'gla_w2': dense(ks[23], (L, GLA_GATE_LORA, G), GLA_GATE_LORA),
        'gla_b': small(ks[24], (L, G), 0.5),
        'gla_norm': gain(ks[25], (L, G)),
        'norm_ffn2': gain(ks[26], (L, D)),
        'ffn2_w_in': dense(ks[27], (L, D, 2 * D_FF), D),
        'ffn2_w_out': dense(ks[28], (L, D_FF, D), D_FF),
        'norm_final': gain(ks[29], (D,)),
    }

def first_block(x, norm_ffn1, ffn1_w_in, ffn1_w_out, norm_mix, w_in, w_out, pool_w, pool_b,
              pool_scale, hgrn_lb_logits, hgrn_norm, rwkv_mu, rwkv_w0, rwkv_w2, rwkv_a0, rwkv_a2,
              rwkv_g2, rwkv_k_k, rwkv_k_a, rwkv_r_k, rwkv_ln_w, rwkv_ln_b, gla_w2, gla_b, gla_norm,
              norm_ffn2, ffn2_w_in, ffn2_w_out, norm_final):
    sm = jax.nn.softmax(hgrn_lb_logits.astype(jnp.float32), axis=0)
    lower_bounds = jnp.cumsum(sm, axis=0) - sm[0]
    for l in range(DEPTH):
        x = x + 0.5 * swiglu_ffn(rms_norm(x, norm_ffn1[l]), ffn1_w_in[l], ffn1_w_out[l])
        x = x + token_mixer(rms_norm(x, norm_mix[l]), w_in[l], w_out[l], pool_w[l], pool_b[l],
                            pool_scale[l], lower_bounds[l], hgrn_norm[l], rwkv_mu[l], rwkv_w0[l],
                            rwkv_w2[l], rwkv_a0[l], rwkv_a2[l], rwkv_g2[l], rwkv_k_k[l], rwkv_k_a[l],
                            rwkv_r_k[l], rwkv_ln_w[l], rwkv_ln_b[l], gla_w2[l], gla_b[l], gla_norm[l])
        x = x + 0.5 * swiglu_ffn(rms_norm(x, norm_ffn2[l]), ffn2_w_in[l], ffn2_w_out[l])
    return rms_norm(x, norm_final)


DEPTH_2 = 2

N_A = DEPTH_2 // 2
N_B = DEPTH_2 - N_A
LRU_WIDTH = D_MODEL
LRU_BLOCKS = 4
LRU_BW = LRU_WIDTH // LRU_BLOCKS
CONV_W = 4
LRU_C = 8.0
N_HEADS = 16
D_ATTN = N_HEADS * HEAD_DIM
Q_BLOCK = 128
EPS = 1e-6


def rms_norm_2(x, gain):
    xf = x.astype(jnp.float32)
    y = xf * lax.rsqrt(jnp.mean(xf * xf, axis=-1, keepdims=True) + EPS)
    return (y * gain.astype(jnp.float32)).astype(x.dtype)

def swiglu(h, w13, w2):
    gate, up = jnp.split(h @ w13, 2, axis=-1)
    return (jax.nn.silu(gate) * up) @ w2

def causal_depthwise_conv(x, w, b):
    S = x.shape[1]
    xp = jnp.pad(x, ((0, 0), (CONV_W - 1, 0), (0, 0)))
    y = b
    for k in range(CONV_W):
        y = y + w[k] * xp[:, k:k + S]
    return y

def block_diag_linear(x, w, b):
    Bt, S, _ = x.shape
    xb = x.reshape(Bt, S, LRU_BLOCKS, LRU_BW)
    y = jnp.einsum('bsnc,ncd->bsnd', xb, w).reshape(Bt, S, LRU_WIDTH)
    return y + b

def linear_recurrence(a, u):
    def step(h, au):
        a_t, u_t = au
        h = a_t * h + u_t
        return h, h
    h0 = jnp.zeros((a.shape[0], a.shape[2]), jnp.float32)
    _, hs = lax.scan(step, h0, (jnp.swapaxes(a, 0, 1), jnp.swapaxes(u, 0, 1)))
    return jnp.swapaxes(hs, 0, 1)

def rglru_block(h, w_in, conv_w, conv_b, w_r, b_r, w_i, b_i, lam, w_out):
    gate_br, rec = jnp.split(h @ w_in, 2, axis=-1)
    gate_br = jax.nn.gelu(gate_br)
    xc = causal_depthwise_conv(rec, conv_w, conv_b)
    r = jax.nn.sigmoid(block_diag_linear(xc, w_r, b_r))
    i = jax.nn.sigmoid(block_diag_linear(xc, w_i, b_i))
    log_a = -LRU_C * r.astype(jnp.float32) * jax.nn.softplus(-lam.astype(jnp.float32))
    a = jnp.exp(log_a)
    mult = jnp.sqrt(-jnp.expm1(2.0 * log_a))
    u = mult * (i * xc).astype(jnp.float32)
    hs = linear_recurrence(a, u)
    y = hs.astype(h.dtype) * gate_br
    return y @ w_out

def heads(t):
    Bt, S, _ = t.shape
    return t.reshape(Bt, S, N_HEADS, HEAD_DIM).transpose(0, 2, 1, 3)

def shared_kv(x, kv_gain, w_kv, k_gain):
    hkv = rms_norm_2(x, kv_gain)
    k, v = jnp.split(hkv @ w_kv, 2, axis=-1)
    k = rms_norm_2(heads(k), k_gain)
    return k, heads(v)

def stick_breaking_attention(q, k, v):
    S = q.shape[2]
    scale = HEAD_DIM ** -0.5
    outs = []
    for blk in range(S // Q_BLOCK):
        q0 = blk * Q_BLOCK
        end = q0 + Q_BLOCK
        z = jnp.einsum('bhqd,bhkd->bhqk', q[:, :, q0:end], k[:, :, :end]).astype(jnp.float32) * scale
        t_pos = q0 + jnp.arange(Q_BLOCK)[:, None]
        s_pos = jnp.arange(end)[None, :]
        mask = s_pos < t_pos
        log_stay = jnp.where(mask, -jax.nn.softplus(z), 0.0)
        stay_after = lax.cumsum(log_stay, axis=3, reverse=True) - log_stay
        log_w = jax.nn.log_sigmoid(z) + stay_after
        w = jnp.where(mask, jnp.exp(log_w), 0.0)
        o = jnp.einsum('bhqk,bhkd->bhqd', w, v[:, :, :end].astype(jnp.float32))
        outs.append(o.astype(v.dtype))
    return jnp.concatenate(outs, axis=2)

def stick_breaking_block(h, k, v, w_q, q_gain, w_o):
    q = rms_norm_2(heads(h @ w_q), q_gain)
    o = stick_breaking_attention(q, k, v)
    Bt, _, S, _ = o.shape
    o = o.transpose(0, 2, 1, 3).reshape(Bt, S, D_ATTN)
    return o @ w_o

def second_inputs(seed: int = 0) -> dict:
    key = jax.random.key(seed)
    keys = jax.random.split(key, 32)
    counter = [0]
    f32 = jnp.float32

    def nk():
        k = keys[counter[0]]
        counter[0] += 1
        return k

    def w(shape, fan_in, scale=1.0):
        return jax.random.normal(nk(), shape, f32) * (scale * fan_in ** -0.5)

    def gain(shape):
        return 1.0 + 0.02 * jax.random.normal(nk(), shape, f32)

    def bias(shape):
        return 0.02 * jax.random.normal(nk(), shape, f32)

    a0 = jax.random.uniform(nk(), (N_A, LRU_WIDTH), f32, 0.9, 0.999)
    return {
        "x": jax.random.normal(nk(), (BATCH, SEQ, D_MODEL), f32),
        "ffn1_norm": gain((DEPTH_2, D_MODEL)),
        "ffn1_w13": w((DEPTH_2, D_MODEL, 2 * D_FF), D_MODEL),
        "ffn1_w2": w((DEPTH_2, D_FF, D_MODEL), D_FF, 0.5),
        "mix_norm": gain((DEPTH_2, D_MODEL)),
        "a_w_in": w((N_A, D_MODEL, 2 * LRU_WIDTH), D_MODEL),
        "a_conv_w": w((N_A, CONV_W, LRU_WIDTH), CONV_W),
        "a_conv_b": bias((N_A, LRU_WIDTH)),
        "a_w_r": w((N_A, LRU_BLOCKS, LRU_BW, LRU_BW), LRU_BW),
        "a_b_r": bias((N_A, LRU_WIDTH)),
        "a_w_i": w((N_A, LRU_BLOCKS, LRU_BW, LRU_BW), LRU_BW),
        "a_b_i": bias((N_A, LRU_WIDTH)),
        "a_lambda": jnp.log(a0) - jnp.log1p(-a0),
        "a_w_out": w((N_A, LRU_WIDTH, D_MODEL), LRU_WIDTH),
        "kv_norm": gain((D_MODEL,)),
        "w_kv": w((D_MODEL, 2 * D_ATTN), D_MODEL),
        "k_norm": gain((HEAD_DIM,)),
        "b_w_q": w((N_B, D_MODEL, D_ATTN), D_MODEL),
        "q_norm": gain((N_B, HEAD_DIM)),
        "b_w_o": w((N_B, D_ATTN, D_MODEL), D_ATTN),
        "ffn2_norm": gain((DEPTH_2, D_MODEL)),
        "ffn2_w13": w((DEPTH_2, D_MODEL, 2 * D_FF), D_MODEL),
        "ffn2_w2": w((DEPTH_2, D_FF, D_MODEL), D_FF, 0.5),
    }

def second_block(x, ffn1_norm, ffn1_w13, ffn1_w2, mix_norm, a_w_in, a_conv_w, a_conv_b,
              a_w_r, a_b_r, a_w_i, a_b_i, a_lambda, a_w_out, kv_norm, w_kv, k_norm,
              b_w_q, q_norm, b_w_o, ffn2_norm, ffn2_w13, ffn2_w2):
    k_shared = None
    v_shared = None
    for l in range(DEPTH_2):
        if l == N_A:
            k_shared, v_shared = shared_kv(x, kv_norm, w_kv, k_norm)
        x = x + 0.5 * swiglu(rms_norm_2(x, ffn1_norm[l]), ffn1_w13[l], ffn1_w2[l])
        h = rms_norm_2(x, mix_norm[l])
        if l < N_A:
            x = x + rglru_block(h, a_w_in[l], a_conv_w[l], a_conv_b[l], a_w_r[l], a_b_r[l],
                                a_w_i[l], a_b_i[l], a_lambda[l], a_w_out[l])
        else:
            j = l - N_A
            x = x + stick_breaking_block(h, k_shared, v_shared, b_w_q[j], q_norm[j], b_w_o[j])
        x = x + 0.5 * swiglu(rms_norm_2(x, ffn2_norm[l]), ffn2_w13[l], ffn2_w2[l])
    return x


def setup_inputs(seed=0):
    out = dict(first_inputs(seed))
    for name, value in second_inputs(seed + 1).items():
        if name != "x":
            out[name + "_2"] = value
    return out


def reference(
    x, norm_ffn1, ffn1_w_in, ffn1_w_out, norm_mix, w_in, w_out, pool_w, pool_b, pool_scale,
    hgrn_lb_logits, hgrn_norm, rwkv_mu, rwkv_w0, rwkv_w2, rwkv_a0, rwkv_a2, rwkv_g2, rwkv_k_k,
    rwkv_k_a, rwkv_r_k, rwkv_ln_w, rwkv_ln_b, gla_w2, gla_b, gla_norm, norm_ffn2, ffn2_w_in,
    ffn2_w_out, norm_final, ffn1_norm_2, ffn1_w13_2, ffn1_w2_2, mix_norm_2, a_w_in_2,
    a_conv_w_2, a_conv_b_2, a_w_r_2, a_b_r_2, a_w_i_2, a_b_i_2, a_lambda_2, a_w_out_2,
    kv_norm_2, w_kv_2, k_norm_2, b_w_q_2, q_norm_2, b_w_o_2, ffn2_norm_2, ffn2_w13_2, ffn2_w2_2,
):
    x = first_block(
        x, norm_ffn1, ffn1_w_in, ffn1_w_out, norm_mix, w_in, w_out, pool_w, pool_b, pool_scale,
        hgrn_lb_logits, hgrn_norm, rwkv_mu, rwkv_w0, rwkv_w2, rwkv_a0, rwkv_a2, rwkv_g2,
        rwkv_k_k, rwkv_k_a, rwkv_r_k, rwkv_ln_w, rwkv_ln_b, gla_w2, gla_b, gla_norm, norm_ffn2,
        ffn2_w_in, ffn2_w_out, norm_final,
    )
    return second_block(
        x, ffn1_norm_2, ffn1_w13_2, ffn1_w2_2, mix_norm_2, a_w_in_2, a_conv_w_2, a_conv_b_2,
        a_w_r_2, a_b_r_2, a_w_i_2, a_b_i_2, a_lambda_2, a_w_out_2, kv_norm_2, w_kv_2, k_norm_2,
        b_w_q_2, q_norm_2, b_w_o_2, ffn2_norm_2, ffn2_w13_2, ffn2_w2_2,
    )


_drawn_inputs = setup_inputs


def setup_inputs(seed=0):
    import zlib

    import numpy as np

    out = dict(_drawn_inputs(seed))
    spreads = {}
    factors = {'pool_b': 8.0,
     'rwkv_k_k': 4.322,
     'rwkv_ln_b': 8.0,
     'ffn1_norm_2': 8.0,
     'mix_norm_2': 4.854,
     'a_b_r_2': 8.0,
     'a_b_i_2': 8.0,
     'kv_norm_2': 14.572,
     'k_norm_2': 25.503,
     'q_norm_2': 24.534,
     'ffn2_norm_2': 8.0,
     'a_conv_b_2': 2.989}
    for name, (base, spread) in spreads.items():
        noise = np.random.default_rng([zlib.crc32(name.encode()), seed]).standard_normal(out[name].shape)
        drawn = base * np.exp(spread * noise) if base else spread * noise
        out[name] = __import__('jax').numpy.asarray(drawn.astype(out[name].dtype))
    for name, factor in factors.items():
        out[name] = (out[name] * factor).astype(out[name].dtype)
    return out
```

```python
import concourse.bass as bass
from concourse import mybir
from contextlib import ExitStack
import math

F32 = mybir.dt.float32
F32R = mybir.dt.float32r
U32 = mybir.dt.uint32
ALU = mybir.AluOpType
ACT = mybir.ActivationFunctionType

P = 128
SEQ = 256
D = 1024
KD = D // P
TB = SEQ // P
G = 256
FF = 2816
NFC = FF // P
HD = 64
QK_SCALE = HD ** -0.5
NORM_EPS = 1e-6
GATE_FLOOR = 1e-30
RWKV_GN_EPS = 64e-5
GLA_GATE_TAU = 16.0
CHUNK = 64
NCH = SEQ // CHUNK
LRU_C = 8.0
MASKED_OUT = -1e30

RING = 6
VERSIONS = 10
BLK = 1024


def plan_blocks():
    first, kinds = {}, []

    def add(phase, names):
        first[phase] = len(kinds)
        kinds.extend(names)

    ffn = ["gate", "up", "down"] * NFC
    add("ffn_a", ffn)
    add("mix_in", ["in"] * 27)
    add("mix_out", ["rows"] * 8)
    add("ffn_b", ffn)
    add("ffn_c", ffn)
    add("lru_in", ["in"] * 16)
    add("lru_gates", ["lru"] * 4)
    add("lru_out", ["rows"] * 8)
    add("ffn_d", ffn)
    add("kv", ["in"] * 8 + ["rows"] * 8)
    add("ffn_e", ffn)
    add("q_in", ["in"] * 8)
    add("attn_out", ["rows"] * 8)
    add("ffn_f", ffn)
    return first, kinds


FIRST, KINDS = plan_blocks()
NBLK = len(KINDS)
ORDER = list(FIRST)
LAST = dict(zip(ORDER, list(FIRST.values())[1:] + [NBLK]))

CONST_WIDTHS = [
    ("g_ffn_a", KD), ("g_mix", KD), ("g_ffn_b", KD), ("g_ffn_c", KD), ("g_lru", KD), ("g_ffn_d", KD),
    ("g_kv", KD), ("g_ffn_e", KD), ("g_attn", KD), ("g_ffn_f", KD),
    ("lb_logits", 2), ("hgrn_norm", 2), ("mu", 8), ("w0", 2), ("a0", 2), ("k_k", 2), ("k_a", 2), ("r_k", 2),
    ("ln_w", 2), ("ln_b", 2), ("gla_b", 2), ("gla_norm", 2), ("pool_b", 2), ("pool_scale", 2),
    ("conv_w", 4 * KD), ("conv_b", KD), ("b_r", KD), ("b_i", KD), ("lam", KD), ("k_norm", 1), ("q_norm", 1),
    ("w2a2", G), ("g2", G), ("gla_w2", G), ("pool_w", 2 * P),
    ("ident", P), ("head_ones", P), ("all_ones", P),
    ("level", 8 * P), ("level_low", 6 * P), ("strict_up", P), ("incl_up", P), ("strict_low", P),
    ("not_before", P), ("inv_count", 2 * SEQ), ("scan_one", 8 * 65),
]


def const_offsets():
    at, out = 0, {}
    for name, width in CONST_WIDTHS:
        out[name] = (at, width)
        at += width
    return out, at


CONST_AT, NCONST = const_offsets()


def slot(n):
    return n % RING


def nth(n, i=0):
    return n // RING + 1 + i


class Chain:

    def __init__(self, engine, sem):
        self.engine, self.sem, self.count, self.later = engine, sem, 0, 0

    def __call__(self, ins):
        ins.then_inc(self.sem, 1)
        self.count += 1
        self.engine.wait_ge(self.sem, self.count + self.later)


def build(nc, x_in, blocks, consts, final_gain, out):
    ctx = ExitStack()
    with ctx:
        def sb(name, shape, dt=F32):
            return ctx.enter_context(nc.sbuf_tensor(name, shape, dt))

        def sem(name):
            return ctx.enter_context(nc.semaphore(name))

        raw = sb("raw", [P, RING, BLK])
        w_hi = sb("w_hi", [P, RING, BLK], F32R)
        w_lo = sb("w_lo", [P, RING, BLK], F32R)
        x = sb("x", [P, TB, D])
        xn_hi = sb("xn_hi", [P, KD, SEQ], F32R)
        xn_lo = sb("xn_lo", [P, KD, SEQ], F32R)
        y_hi = sb("y_hi", [P, KD, SEQ], F32R)
        y_lo = sb("y_lo", [P, KD, SEQ], F32R)
        h_hi = sb("h_hi", [P, 2, SEQ], F32R)
        h_lo = sb("h_lo", [P, 2, SEQ], F32R)
        sig = sb("sig", [P, 2, SEQ])
        gs = sb("gs", [P, SEQ])
        h = sb("h", [P, SEQ])
        cst = sb("cst", [P, NCONST])
        ssq = sb("ssq", [P, TB])
        ms = sb("ms", [P, TB])
        rms = sb("rms", [P, TB])
        rstd = sb("rstd", [P, TB])
        ARENA = 17100
        arena = sb("arena", [P, ARENA])
        ps = ctx.enter_context(nc.psum_tensor("ps", [P, 8, 512], F32))

        xs = arena[:, 0:TB * D].rearrange("p (t d) -> p t d", t=TB)
        gain_row = arena[:, 4096:4096 + D]

        def const(name, i=None, width=1):
            at, w = CONST_AT[name]
            if i is None:
                return cst[:, at:at + w]
            return cst[:, at + i * width:at + (i + 1) * width]

        arrived = [sem(f"arrived{s}") for s in range(RING)]
        hi_ready = [sem(f"hi_ready{s}") for s in range(RING)]
        lo_ready = [sem(f"lo_ready{s}") for s in range(RING)]
        used = [sem(f"used{s}") for s in range(RING)]
        x_loaded = sem("x_loaded")
        const_loaded = sem("const_loaded")
        gain_loaded = sem("gain_loaded")
        stored = sem("stored")
        x_ready = sem("x_ready")
        ssq_ready = sem("ssq_ready")
        ms_ready = sem("ms_ready")
        rms_ready = sem("rms_ready")
        xs_ready = sem("xs_ready")
        xt_ready = sem("xt_ready")
        xn_hi_ready = sem("xn_hi_ready")
        xn_lo_ready = sem("xn_lo_ready")
        sig_ready = sem("sig_ready")
        h_ready = sem("h_ready")
        dve_chain = sem("dve_chain")
        act_chain = sem("act_chain")

        def xt_tile(k):
            return ps[:, 4 + k // 2, (k % 2) * SEQ:(k % 2 + 1) * SEQ]


        def carve(at, *shape):
            size = 1
            for d in shape:
                size *= d
            piece = arena[:, at:at + size]
            if len(shape) == 2:
                return piece.rearrange("p (a b) -> p a b", a=shape[0])
            if len(shape) == 3:
                return piece.rearrange("p (a b c) -> p a b c", a=shape[0], b=shape[1])
            return piece

        def over(ap, n):
            return ap.unsqueeze(1).broadcast_to([ap.shape[0], n, ap.shape[1]])

        def flat(ap):
            return ap.rearrange("p a b -> p (a b)")

        def pair(b, n=8):
            return ps[:, b:b + 2, :].rearrange("p b (m s) -> p (b m) s", m=n // 2)

        def bank(b, n=2):
            return ps[:, b, :].rearrange("p (m s) -> p m s", m=n)

        rw_raw = carve(0, 8, SEQ + 1)
        rw = carve(2056, 8, SEQ)
        gla_in = dict(q=carve(4104, 2, SEQ), k=carve(4616, 2, SEQ), v=carve(5128, 2, SEQ), gate=carve(5640, 2, SEQ))
        hgrn_in = dict(q=carve(6152, 2, SEQ), k=carve(6664, 2, SEQ), v=carve(7176, 2, SEQ), gate=carve(7688, 2, SEQ))
        PAD = 16
        pool_in = carve(8200, 2, PAD + SEQ)
        win_a = carve(8744, 2, PAD + SEQ)
        win_b = carve(9288, 2, PAD + SEQ)
        decay_to = carve(9832, 2, SEQ)
        decay_from = carve(10344, 2, SEQ)
        q_dec = [carve(10856, 2, SEQ), carve(11368, 2, SEQ)]
        k_dec = [carve(11880, 2, SEQ), carve(12392, 2, SEQ)]
        v_rows = carve(12904, 2, G)
        scores = carve(13416, 8, P)
        scores_far = carve(14440, 4, P)
        o_sb = carve(14952, 2, SEQ)
        tmp = carve(15464, 2, SEQ)
        tmp2 = carve(15976, 2, SEQ)
        norm_sb = carve(16488, 2, SEQ)
        lb = sb("lb", [P, 8])
        last_dec = sb("last_dec", [P, 8])
        ga_sb = carve(14952, SEQ)
        dec = carve(4104, 8, CHUNK + 1)
        cum = carve(4624, 8, CHUNK + 1)
        kk = carve(5144, 2, SEQ)
        iclr = carve(5656, 2, SEQ)
        k_new = carve(6168, 2, SEQ)
        inv = carve(4104, 8, P)
        inv_t = carve(5128, 8, P)
        r_dec, a_dec, b_dec, kk_dec, b_last, k_last = (carve(6680 + 512 * i, 2, SEQ) for i in range(6))
        g_r = carve(9752, 2, SEQ)
        bonus = carve(10264, 2, SEQ)
        v_tok = carve(10776, 2, G)
        a_tok = carve(2056, 2, G)
        b_tok = carve(2056 + 512, 2, G)
        k_tok = carve(2056 + 6 * SEQ, 2, G)
        l_t = carve(0, 8, P)
        lak_t = carve(1024, 8, P)
        mrb_t = carve(11288, 8, P)
        mrk_t = carve(12312, 8, P)
        y_m = carve(13336, 8, P)
        lora = carve(13336, 2, SEQ)
        sz = carve(13848, 2, SEQ)
        inv_cum = carve(11288, 2, SEQ)
        sq = carve(11800, 2, SEQ)
        lv = carve(13336, 2, G)
        w_t = carve(14360, 2, SEQ)
        u_tilde = carve(14872, 2, G)
        u = carve(15384, 2, G)
        state = [None] + [carve(15896 + 256 * i, 2, P) for i in range(3)]
        state_dec = carve(16664, 2, P)
        o_r, dev, t_r = a_dec, b_dec, kk_dec
        rms_r = carve(13336, 2, SEQ)

        ev = {name: sem(name) for name in (
            "proj_out gla_z gla_abs gla_ln gla_min gla_decay vt_done vt_out gla_qk sc_done sc_out o_done o_sq "
            "on_done on_ms on_root y_ready y_split lb_zero lb_exp hg_ready pool_ready pool_done pads "
            "rw_mixed rw_lora_in rw_lora rw_iclr rw_decay rw_g rw_kk_sq rw_kk_n rw_kk_ms rw_kk_root rw_dec "
            "rw_bonus_in rw_bonus rw_tok rw_tok_act rw_tok_out rw_mat rw_mat_out rw_y rw_ym rw_z rw_z_out rw_lv rw_lv_out "
            "rw_wt rw_ut rw_wu_out rw_u rw_u_out rw_st rw_st_out rw_o rw_o_out rw_mean rw_dev rw_var rw_gn_ms rw_gn_root").split()}

        def need(engine, name, value):
            engine.wait_ge(ev[name], value)

        TAPS = 4
        rec = carve(0, KD, TAPS - 1 + SEQ)
        xc = carve(2072, KD, SEQ)
        lru_gate = carve(4120, KD, SEQ)
        gelu_z = carve(6168, KD, SEQ)
        lru_a = carve(8216, KD, SEQ)
        lru_i = carve(10264, KD, SEQ)
        lru_h = carve(12312, KD, SEQ)
        lru_t = carve(14360, KD, SEQ)
        sp = sb("sp", [P, 4, KD])

        raw_heads = carve(4096, KD, SEQ)
        sq_heads = carve(6144, KD, SEQ)
        rms_heads = carve(8192, KD, SEQ)
        q_t = carve(2048, KD, SEQ)
        k_t = carve(13004, KD, SEQ)
        v_heads = carve(15052, TB, D)
        stick = [carve(4096 + 768 * i, 6, P) for i in range(2)]
        pass_on = [carve(5632 + 774 * i, 6, P + 1) for i in range(2)]
        left = carve(7180, 6, P + 1)
        row_end = carve(11026, 6, P + 1)
        weights = [carve(7954 + 768 * i, 6, P) for i in range(2)]
        weights_t = [carve(9490 + 768 * i, 6, P) for i in range(2)]

        for name in ("lru_abs lru_ln lru_conv lru_gate_in lru_z lru_gelu lru_gates_done lru_ri lru_sp lru_a lru_m lru_root "
                     "pad_rec heads_sq heads_n heads_ms heads_root heads_ready v_out at_z at_mask at_sig at_w at_wt "
                     "at_wt_out at_o at_yhi at_sep").split():
            ev[name] = sem(name)
        PROJ_BEFORE = {"mix_in": 0, "lru_in": 27, "kv": 43, "q_in": 51}
        block = ctx.enter_context(nc.Block())

        @block.sync
        def _(sp):
            for n in range(RING):
                if n == 0:
                    sp.dma_start(x[:, :, :], x_in).then_inc(x_loaded, 16)
                sp.dma_start(raw[:, n, :], blocks[n, :, :]).then_inc(arrived[n], 16)
                if n == 1:
                    sp.dma_start(cst[:, :], consts).then_inc(const_loaded, 16)
            rounds = NBLK // RING
            with sp.Fori(1, rounds) as r:
                for s in range(RING):
                    sp.wait_ge(lo_ready[s], r)
                    sp.dma_start(raw[:, s, :], blocks[bass.ds(r * RING + s, 1), :, :].rearrange("o p m -> p (o m)"))\
                        .then_inc(arrived[s], 16)
            for n in range(rounds * RING, NBLK):
                sp.wait_ge(lo_ready[slot(n)], n // RING)
                sp.dma_start(raw[:, slot(n), :], blocks[n, :, :]).then_inc(arrived[slot(n)], 16)
            for t in range(TB):
                sp.wait_ge(x_ready, TB * (VERSIONS - 1) + t + 1)
                sp.dma_start(out[t, :, :], x[:, t, :]).then_inc(stored, 16)
            sp.wait_ge(stored, 16 * TB)

        @block.gpsimd
        def _(pool):
            def lo(n, i=0):
                pool.wait_ge(hi_ready[slot(n)], nth(n, i))
                nc.gpsimd.tensor_tensor(w_lo[:, slot(n), :], raw[:, slot(n), :], w_hi[:, slot(n), :],
                                        ALU.subtract).then_inc(lo_ready[slot(n)], 1)

            for phase in ORDER:
                n0 = FIRST[phase]
                if phase.startswith("ffn"):
                    with pool.Fori(0, NFC // 2) as i:
                        for n in range(n0, n0 + 6):
                            if KINDS[n] != "down":
                                lo(n, i)
                else:
                    for n in range(n0, LAST[phase]):
                        lo(n)

        @block.scalar
        def _(act):
            chain = Chain(act, act_chain)
            state = {"next": 0}
            end = NBLK

            def hi(n, i=0):
                act.wait_ge(arrived[slot(n)], 16 * nth(n, i))
                if n >= RING:
                    act.wait_ge(used[slot(n)], nth(n, i) - 1)
                nc.scalar.activation(w_hi[:, slot(n), :], raw[:, slot(n), :], ACT.Copy)\
                    .then_inc(hi_ready[slot(n)], 1)

            def hi_until(n):
                while state["next"] <= min(n, end - 1):
                    hi(state["next"])
                    state["next"] += 1

            def norm(g, version):
                if version == 0:
                    act.wait_ge(x_loaded, 16)
                for t in range(TB):
                    if version:
                        act.wait_ge(x_ready, TB * (version - 1) + t + 1)
                    nc.scalar.activation(xs[:, t, :], x[:, t, :], ACT.Square, accum_out=ssq[:, t:t + 1])\
                        .then_inc(ssq_ready, 1)
                for t in range(TB):
                    act.wait_ge(ms_ready, TB * g + t + 1)
                    nc.scalar.activation(rms[:, t:t + 1], ms[:, t:t + 1], ACT.Sqrt).then_inc(rms_ready, 1)

            def norm_hi(g, gains):
                for k in range(KD):
                    act.wait_ge(xt_ready, KD * g + k // 2 * 2 + 2)
                    nc.scalar.activation(xn_hi[:, k, :], xt_tile(k), ACT.Copy, scale=const(gains, k))\
                        .then_inc(xn_hi_ready, 1)

            def ffn(f, n0):
                def sigmoid(c, ci, i):
                    up = n0 + 3 * c + 1
                    act.wait_ge(used[slot(up)], nth(up, i))
                    if f > 0 or c >= 2:
                        act.wait_ge(h_ready, NFC * f + ci - 1)
                    nc.scalar.activation(sig[:, c % 2, :], ps[:, 4 + c % 2, 0:SEQ], ACT.Sigmoid)\
                        .then_inc(sig_ready, 1)

                def tile(c, i=0):
                    sigmoid(c, c + 2 * i, i)
                    for n in (n0 + 3 * c + 5, n0 + 3 * c + 6, n0 + 3 * c + 7):
                        if n < end:
                            hi(n, i)
                tile(0)
                tile(1)
                with act.Fori(0, (NFC - 4) // 2) as i:
                    tile(2, i)
                    tile(3, i)
                tile(NFC - 2)
                tile(NFC - 1)
                state["next"] = n0 + 3 * (NFC - 1) + 8

            act.wait_ge(const_loaded, 16)
            for n in range(5):
                hi(n)
            state["next"] = 5
            def project_out(i, n, out_ap, func=ACT.Copy, parts=P, **k):
                act.wait_ge(used[slot(n)], nth(n))
                nc.scalar.activation(out_ap, ps[0:parts, 4 + i % 4, 0:SEQ], func, **k).then_inc(ev["proj_out"], 1)

            def mixer_one():
                n0 = FIRST["mix_in"]

                def tile(i, out_ap, func=ACT.Copy, **k):
                    project_out(i, n0 + i, out_ap, func, **k)
                    hi_until(n0 + i + 5)

                hi_until(n0 + 4)
                tile(0, ga_sb[0:32, :], parts=32)
                for c in range(2):
                    tile(1 + c, gla_in["q"][:, c, :], scale=QK_SCALE)
                for c in range(2):
                    tile(3 + c, gla_in["k"][:, c, :])
                need(act, "gla_abs", 1)
                nc.scalar.activation(tmp2[:, :, :], tmp2[:, :, :], ACT.Exp, scale=-1.0).then_inc(act_chain, 1)
                chain.count += 1
                act.wait_ge(act_chain, chain.count)
                nc.scalar.activation(tmp2[:, :, :], tmp2[:, :, :], ACT.Ln, bias=1.0).then_inc(ev["gla_ln"], 1)
                for c in range(2):
                    tile(5 + c, gla_in["v"][:, c, :])
                need(act, "gla_min", 1)
                nc.scalar.activation(decay_to[:, :, :], tmp[:, :, :], ACT.Exp, scale=1.0 / GLA_GATE_TAU)\
                    .then_inc(ev["gla_decay"], 1)
                need(act, "lb_zero", 1)
                nc.scalar.activation(lb[:, 2:4], lb[:, 0:2], ACT.Exp).then_inc(ev["lb_exp"], 1)
                for c in range(2):
                    tile(7 + c, gla_in["gate"][:, c, :], ACT.Silu)
                for c in range(2):
                    tile(9 + c, hgrn_in["k"][:, c, :], ACT.Sigmoid)
                for c in range(2):
                    tile(11 + c, hgrn_in["q"][:, c, :], ACT.Silu)
                for c in range(2):
                    tile(13 + c, hgrn_in["v"][:, c, :])
                for c in range(2):
                    tile(15 + c, hgrn_in["gate"][:, c, :], ACT.Sigmoid)
                need(act, "pads", 1)
                for c in range(2):
                    tile(17 + c, pool_in[:, c, PAD:])

                def root(k):
                    need(act, "on_ms", k)
                    nc.scalar.activation(norm_sb[:, :, :], norm_sb[:, :, :], ACT.Sqrt).then_inc(ev["on_root"], 1)
                root(1)
                for i in range(8):
                    tile(19 + i, rw_raw[:, i, 1:])
                root(2)
                need(act, "rw_mixed", 1)
                nc.scalar.activation(lora[0:64, 0, :], rw[0:64, 6, :], ACT.Tanh)
                nc.scalar.activation(lora[:, 1, :], rw[:, 7, :], ACT.Sigmoid).then_inc(ev["rw_lora_in"], 1)
                need(act, "rw_lora", 1)
                for c in range(2):
                    ins = nc.scalar.activation(iclr[:, c, :], bank(1)[:, c, :], ACT.Sigmoid, bias=const("a0", c))
                ins.then_inc(ev["rw_iclr"], 1)
                for c in range(2):
                    ins = nc.scalar.activation(sz[:, c, :], bank(0)[:, c, :], ACT.Sigmoid, bias=const("w0", c))
                chain(ins)
                nc.scalar.activation(dec[:, :, 1:], flat(sz).rearrange("p (a b) -> p a b", b=CHUNK), ACT.Exp,
                                     scale=-float(math.exp(-0.5))).then_inc(ev["rw_decay"], 1)
                nc.scalar.activation(g_r[:, :, :], bank(2), ACT.Copy).then_inc(ev["rw_g"], 1)
                need(act, "rw_kk_n", 1)
                nc.scalar.activation(sq[:, :, :], bank(3), ACT.Sqrt).then_inc(ev["rw_kk_root"], 1)
                need(act, "rw_tok", 2)
                nc.scalar.activation(b_tok[:, :, :], bank(5), ACT.Copy).then_inc(ev["rw_tok_act"], 1)
                need(act, "rw_tok", 3)
                nc.scalar.activation(k_tok[:, :, :], bank(6), ACT.Copy).then_inc(ev["rw_tok_act"], 1)
                hi_until(FIRST["mix_out"] + 5)
                need(act, "rw_gn_ms", 1)
                nc.scalar.activation(rms_r[:, :, :], rms_r[:, :, :], ACT.Sqrt).then_inc(ev["rw_gn_root"], 1)
                hi_until(FIRST["mix_out"] + 8 + 4)

            def load_gain():
                act.wait_ge(x_ready, 2 * TB)
                act.dma_start(gain_row, final_gain).then_inc(gain_loaded, 16)

            def lru():
                n0 = FIRST["lru_in"]
                need(act, "lru_abs", 1)
                chain(nc.scalar.activation(sp[:, 1, :], sp[:, 0, :], ACT.Exp, scale=-1.0))
                nc.scalar.activation(sp[:, 1, :], sp[:, 1, :], ACT.Ln, bias=1.0).then_inc(ev["lru_ln"], 1)
                need(act, "pad_rec", 1)
                for i in range(KD):
                    project_out(i, n0 + i, rec[:, i, TAPS - 1:])
                    hi_until(n0 + i + 5)
                for i in range(KD, 2 * KD):
                    project_out(i, n0 + i, lru_gate[:, i - KD, :])
                    hi_until(n0 + i + 5)
                for half in range(2):
                    need(act, "lru_z", half + 1)
                    fours = slice(4 * half, 4 * half + 4)
                    nc.scalar.activation(gelu_z[:, fours, :], gelu_z[:, fours, :], ACT.Sigmoid,
                                         scale=2 * math.sqrt(2 / math.pi)).then_inc(ev["lru_gelu"], 1)
                for i in range(KD):
                    n = FIRST["lru_gates"] + i // 2
                    if i % 2:
                        act.wait_ge(used[slot(n)], nth(n))
                    else:
                        need(act, "lru_gates_done", i // 2 + 1)
                    nc.scalar.activation(lru_a[:, i, :], bank(4 + i % 4)[:, 0, :], ACT.Sigmoid, bias=const("b_r", i))
                    nc.scalar.activation(lru_i[:, i, :], bank(4 + i % 4)[:, 1, :], ACT.Sigmoid, bias=const("b_i", i))\
                        .then_inc(ev["lru_ri"], 1)
                    hi_until(FIRST["lru_gates"] + i // 2 + 5)
                act.wait_ge(ev["lru_ri"], KD)
                need(act, "lru_sp", 1)
                for half in range(2):
                    for i in range(4 * half, 4 * half + 4):
                        ins = nc.scalar.activation(lru_t[:, i, :], lru_a[:, i, :], ACT.Tanh, scale=sp[:, 3, i:i + 1])
                    chain(ins)
                    for i in range(4 * half, 4 * half + 4):
                        ins = nc.scalar.activation(lru_a[:, i, :], lru_a[:, i, :], ACT.Exp, scale=sp[:, 2, i:i + 1])
                    ins.then_inc(ev["lru_a"], 1)
                for half in range(2):
                    fours = slice(4 * half, 4 * half + 4)
                    need(act, "lru_m", half + 1)
                    nc.scalar.activation(lru_t[:, fours, :], lru_t[:, fours, :], ACT.Sqrt).then_inc(ev["lru_root"], 1)
                hi_until(FIRST["lru_out"] + 8 + 4)

            def heads_root(k):
                need(act, "heads_ms", k)
                nc.scalar.activation(rms_heads[:, :, :], rms_heads[:, :, :], ACT.Sqrt).then_inc(ev["heads_root"], 1)

            def shared_kv():
                n0 = FIRST["kv"]
                for i in range(KD):
                    project_out(i, n0 + i, raw_heads[:, i, :])
                    hi_until(n0 + i + 5)
                hi_until(n0 + KD + 5)
                heads_root(1)
                hi_until(n0 + 2 * KD - 1)
                act.wait_ge(used[slot(n0 + 2 * KD - 1)], nth(n0 + 2 * KD - 1))
                for t in range(TB):
                    ins = nc.scalar.activation(v_heads[:, t, :], ps[:, 2 * t:2 * t + 2, :].rearrange("p b s -> p (b s)"), ACT.Copy)
                ins.then_inc(ev["v_out"], 1)
                hi_until(n0 + 2 * KD + 4)

            def attention():
                n0 = FIRST["q_in"]
                for i in range(KD):
                    project_out(i, n0 + i, raw_heads[:, i, :])
                    hi_until(n0 + i + 5)
                hi_until(n0 + KD + 5)
                heads_root(2)
                need(act, "at_sep", 1)
                for step in range(KD + 2):
                    if step < KD:
                        c = step
                        need(act, "at_mask", c + 1)
                        z = ps[:, 2 * (c % 2):2 * (c % 2) + 2, 0:3 * P].rearrange("p b (m s) -> p b m s", m=3)
                        if c >= 2:
                            need(act, "at_w", c - 1)
                        for out_ap, scale in ((stick[c % 2][:, :, :], QK_SCALE), (pass_on[c % 2][:, :, 0:P], -QK_SCALE)):
                            ins = nc.scalar.activation(out_ap.rearrange("p (b m) s -> p b m s", b=2), z, ACT.Sigmoid, scale=scale)
                        ins.then_inc(ev["at_sig"], 1)
                    if 0 <= step - 1 < KD:
                        c = step - 1
                        need(act, "at_wt", c + 1)
                        nc.scalar.activation(weights_t[c % 2][:, :, :].rearrange("p (b m) s -> p b (m s)", b=2),
                                             ps[:, 4:6, 0:3 * P], ACT.Copy).then_inc(ev["at_wt_out"], 1)
                    if 0 <= step - 2 < KD:
                        c = step - 2
                        need(act, "at_o", c + 1)
                        nc.scalar.activation(y_hi[:, c, :], bank(6 + c % 2)[:, 0, :], ACT.Copy).then_inc(ev["at_yhi"], 1)
                hi_until(FIRST["attn_out"] + 8 + 4)

            steps = [
                lambda: (norm(0, 0), norm_hi(0, "g_ffn_a")),
                lambda: ffn(0, FIRST["ffn_a"]),
                lambda: (norm(1, 1), norm_hi(1, "g_mix"), mixer_one()),
                lambda: (load_gain(), norm(2, 2), norm_hi(2, "g_ffn_b"), hi_until(FIRST["ffn_b"] + 4)),
                lambda: ffn(1, FIRST["ffn_b"]),
                lambda: norm(3, 3),
                lambda: (norm(4, 4), norm_hi(3, "g_ffn_c"), ffn(2, FIRST["ffn_c"])),
                lambda: (norm(5, 5), norm_hi(4, "g_lru"), lru()),
                lambda: (norm(6, 6), norm_hi(5, "g_ffn_d"), ffn(3, FIRST["ffn_d"])),
                lambda: (norm(7, 7), norm_hi(6, "g_kv"), shared_kv()),
                lambda: (norm_hi(7, "g_ffn_e"), ffn(4, FIRST["ffn_e"])),
                lambda: (norm(8, 8), norm_hi(8, "g_attn"), attention()),
                lambda: (norm(9, 9), norm_hi(9, "g_ffn_f"), ffn(5, FIRST["ffn_f"])),
            ]
            for step in steps:
                step()

        @block.vector
        def _(v):
            chain = Chain(v, dve_chain)
            x_tiles = [0]

            def lo(n, i=0):
                v.wait_ge(hi_ready[slot(n)], nth(n, i))
                nc.vector.tensor_tensor(w_lo[:, slot(n), :], raw[:, slot(n), :], w_hi[:, slot(n), :],
                                        ALU.subtract).then_inc(lo_ready[slot(n)], 1)

            def norm(g):
                for t in range(TB):
                    v.wait_ge(ssq_ready, TB * g + t + 1)
                    nc.vector.tensor_scalar(ms[:, t:t + 1], ssq[:, t:t + 1], 1.0 / D, NORM_EPS, ALU.mult, ALU.add)\
                        .then_inc(ms_ready, 1)
                for t in range(TB):
                    v.wait_ge(rms_ready, TB * g + t + 1)
                    chain(nc.vector.reciprocal(rstd[:, t:t + 1], rms[:, t:t + 1]))

            def norm_rows(g):
                norm(g)
                for t in range(TB):
                    nc.vector.tensor_scalar(xs[:, t, :], x[:, t, :], rstd[:, t:t + 1], None, ALU.mult)\
                        .then_inc(xs_ready, 1)

            def norm_lo(g, gains):
                for k in range(KD):
                    v.wait_ge(xn_hi_ready, KD * g + k // 2 * 2 + 2)
                    nc.vector.scalar_tensor_tensor(xn_lo[:, k, :], xt_tile(k), const(gains, k), xn_hi[:, k, :],
                                                   ALU.mult, ALU.subtract).then_inc(xn_lo_ready, 1)

            def ffn(f, n0):
                def hidden(c, ci, i):
                    v.wait_ge(sig_ready, NFC * f + ci + 1)
                    chain(nc.vector.tensor_tensor(gs[:, :], ps[:, 4 + c % 2, 0:SEQ], sig[:, c % 2, :], ALU.mult))
                    if c >= 2:
                        down = n0 + 3 * c - 4
                        v.wait_ge(used[slot(down)], nth(down, i))
                    nc.vector.tensor_tensor(h_hi[:, c % 2, :], ps[:, 4 + c % 2, SEQ:], gs[:, :], ALU.mult)
                    chain(nc.vector.tensor_tensor(h[:, :], ps[:, 4 + c % 2, SEQ:], gs[:, :], ALU.mult))
                    nc.vector.tensor_tensor(h_lo[:, c % 2, :], h[:, :], h_hi[:, c % 2, :], ALU.subtract)\
                        .then_inc(h_ready, 1)
                    v.wait_ge(h_ready, NFC * f + ci + 1)

                def tile(c, i=0):
                    hidden(c, c + 2 * i, i)
                    if c + 1 < NFC:
                        lo(n0 + 3 * c + 5, i)
                lo(n0 + 2)
                tile(0)
                tile(1)
                trips = (NFC - 4) // 2
                count = chain.count
                with v.Fori(0, trips) as i:
                    chain.later = i * 4
                    tile(2, i)
                    tile(3, i)
                assert chain.count == count + 4
                chain.count, chain.later = count + 4 * trips, 0
                tile(NFC - 2)
                tile(NFC - 1)
                down = n0 + 3 * NFC - 1
                v.wait_ge(used[slot(down)], nth(down))

            def add_to_x(scale):
                for t in range(TB):
                    for c in range(2):
                        ins = nc.vector.scalar_tensor_tensor(x[:, t, 512 * c:512 * c + 512], ps[:, 2 * t + c, :], scale,
                                                             x[:, t, 512 * c:512 * c + 512], ALU.mult, ALU.add)
                        if c == 0:
                            chain(ins)
                    ins.then_inc(x_ready, 1)
                    x_tiles[0] += 1
                    v.wait_ge(x_ready, x_tiles[0])

            def gain_x(g):
                norm(g)
                v.wait_ge(gain_loaded, 16)
                for t in range(TB):
                    nc.vector.scalar_tensor_tensor(x[:, t, :], x[:, t, :], rstd[:, t:t + 1], gain_row,
                                                   ALU.mult, ALU.mult).then_inc(x_ready, 1)
                    x_tiles[0] += 1
                    v.wait_ge(x_ready, x_tiles[0])

            def signal(ins, name):
                ins.then_inc(ev[name], 1)
                sent[name] = sent.get(name, 0) + 1
                v.wait_ge(ev[name], sent[name])

            sent = {}
            tt = nc.vector.tensor_tensor
            stt = nc.vector.scalar_tensor_tensor
            tsc = nc.vector.tensor_scalar

            def split_y(tile, make, scratch):
                make(y_hi[:, tile, :])
                chain(make(scratch))
                signal(tt(y_lo[:, tile, :], scratch, y_hi[:, tile, :], ALU.subtract), "y_ready")

            def value_rows(k):
                need(v, "vt_done", k)
                signal(nc.vector.tensor_copy(v_rows[:, :, :], bank(2)), "vt_out")

            def decayed_attention(src, k):
                chain(nc.vector.memset(decay_from[:, :, :], 1.0))
                chain(nc.vector.memset(scores[:, :, :], 0.0))
                for lev in range(8):
                    n = 1 << lev
                    b = lev % 2
                    chain(tt(q_dec[b][:, :, :], src["q"][:, :, :], decay_to[:, :, :], ALU.mult))
                    signal(tt(k_dec[b][:, :, :], src["k"][:, :, :], decay_from[:, :, :], ALU.mult), "gla_qk")
                    if n < P:
                        to, frm = (flat(a).rearrange("p (m e s) -> p m e s", e=2, s=n) for a in (decay_to, decay_from))
                        m = 2 * SEQ // (2 * n)
                        chain(tt(frm[:, :, 0, :], frm[:, :, 0, :], to[:, :, 1, n - 1:n].broadcast_to([P, m, n]), ALU.mult))
                        chain(tt(to[:, :, 1, :], to[:, :, 1, :], to[:, :, 0, n - 1:n].broadcast_to([P, m, n]), ALU.mult))
                    take_level(lev, k)
                take_level(8, k)

            def take_level(lev, k):
                need(v, "sc_done", 9 * (k - 1) + lev + 1)
                b = 2 * (lev % 2)
                if lev < 8:
                    mask = over(const("level", lev, P), 8).bitcast(U32)
                    signal(nc.vector.copy_predicated(scores[:, :, :], mask, pair(b)), "sc_out")
                else:
                    signal(nc.vector.tensor_copy(scores_far[:, :, :].rearrange("p (j c) t -> p j (c t)", j=2),
                                                 ps[:, b:b + 2, 0:2 * P]), "sc_out")

            def attended(k, per_head):
                need(v, "o_done", k)
                chain(nc.vector.tensor_copy(o_sb[:, :, :], bank(2)))
                signal(tt(tmp[:, :, :], o_sb[:, :, :], o_sb[:, :, :], ALU.mult), "o_sq")
                need(v, "on_done", k)
                if per_head:
                    signal(tsc(norm_sb[:, :, :], bank(3), 1.0 / HD, NORM_EPS, ALU.mult, ALU.add), "on_ms")
                else:
                    for c in range(2):
                        ins = tsc(norm_sb[:, c, :], bank(3)[:, 0, :], 1.0 / G, NORM_EPS, ALU.mult, ALU.add)
                    signal(ins, "on_ms")
                need(v, "on_root", k)
                chain(nc.vector.reciprocal(norm_sb[:, :, :], norm_sb[:, :, :]))
                chain(tt(o_sb[:, :, :], o_sb[:, :, :], norm_sb[:, :, :], ALU.mult))

            def pooling():
                for c in range(2):
                    need(v, "proj_out", 18 + c)
                previous = pool_in
                for step, group in ((1, 0), (2, 1), (4, 2), (8, 3)):
                    now = win_a if group % 2 == 0 else win_b
                    chain(tt(now[:, :, PAD:], previous[:, :, PAD:], previous[:, :, PAD - step:PAD + SEQ - step], ALU.add))
                    c, rows = group // 2, slice(HD * (group % 2), HD * (group % 2) + HD)
                    chain(tt(tmp[rows, c, :], now[rows, c, PAD:],
                             const("inv_count", c, SEQ)[rows, :], ALU.mult))
                    ins = tt(tmp[rows, c, :], tmp[rows, c, :], pool_in[rows, c, PAD:], ALU.subtract)
                    if group < 3:
                        chain(ins)
                    previous = now
                signal(ins, "pool_ready")
                need(v, "pool_done", 1)
                for c in range(2):
                    split_y(c, lambda out: tsc(out, bank(2)[:, c, :], const("pool_b", c), const("pool_scale", c),
                                               ALU.add, ALU.mult), tmp2[:, c, :])

            def mixer_one():
                chain(nc.vector.memset(rw_raw[:, :, 0:1], 0.0))
                for buf in (pool_in, win_a):
                    chain(nc.vector.memset(buf[:, :, 0:PAD], 0.0))
                signal(nc.vector.memset(win_b[:, :, 0:PAD], 0.0), "pads")
                logits = const("lb_logits")
                signal(tt(lb[:, 0:2], logits, logits, ALU.subtract), "lb_zero")
                need(v, "gla_z", 1)
                for c in range(2):
                    chain(tsc(tmp[:, c, :], bank(3)[:, c, :], const("gla_b", c), None, ALU.add))
                signal(stt(tmp2[:, :, :], tmp[:, :, :], -1.0, tmp[:, :, :], ALU.mult, ALU.max), "gla_abs")
                need(v, "gla_ln", 1)
                signal(stt(tmp[:, :, :], tmp[:, :, :], 0.0, tmp2[:, :, :], ALU.min, ALU.subtract), "gla_min")
                need(v, "lb_exp", 1)
                chain(nc.vector.reciprocal(lb[:, 4:6], lb[:, 2:4]))
                chain(tt(lb[:, 4:6], lb[:, 4:6], lb[:, 2:4], ALU.mult))
                chain(tt(lb[:, 6:8], lb[:, 4:6], lb[:, 4:6], ALU.subtract))
                chain(tsc(lb[:, 0:2], lb[:, 6:8], -1.0, 1.0, ALU.mult, ALU.add))
                need(v, "proj_out", 7)
                value_rows(1)
                need(v, "gla_decay", 1)
                decayed_attention(gla_in, 1)
                attended(1, True)
                need(v, "proj_out", 9)
                for c in range(2):
                    split_y(6 + c, lambda out: stt(out, o_sb[:, c, :], const("gla_norm", c), gla_in["gate"][:, c, :],
                                                   ALU.mult, ALU.mult), tmp[:, c, :])
                need(v, "proj_out", 17)
                value_rows(2)
                for c in range(2):
                    chain(tsc(tmp[:, c, :], hgrn_in["k"][:, c, :], lb[:, c:c + 1], lb[:, 6 + c:7 + c], ALU.mult, ALU.add))
                chain(tsc(hgrn_in["k"][:, :, :], tmp[:, :, :], -1.0, 1.0, ALU.mult, ALU.add))
                chain(tsc(decay_to[:, :, :], tmp[:, :, :], GATE_FLOOR, None, ALU.max))
                signal(tsc(hgrn_in["q"][:, :, :], hgrn_in["q"][:, :, :], QK_SCALE, None, ALU.mult), "hg_ready")
                decayed_attention(hgrn_in, 2)
                attended(2, False)
                for c in range(2):
                    split_y(2 + c, lambda out: stt(out, o_sb[:, c, :], const("hgrn_norm", c), hgrn_in["gate"][:, c, :],
                                                   ALU.mult, ALU.mult), tmp[:, c, :])
                pooling()
                rwkv()
                last = FIRST["mix_out"] + 7
                v.wait_ge(used[slot(last)], nth(last))

            def rwkv():
                need(v, "proj_out", 27)
                chain(tt(rw[:, :, :], rw_raw[:, :, 0:SEQ], rw_raw[:, :, 1:], ALU.subtract))
                for i in (6, 7, 0, 1, 2, 3, 4, 5):
                    ins = stt(rw[:, i, :], rw[:, i, :], const("mu", i), rw_raw[:, i, 1:], ALU.mult, ALU.add)
                    if i == 7:
                        signal(ins, "rw_mixed")
                chain(ins)
                r_in, k_in, v_in = rw[:, 0:2, :], rw[:, 2:4, :], rw[:, 4:6, :]
                chain(nc.vector.memset(dec[:, :, 0:1], 0.0))
                for c in range(2):
                    chain(tsc(kk[:, c, :], k_in[:, c, :], const("k_k", c), None, ALU.mult))
                signal(tt(sq[:, :, :], kk[:, :, :], kk[:, :, :], ALU.mult), "rw_kk_sq")
                need(v, "rw_iclr", 1)
                for c in range(2):
                    chain(tsc(k_new[:, c, :], iclr[:, c, :], -1.0, const("k_a", c), ALU.add, ALU.mult))
                chain(stt(k_new[:, :, :], k_new[:, :, :], 1.0, k_in, ALU.add, ALU.mult))
                need(v, "rw_kk_root", 1)
                chain(tsc(sq[:, :, :], sq[:, :, :], 1e-12, None, ALU.max))
                chain(nc.vector.reciprocal(sq[:, :, :], sq[:, :, :]))
                chain(tt(kk[:, :, :], kk[:, :, :], sq[:, :, :], ALU.mult))
                need(v, "rw_decay", 1)
                chain(nc.vector.tensor_tensor_scan(flat(cum), flat(dec), const("scan_one"), 0.0, ALU.mult, ALU.add))

                def by_chunk(ap):
                    return ap.rearrange("p c (q s) -> p (c q) s", s=CHUNK)
                after, before = cum[:, :, 1:], cum[:, :, 0:CHUNK]
                last = cum[:, :, CHUNK:].broadcast_to([P, 8, CHUNK])
                chain(nc.vector.tensor_copy(last_dec[:, :], cum[:, :, CHUNK:].rearrange("p a b -> p (a b)")))
                chain(nc.vector.reciprocal(by_chunk(inv_cum), after))
                chain(tt(by_chunk(r_dec), by_chunk(r_in), after, ALU.mult))
                signal(tt(by_chunk(a_dec), by_chunk(kk), before, ALU.mult), "rw_dec")
                chain(tt(b_dec[:, :, :], kk[:, :, :], iclr[:, :, :], ALU.mult))
                chain(tt(b_dec[:, :, :], b_dec[:, :, :], inv_cum[:, :, :], ALU.mult))
                signal(tt(by_chunk(b_last), by_chunk(b_dec), last, ALU.mult), "rw_dec")
                chain(tt(kk_dec[:, :, :], k_new[:, :, :], inv_cum[:, :, :], ALU.mult))
                signal(tt(by_chunk(k_last), by_chunk(kk_dec), last, ALU.mult), "rw_dec")
                for c in range(2):
                    ins = stt(sq[:, c, :], r_in[:, c, :], const("r_k", c), k_new[:, c, :], ALU.mult, ALU.mult)
                signal(ins, "rw_bonus_in")
                need(v, "rw_tok", 1)
                chain(nc.vector.tensor_copy(a_tok[:, :, :], bank(4)))
                need(v, "rw_tok", 4)
                signal(nc.vector.tensor_copy(v_tok[:, :, :], bank(7)), "rw_tok_out")
                need(v, "rw_bonus", 1)
                chain(tt(bonus[:, :, :], bank(3), v_in, ALU.mult))
                need(v, "rw_mat", 1)
                signal(tt(l_t[:, :, :], pair(0), over(const("strict_up"), 8), ALU.mult), "rw_mat_out")
                need(v, "rw_mat", 2)
                signal(stt(inv[:, :, :], pair(4), -1.0, over(const("level_low", 0, P), 8), ALU.mult, ALU.mult), "rw_mat_out")
                chain(tt(inv[:, :, :], inv[:, :, :], over(const("ident"), 8), ALU.add))
                chain(stt(inv_t[:, :, :], l_t[:, :, :], -1.0, over(const("level", 1, P), 8), ALU.mult, ALU.mult))
                signal(tt(inv_t[:, :, :], inv_t[:, :, :], over(const("ident"), 8), ALU.add), "rw_z_out")
                need(v, "rw_mat", 3)
                signal(tt(lak_t[:, :, :], pair(0), over(const("strict_up"), 8), ALU.mult), "rw_mat_out")
                need(v, "rw_mat", 4)
                signal(tt(mrb_t[:, :, :], pair(2), over(const("incl_up"), 8), ALU.mult), "rw_mat_out")
                need(v, "rw_mat", 5)
                signal(tt(mrk_t[:, :, :], pair(0), over(const("incl_up"), 8), ALU.mult), "rw_mat_out")
                need(v, "rw_lv", 1)
                for lev in range(1, 6):
                    for j in range(2):
                        half = slice(4 * j, 4 * j + 4)
                        need(v, "rw_y", 2 * (lev - 1) + j + 1)
                        signal(tt(y_m[:, half, :], bank(j, 4), over(const("level_low", lev, P), 4), ALU.mult), "rw_ym")
                    for j in range(2):
                        half = slice(4 * j, 4 * j + 4)
                        need(v, "rw_z", 2 * (lev - 1) + j + 1)
                        if lev < 5:
                            chain(tt(inv[:, half, :], inv[:, half, :], bank(2 + j, 4), ALU.subtract))
                        signal(tt(inv_t[:, half, :], inv_t[:, half, :], bank(4 + j, 4), ALU.subtract), "rw_z_out")
                signal(nc.vector.tensor_copy(lv[:, :, :], bank(6)), "rw_lv_out")
                need(v, "rw_wt", 1)
                chain(nc.vector.tensor_copy(w_t[:, :, :], bank(0)))
                need(v, "rw_ut", 1)
                signal(nc.vector.tensor_copy(u_tilde[:, :, :], bank(1)), "rw_wu_out")
                for q in range(NCH):
                    rows, t = slice(CHUNK * (q % 2), CHUNK * (q % 2) + CHUNK), q // 2
                    if q == 0:
                        signal(tsc(u[rows, t, :], u_tilde[rows, t, :], -1.0, None, ALU.mult), "rw_u_out")
                    else:
                        need(v, "rw_u", q)
                        signal(stt(u[rows, t, :], ps[rows, 2 + q % 2, 0:G], -1.0, u_tilde[rows, t, :],
                                   ALU.mult, ALU.subtract), "rw_u_out")
                    if q + 1 < NCH:
                        if q:
                            for c in range(2):
                                chain(tsc(state_dec[:, c, :], state[q][:, c, :], last_dec[:, 4 * c + q:4 * c + q + 1],
                                          None, ALU.mult))
                        need(v, "rw_st", q + 1)
                        new = ps[:, 4 + q % 2, 0:2 * P].rearrange("p (c s) -> p c s", c=2)
                        ins = tt(state[q + 1][:, :, :], new, over(const("head_ones"), 2), ALU.mult)
                        if q:
                            chain(ins)
                            ins = tt(state[q + 1][:, :, :], state[q + 1][:, :, :], state_dec[:, :, :], ALU.add)
                        signal(ins, "rw_st_out")
                need(v, "rw_o", 1)
                signal(nc.vector.tensor_copy(o_r[:, :, :], bank(6)), "rw_o_out")
                need(v, "rw_mean", 1)
                chain(stt(dev[:, :, :], bank(4), -1.0 / HD, o_r[:, :, :], ALU.mult, ALU.add))
                signal(tt(t_r[:, :, :], dev[:, :, :], dev[:, :, :], ALU.mult), "rw_dev")
                need(v, "rw_var", 1)
                signal(tsc(rms_r[:, :, :], bank(5), 1.0 / HD, RWKV_GN_EPS, ALU.mult, ALU.add), "rw_gn_ms")
                need(v, "rw_gn_root", 1)
                chain(nc.vector.reciprocal(rms_r[:, :, :], rms_r[:, :, :]))
                chain(tt(dev[:, :, :], dev[:, :, :], rms_r[:, :, :], ALU.mult))
                for c in range(2):
                    chain(tsc(dev[:, c, :], dev[:, c, :], const("ln_w", c), const("ln_b", c), ALU.mult, ALU.add))
                chain(tt(dev[:, :, :], dev[:, :, :], bonus[:, :, :], ALU.add))
                need(v, "rw_g", 1)
                for c in range(2):
                    split_y(4 + c, lambda out: tt(out, dev[:, c, :], g_r[:, c, :], ALU.mult), t_r[:, c, :])

            def lru():
                signal(nc.vector.memset(rec[:, :, 0:TAPS - 1], 0.0), "pad_rec")
                signal(stt(sp[:, 0, :], const("lam"), -1.0, const("lam"), ALU.mult, ALU.max), "lru_abs")
                need(v, "lru_ln", 1)
                chain(tsc(sp[:, 0, :], const("lam"), -1.0, 0.0, ALU.mult, ALU.max))
                chain(tt(sp[:, 0, :], sp[:, 0, :], sp[:, 1, :], ALU.add))
                chain(tsc(sp[:, 2, :], sp[:, 0, :], -LRU_C, None, ALU.mult))
                signal(tsc(sp[:, 3, :], sp[:, 0, :], LRU_C, None, ALU.mult), "lru_sp")
                before = PROJ_BEFORE["lru_in"]
                for i in range(KD):
                    need(v, "proj_out", before + i + 1)
                    chain(tsc(xc[:, i, :], rec[:, i, 0:SEQ], const("conv_w", i), const("conv_b", i), ALU.mult, ALU.add))
                    for k in range(1, TAPS):
                        if k == TAPS - 1:
                            chain(stt(y_hi[:, i, :], rec[:, i, k:k + SEQ], const("conv_w", k * KD + i), xc[:, i, :],
                                      ALU.mult, ALU.add))
                        chain(stt(xc[:, i, :], rec[:, i, k:k + SEQ], const("conv_w", k * KD + i), xc[:, i, :],
                                  ALU.mult, ALU.add))
                    signal(tt(y_lo[:, i, :], xc[:, i, :], y_hi[:, i, :], ALU.subtract), "lru_conv")
                for half in range(2):
                    fours = slice(4 * half, 4 * half + 4)
                    need(v, "proj_out", before + KD + 4 * half + 4)
                    g, z = lru_gate[:, fours, :], gelu_z[:, fours, :]
                    chain(tt(z, g, g, ALU.mult))
                    chain(tsc(z, z, 0.044715, 1.0, ALU.mult, ALU.add))
                    signal(tt(z, z, g, ALU.mult), "lru_z")
                for half in range(2):
                    fours = slice(4 * half, 4 * half + 4)
                    need(v, "lru_gelu", half + 1)
                    chain(tt(lru_gate[:, fours, :], lru_gate[:, fours, :], gelu_z[:, fours, :], ALU.mult))
                need(v, "lru_ri", KD)
                for half in range(2):
                    fours = slice(4 * half, 4 * half + 4)
                    chain(tt(lru_h[:, fours, :], lru_i[:, fours, :], xc[:, fours, :], ALU.mult))
                for half in range(2):
                    fours = slice(4 * half, 4 * half + 4)
                    need(v, "lru_a", half + 1)
                    chain(tt(gelu_z[:, fours, :], lru_a[:, fours, :], lru_a[:, fours, :], ALU.mult))
                    signal(stt(lru_t[:, fours, :], gelu_z[:, fours, :], 1.0, lru_t[:, fours, :], ALU.add, ALU.mult), "lru_m")
                for half in range(2):
                    fours = slice(4 * half, 4 * half + 4)
                    need(v, "lru_root", half + 1)
                    chain(tt(lru_h[:, fours, :], lru_h[:, fours, :], lru_t[:, fours, :], ALU.mult))
                    for i in range(4 * half, 4 * half + 4):
                        chain(nc.vector.tensor_tensor_scan(lru_i[:, i, :], lru_a[:, i, :], lru_h[:, i, :], 0.0,
                                                           ALU.mult, ALU.add))
                        split_y(i, lambda out: tt(out, lru_i[:, i, :], lru_gate[:, i, :], ALU.mult), gelu_z[:, i, :])
                last = FIRST["lru_out"] + 7
                v.wait_ge(used[slot(last)], nth(last))

            def heads_norm(k, before, dst, gain):
                need(v, "proj_out", before + KD)
                signal(tt(sq_heads[:, :, :], raw_heads[:, :, :], raw_heads[:, :, :], ALU.mult), "heads_sq")
                need(v, "heads_n", k)
                signal(tsc(rms_heads[:, :, :].rearrange("p (a c) s -> p a (c s)", c=2), ps[:, 4:8, :],
                           1.0 / HD, NORM_EPS, ALU.mult, ALU.add), "heads_ms")
                need(v, "heads_root", k)
                chain(nc.vector.reciprocal(rms_heads[:, :, :], rms_heads[:, :, :]))
                signal(stt(dst[:, :, :], raw_heads[:, :, :], const(gain), rms_heads[:, :, :], ALU.mult, ALU.mult),
                       "heads_ready")

            def shared_kv():
                heads_norm(1, PROJ_BEFORE["kv"], k_t, "k_norm")

            def attention():
                heads_norm(2, PROJ_BEFORE["q_in"], q_t, "q_norm")
                for buf in pass_on:
                    chain(nc.vector.memset(buf[:, :, P:], 0.0))
                    for j in range(2):
                        chain(nc.vector.memset(buf[:, 3 * j, P:], 1.0))
                chain(nc.vector.memset(row_end[:, :, :], 0.0))
                for j in range(2):
                    ins = nc.vector.memset(row_end[:, 3 * j + 1:3 * j + 3, P:], 1.0)
                signal(ins, "at_sep")
                for step in range(KD + 3):
                    if step < KD:
                        c = step
                        need(v, "at_z", c + 1)
                        z = ps[:, 2 * (c % 2):2 * (c % 2) + 2, P:3 * P].rearrange("p b (m s) -> p b m s", m=2)
                        mask = const("not_before").unsqueeze(1).unsqueeze(1).broadcast_to([P, 2, 2, P])
                        signal(tt(z, z, mask, ALU.add), "at_mask")
                    if 0 <= step - 1 < KD:
                        c = step - 1
                        need(v, "at_sig", c + 1)
                        chain(nc.vector.tensor_tensor_scan(flat(left)[:, ::-1], flat(pass_on[c % 2])[:, ::-1],
                                                           flat(row_end)[:, ::-1], 1.0, ALU.mult, ALU.add))
                        if c >= 2:
                            need(v, "at_wt", c - 1)
                        signal(tt(weights[c % 2][:, :, :], stick[c % 2][:, :, :], left[:, :, 1:], ALU.mult), "at_w")
                    if 0 <= step - 3 < KD:
                        c = step - 3
                        need(v, "at_yhi", c + 1)
                        signal(tt(y_lo[:, c, :], bank(6 + c % 2)[:, 0, :], y_hi[:, c, :], ALU.subtract), "y_ready")
                last = FIRST["attn_out"] + 7
                v.wait_ge(used[slot(last)], nth(last))

            v.wait_ge(x_loaded, 16)
            v.wait_ge(const_loaded, 16)
            steps = [
                lambda: (norm_rows(0), norm_lo(0, "g_ffn_a")),
                lambda: (ffn(0, FIRST["ffn_a"]), add_to_x(0.5)),
                lambda: (norm_rows(1), norm_lo(1, "g_mix"), mixer_one(), add_to_x(1.0)),
                lambda: (norm_rows(2), norm_lo(2, "g_ffn_b")),
                lambda: (ffn(1, FIRST["ffn_b"]), add_to_x(0.5)),
                lambda: gain_x(3),
                lambda: (norm_rows(4), norm_lo(3, "g_ffn_c"), ffn(2, FIRST["ffn_c"]), add_to_x(0.5)),
                lambda: (norm_rows(5), norm_lo(4, "g_lru"), lru(), add_to_x(1.0)),
                lambda: (norm_rows(6), norm_lo(5, "g_ffn_d"), ffn(3, FIRST["ffn_d"]), add_to_x(0.5)),
                lambda: (norm_rows(7), norm_lo(6, "g_kv"), shared_kv()),
                lambda: (norm_lo(7, "g_ffn_e"), ffn(4, FIRST["ffn_e"]), add_to_x(0.5)),
                lambda: (norm_rows(8), norm_lo(8, "g_attn"), attention(), add_to_x(1.0)),
                lambda: (norm_rows(9), norm_lo(9, "g_ffn_f"), ffn(5, FIRST["ffn_f"]), add_to_x(0.5)),
            ]
            for step in steps:
                step()

        @block.tensor
        def _(pe):
            pe.wait_ge(const_loaded, 16)

            def transposes(g, rows):
                for t in range(TB):
                    pe.wait_ge(xs_ready, TB * rows + t + 1)
                for k in range(KD):
                    for t in range(TB):
                        ins = nc.tensor.transpose(xt_tile(k)[:, t * P:t * P + P], xs[:, t, k * P:k * P + P],
                                                  const("ident"))
                    ins.then_inc(xt_ready, 1)

            def feature_tile(n, where, i=0, after_norm=None, hi_in=None, lo_in=None):
                hi_in, lo_in = xn_hi, xn_lo
                pe.wait_ge(lo_ready[slot(n)], nth(n, i))
                for k in range(KD):
                    if after_norm is not None:
                        pe.wait_ge(xn_lo_ready, KD * after_norm + k // 2 * 2 + 2)
                    wh, wl = (w[:, slot(n), k * P:k * P + P] for w in (w_hi, w_lo))
                    nc.tensor.matmul(where, wh, hi_in[:, k, :], start=k == 0, stop=False)
                    nc.tensor.matmul(where, wh, lo_in[:, k, :], start=False, stop=False)
                    ins = nc.tensor.matmul(where, wl, hi_in[:, k, :], start=False, stop=k == KD - 1)
                ins.then_inc(used[slot(n)], 1)

            def rows_tile(n, lhs_hi, lhs_lo, i=0, start=False, stop=False, bank=0):
                pe.wait_ge(lo_ready[slot(n)], nth(n, i))
                for t in range(TB):
                    lh, ll = (a[:, t * P:t * P + P] for a in (lhs_hi, lhs_lo))
                    for c in range(2):
                        acc = ps[:, bank + 2 * t + c, :]
                        wh, wl = (w[:, slot(n), 512 * c:512 * c + 512] for w in (w_hi, w_lo))
                        nc.tensor.matmul(acc, lh, wh, start=start, stop=False)
                        nc.tensor.matmul(acc, lh, wl, start=False, stop=False)
                        ins = nc.tensor.matmul(acc, ll, wh, start=False, stop=stop)
                ins.then_inc(used[slot(n)], 1)

            def ffn(f, g, n0):
                def gate_up(c, i=0):
                    after = g if c == 0 else None
                    feature_tile(n0 + 3 * c, ps[:, 4 + c % 2, 0:SEQ], i, after)
                    feature_tile(n0 + 3 * c + 1, ps[:, 4 + c % 2, SEQ:], i)

                def down(c, i=0, **k):
                    pe.wait_ge(h_ready, NFC * f + c + 2 * i + 1)
                    rows_tile(n0 + 3 * c + 2, h_hi[:, c % 2, :], h_lo[:, c % 2, :], i, **k)
                gate_up(0)
                gate_up(1)
                down(0, start=True)
                with pe.Fori(0, (NFC - 2) // 2) as i:
                    gate_up(2, i)
                    down(1, i)
                    gate_up(3, i)
                    down(2, i)
                down(NFC - 1, stop=True)

            mm = nc.tensor.matmul

            def attention_level(lev, src, k):
                at = 9 * (k - 1) + lev
                if lev:
                    need(pe, "gla_qk", 8 * (k - 1) + lev)
                    q_of, k_of = q_dec[(lev - 1) % 2], k_dec[(lev - 1) % 2]
                else:
                    q_of, k_of = src["q"], src["k"]
                if lev >= 2:
                    need(pe, "sc_out", at - 1)
                b = 2 * (lev % 2)
                for j in range(2):
                    rows = slice(HD * j, HD * j + HD)
                    for c in range(2):
                        if lev == 8:
                            ins = mm(ps[:, b + j, c * P:c * P + P], k_of[rows, c, 0:P], q_of[rows, c, P:], start=True, stop=True)
                            continue
                        for t in range(TB):
                            cols = slice(t * P, t * P + P)
                            ins = mm(ps[:, b + j, (2 * c + t) * P:(2 * c + t + 1) * P], k_of[rows, c, cols],
                                     q_of[rows, c, cols], start=True, stop=True)
                ins.then_inc(ev["sc_done"], 1)

            def to_rows(src, b, name):
                for t in range(TB):
                    for c in range(2):
                        ins = nc.tensor.transpose(bank(b)[:, t, c * P:c * P + P], src[:, c, t * P:t * P + P], const("ident"))
                ins.then_inc(ev[name], 1)

            def attend(k):
                need(pe, "sc_out", 9 * k)
                for c in range(2):
                    for j in range(2):
                        rows = slice(HD * j, HD * j + HD)
                        cols = slice(c * P + j * HD, c * P + j * HD + HD)
                        m = 4 * j + 2 * c
                        mm(bank(2)[rows, c, 0:P], v_rows[:, 0, cols], scores[:, m, :], start=True, stop=True)
                        mm(bank(2)[rows, c, P:], v_rows[:, 0, cols], scores_far[:, 2 * j + c, :], start=True, stop=False)
                        ins = mm(bank(2)[rows, c, P:], v_rows[:, 1, cols], scores[:, m + 1, :], start=False, stop=True)
                ins.then_inc(ev["o_done"], 1)

            def attend_norm(k, per_head):
                need(pe, "o_sq", k)
                if per_head:
                    ins = mm(ps[:, 3, :], const("head_ones"), flat(tmp), start=True, stop=True)
                else:
                    mm(bank(3)[:, 0, :], const("all_ones"), tmp[:, 0, :], start=True, stop=False)
                    ins = mm(bank(3)[:, 0, :], const("all_ones"), tmp[:, 1, :], start=False, stop=True)
                ins.then_inc(ev["on_done"], 1)

            def project(i, n, g, **k):
                if i >= 4:
                    need(pe, "proj_out", k.pop("before", 0) + i - 3)
                feature_tile(n, ps[:, 4 + i % 4, 0:SEQ], after_norm=g if i == 0 else None)

            def mixer_one():
                n0 = FIRST["mix_in"]
                todo = iter(range(27))

                def tile(count=1):
                    for _ in range(count):
                        i = next(todo)
                        project(i, n0 + i, 1)
                tile(3)
                need(pe, "proj_out", 1)
                for c in range(2):
                    ins = mm(bank(3)[:, c, :], const("gla_w2")[0:32, c * P:c * P + P], ga_sb[0:32, :], start=True, stop=True)
                ins.then_inc(ev["gla_z"], 1)
                tile(4)
                need(pe, "proj_out", 7)
                to_rows(gla_in["v"], 2, "vt_done")
                tile()
                need(pe, "gla_abs", 1)
                need(pe, "vt_out", 1)
                for lev in range(9):
                    attention_level(lev, gla_in, 1)
                    tile()
                attend(1)
                tile()
                attend_norm(1, True)
                tile()
                need(pe, "on_ms", 1)
                need(pe, "proj_out", 17)
                to_rows(hgrn_in["v"], 2, "vt_done")
                tile()
                need(pe, "hg_ready", 1)
                for lev in range(9):
                    attention_level(lev, hgrn_in, 2)
                    if lev < 7:
                        tile()
                attend(2)
                attend_norm(2, False)
                need(pe, "pool_ready", 1)
                for c in range(2):
                    ins = mm(bank(2)[:, c, :], const("pool_w", c, P), tmp[:, c, :], start=True, stop=True)
                ins.then_inc(ev["pool_done"], 1)
                rwkv()
                mix_rows(6, 8)

            def mix_rows(first, end):
                for step in range(first, end):
                    i = (0, 1, 2, 3, 6, 7, 4, 5)[step]
                    need(pe, "y_ready", 6 + max(0, step - 5))
                    rows_tile(FIRST["mix_out"] + step, y_hi[:, i, :], y_lo[:, i, :], start=step == 0, stop=step == 7)

            def rwkv():
                need(pe, "y_ready", 6)
                need(pe, "rw_lora_in", 1)
                for c in range(2):
                    cols = slice(c * P, c * P + P)
                    mm(bank(1)[:, c, :], const("w2a2")[64:128, cols], rw[64:128, 6, :], start=True, stop=True)
                    mm(bank(0)[:, c, :], const("w2a2")[0:64, cols], lora[0:64, 0, :], start=True, stop=True)
                    ins = mm(bank(2)[:, c, :], const("g2")[:, cols], lora[:, 1, :], start=True, stop=True)
                ins.then_inc(ev["rw_lora"], 1)
                need(pe, "rw_kk_sq", 1)
                mm(ps[:, 3, :], const("head_ones"), flat(sq), start=True, stop=True).then_inc(ev["rw_kk_n"], 1)
                for i, src in enumerate((a_dec, b_last, k_last)):
                    need(pe, "rw_dec", i + 1)
                    to_rows(src, 4 + i, "rw_tok")
                to_rows(rw[:, 4:6, :], 7, "rw_tok")
                need(pe, "rw_bonus_in", 1)
                mm(ps[:, 3, :], const("head_ones"), flat(sq), start=True, stop=True).then_inc(ev["rw_bonus"], 1)

                def products(b, lhs, rhs):
                    for j in range(2):
                        rows = slice(HD * j, HD * j + HD)
                        for c in range(2):
                            for t in range(TB):
                                cols = slice(t * P, t * P + P)
                                ins = mm(ps[:, b + j, (2 * c + t) * P:(2 * c + t + 1) * P], lhs[rows, c, cols],
                                         rhs[rows, c, cols], start=True, stop=True)
                    ins.then_inc(ev["rw_mat"], 1)
                need(pe, "rw_g", 1)
                products(0, b_dec, a_dec)
                need(pe, "rw_tok_out", 1)
                need(pe, "rw_tok_act", 2)
                products(4, a_dec, b_dec)
                need(pe, "rw_mat_out", 1)
                products(0, kk_dec, a_dec)
                products(2, b_dec, r_dec)
                need(pe, "rw_mat_out", 3)
                products(0, kk_dec, r_dec)
                for c in range(2):
                    for j in range(2):
                        cols = slice(c * P + j * HD, c * P + j * HD + HD)
                        for t in range(TB):
                            ins = mm(bank(6)[:, t, cols], lak_t[:, 4 * j + 2 * c + t, :], v_tok[:, t, cols],
                                     start=True, stop=True)
                ins.then_inc(ev["rw_lv"], 1)
                need(pe, "rw_mat_out", 5)
                for lev in range(1, 6):
                    for j in range(2):
                        need(pe, "rw_z_out", 1 if lev == 1 else 2 * (lev - 2) + j + 2)
                        for m in range(4):
                            ins = mm(bank(j, 4)[:, m, :], l_t[:, 4 * j + m, :], inv[:, 4 * j + m, :], start=True, stop=True)
                        ins.then_inc(ev["rw_y"], 1)
                    for j in range(2):
                        need(pe, "rw_ym", 2 * (lev - 1) + j + 1)
                        for m in range(4):
                            if lev < 5:
                                mm(bank(2 + j, 4)[:, m, :], inv_t[:, 4 * j + m, :], y_m[:, 4 * j + m, :], start=True, stop=True)
                            ins = mm(bank(4 + j, 4)[:, m, :], y_m[:, 4 * j + m, :], inv_t[:, 4 * j + m, :], start=True, stop=True)
                        ins.then_inc(ev["rw_z"], 1)
                need(pe, "rw_z_out", 11)
                for c in range(2):
                    for j in range(2):
                        cols = slice(c * P + j * HD, c * P + j * HD + HD)
                        for t in range(TB):
                            ins = mm(bank(0)[HD * j:HD * j + HD, c, t * P:t * P + P], a_tok[:, t, cols],
                                     inv_t[:, 4 * j + 2 * c + t, :], start=True, stop=True)
                ins.then_inc(ev["rw_wt"], 1)
                need(pe, "rw_lv_out", 1)
                for c in range(2):
                    for j in range(2):
                        cols = slice(c * P + j * HD, c * P + j * HD + HD)
                        for t in range(TB):
                            ins = mm(bank(1)[:, t, cols], inv_t[:, 4 * j + 2 * c + t, :], lv[:, t, cols], start=True, stop=True)
                ins.then_inc(ev["rw_ut"], 1)
                need(pe, "rw_wu_out", 1)
                for q in range(NCH):
                    rows, t = slice(CHUNK * (q % 2), CHUNK * (q % 2) + CHUNK), q // 2
                    if q:
                        need(pe, "rw_st_out", q)
                        for c in range(2):
                            ins = mm(ps[rows, 2 + q % 2, c * P:c * P + P], w_t[:, c, q * CHUNK:(q + 1) * CHUNK],
                                     state[q][:, c, :], start=True, stop=True)
                        ins.then_inc(ev["rw_u"], 1)
                    need(pe, "rw_u_out", q + 1)
                    if q + 1 < NCH:
                        for c in range(2):
                            cols = slice(c * P, c * P + P)
                            mm(ps[:, 4 + q % 2, cols], b_tok[rows, t, cols], u[rows, t, cols], start=True, stop=False)
                            ins = mm(ps[:, 4 + q % 2, cols], k_tok[rows, t, cols], v_tok[rows, t, cols], start=False, stop=True)
                        ins.then_inc(ev["rw_st"], 1)
                for c in range(2):
                    for q in range(NCH):
                        t, tok = q // 2, slice(q * CHUNK, (q + 1) * CHUNK)
                        if q:
                            mm(bank(6)[:, c, tok], state[q][:, c, :], r_dec[:, c, tok], start=True, stop=False)
                        for j in range(2):
                            rows = slice(HD * j, HD * j + HD)
                            cols = slice(c * P + j * HD, c * P + j * HD + HD)
                            m, own = 4 * j + 2 * c + t, slice((q % 2) * CHUNK, (q % 2) * CHUNK + CHUNK)
                            mm(bank(6)[rows, c, tok], u[:, t, cols], mrb_t[:, m, own], start=q == 0, stop=False)
                            ins = mm(bank(6)[rows, c, tok], v_tok[:, t, cols], mrk_t[:, m, own], start=False, stop=True)
                ins.then_inc(ev["rw_o"], 1)
                mix_rows(0, 1)
                need(pe, "rw_o_out", 1)
                mm(ps[:, 4, :], const("head_ones"), flat(o_r), start=True, stop=True).then_inc(ev["rw_mean"], 1)
                mix_rows(1, 2)
                need(pe, "rw_dev", 1)
                mm(ps[:, 5, :], const("head_ones"), flat(t_r), start=True, stop=True).then_inc(ev["rw_var"], 1)
                mix_rows(2, 6)

            def lru():
                before = PROJ_BEFORE["lru_in"]
                n0 = FIRST["lru_in"]
                for i in range(2 * KD):
                    project(i, n0 + i, 4, before=before)
                n0 = FIRST["lru_gates"]
                for b in range(4):
                    n = n0 + b
                    need(pe, "lru_conv", 2 * b + 2)
                    pe.wait_ge(lo_ready[slot(n)], nth(n))
                    for half in range(2):
                        i = 2 * b + half
                        need(pe, *(("proj_out", before + 2 * KD - 3 + i) if i < 4 else ("lru_ri", i - 3)))
                        for gate in range(2):
                            where = bank(4 + i % 4)[:, gate, :]
                            for k in range(2):
                                at = ((half * 2 + gate) * 2 + k) * P
                                wh, wl = (w[:, slot(n), at:at + P] for w in (w_hi, w_lo))
                                mm(where, wh, y_hi[:, 2 * b + k, :], start=k == 0, stop=False)
                                mm(where, wh, y_lo[:, 2 * b + k, :], start=False, stop=False)
                                ins = mm(where, wl, y_hi[:, 2 * b + k, :], start=False, stop=k == 1)
                        ins.then_inc(used[slot(n)] if half else ev["lru_gates_done"], 1)
                for i in range(KD):
                    n = FIRST["lru_out"] + i
                    need(pe, "y_ready", 8 + i + 1)
                    rows_tile(n, y_hi[:, i, :], y_lo[:, i, :], start=i == 0, stop=i == KD - 1)

            def heads_squares(k):
                need(pe, "heads_sq", k)
                for a in range(4):
                    ins = mm(ps[:, 4 + a, :], const("head_ones"), sq_heads[:, 2 * a:2 * a + 2, :].rearrange("p a b -> p (a b)"),
                             start=True, stop=True)
                ins.then_inc(ev["heads_n"], 1)

            def shared_kv():
                n0 = FIRST["kv"]
                for i in range(KD):
                    project(i, n0 + i, 6, before=PROJ_BEFORE["kv"])
                for k in range(KD):
                    rows_tile(n0 + KD + k, xn_hi[:, k, :], xn_lo[:, k, :], start=k == 0, stop=k == KD - 1)
                    if k == 2:
                        heads_squares(1)
                need(pe, "heads_ms", 1)
                need(pe, "v_out", 1)

            def attention():
                n0 = FIRST["q_in"]
                for i in range(KD):
                    project(i, n0 + i, 8, before=PROJ_BEFORE["q_in"])
                need(pe, "proj_out", PROJ_BEFORE["q_in"] + KD)
                heads_squares(2)
                need(pe, "heads_ready", 2)

                def logits(c):
                    if c >= 2:
                        need(pe, "at_sig", c - 1)
                    for j in range(2):
                        rows, b = slice(HD * j, HD * j + HD), 2 * (c % 2) + j
                        mm(ps[:, b, 0:2 * P], q_t[rows, c, P:], k_t[rows, c, :], start=True, stop=True)
                        ins = mm(ps[:, b, 2 * P:3 * P], q_t[rows, c, 0:P], k_t[rows, c, 0:P], start=True, stop=True)
                    ins.then_inc(ev["at_z"], 1)
                logits(0)
                logits(1)
                for c in range(KD):
                    need(pe, "at_w", c + 1)
                    if c:
                        need(pe, "at_wt_out", c)
                    for j in range(2):
                        for m in range(3):
                            ins = nc.tensor.transpose(ps[:, 4 + j, m * P:m * P + P], weights[c % 2][:, 3 * j + m, :], const("ident"))
                    ins.then_inc(ev["at_wt"], 1)
                    if c + 2 < KD:
                        logits(c + 2)
                    need(pe, "at_wt_out", c + 1)
                    if c >= 2:
                        need(pe, "y_ready", 16 + c - 1)
                    for j in range(2):
                        rows, cols = slice(HD * j, HD * j + HD), slice(c * P + HD * j, c * P + HD * j + HD)
                        o, w = bank(6 + c % 2)[rows, 0, :], weights_t[c % 2]
                        mm(o[:, P:], v_heads[:, 0, cols], w[:, 3 * j, :], start=True, stop=False)
                        mm(o[:, P:], v_heads[:, 1, cols], w[:, 3 * j + 1, :], start=False, stop=True)
                        ins = mm(o[:, 0:P], v_heads[:, 0, cols], w[:, 3 * j + 2, :], start=True, stop=True)
                    ins.then_inc(ev["at_o"], 1)
                for i in range(KD):
                    need(pe, "y_ready", 16 + i + 1)
                    rows_tile(FIRST["attn_out"] + i, y_hi[:, i, :], y_lo[:, i, :], start=i == 0, stop=i == KD - 1)

            steps = [
                lambda: transposes(0, 0),
                lambda: ffn(0, 0, FIRST["ffn_a"]),
                lambda: (transposes(1, 1), mixer_one()),
                lambda: transposes(2, 2),
                lambda: ffn(1, 2, FIRST["ffn_b"]),
                lambda: None,
                lambda: (transposes(3, 3), ffn(2, 3, FIRST["ffn_c"])),
                lambda: (transposes(4, 4), lru()),
                lambda: (transposes(5, 5), ffn(3, 5, FIRST["ffn_d"])),
                lambda: (transposes(6, 6), shared_kv()),
                lambda: (transposes(7, 6), ffn(4, 7, FIRST["ffn_e"])),
                lambda: (transposes(8, 7), attention()),
                lambda: (transposes(9, 8), ffn(5, 9, FIRST["ffn_f"])),
            ]
            for step in steps:
                step()


def lay_out(inp):
    import numpy as np

    def features(w, cols=None):
        w = np.asarray(w)
        m = w.shape[1] // P
        return w.reshape(KD, P, m, P).transpose(2, 1, 0, 3).reshape(m, P, BLK)

    def rows(w):
        return np.asarray(w).reshape(-1, P, BLK)

    def ffn(w_in, w_out):
        w_in, w_out = np.asarray(w_in), np.asarray(w_out)
        gate, up, down = features(w_in[:, :FF]), features(w_in[:, FF:]), rows(w_out)
        return np.stack([gate, up, down], 1).reshape(-1, P, BLK)

    w_in, w_out = np.asarray(inp["w_in"][0]), np.asarray(inp["w_out"][0])
    pool, hg, rw, gl = w_in[:, :G], w_in[:, G:5 * G], w_in[:, 5 * G:9 * G], w_in[:, 9 * G:]
    ga = np.zeros((D, P), np.float32)
    ga[:, :16] = gl[:, 4 * G:]
    mix_in = np.concatenate([ga, gl[:, :4 * G], hg[:, G:2 * G], hg[:, :G], hg[:, 2 * G:], pool, rw], 1)
    wr = np.asarray(inp["a_w_r_2"][0])
    wi = np.asarray(inp["a_w_i_2"][0])
    lru = np.stack([wr, wi], 1).reshape(4, 2, 2, P, 2, P).transpose(0, 3, 4, 1, 2, 5).reshape(4, P, BLK)
    a_in = np.asarray(inp["a_w_in_2"][0])
    a_in = np.concatenate([a_in[:, D:], a_in[:, :D]], 1)
    w_kv = np.asarray(inp["w_kv_2"])
    w13, w2 = inp["ffn1_w13_2"], inp["ffn1_w2_2"]
    v13, v2 = inp["ffn2_w13_2"], inp["ffn2_w2_2"]
    blocks = np.concatenate([
        ffn(inp["ffn1_w_in"][0], inp["ffn1_w_out"][0]), features(mix_in), rows(w_out)[[0, 1, 2, 3, 6, 7, 4, 5]],
        ffn(inp["ffn2_w_in"][0], inp["ffn2_w_out"][0]), ffn(w13[0], w2[0]),
        features(a_in), lru, rows(inp["a_w_out_2"][0]), ffn(v13[0], v2[0]),
        features(w_kv[:, :D]), rows(w_kv[:, D:]), ffn(w13[1], w2[1]),
        features(inp["b_w_q_2"][0]), rows(inp["b_w_o_2"][0]), ffn(v13[1], v2[1])])
    assert blocks.shape == (NBLK, P, BLK)

    cst = np.zeros((P, NCONST), np.float32)

    def put(name, a):
        at, w = CONST_AT[name]
        a = np.asarray(a)
        cst[:a.shape[0], at:at + w] = a.reshape(a.shape[0], w)

    def columns(a):
        return np.asarray(a).reshape(-1, P).T

    for name, a in [("g_ffn_a", inp["norm_ffn1"][0]), ("g_mix", inp["norm_mix"][0]), ("g_ffn_b", inp["norm_ffn2"][0]),
                    ("g_ffn_c", inp["ffn1_norm_2"][0]), ("g_lru", inp["mix_norm_2"][0]), ("g_ffn_d", inp["ffn2_norm_2"][0]),
                    ("g_kv", inp["kv_norm_2"]), ("g_ffn_e", inp["ffn1_norm_2"][1]), ("g_attn", inp["mix_norm_2"][1]),
                    ("g_ffn_f", inp["ffn2_norm_2"][1]), ("lb_logits", inp["hgrn_lb_logits"][0]),
                    ("hgrn_norm", inp["hgrn_norm"][0]), ("mu", inp["rwkv_mu"][0]), ("w0", inp["rwkv_w0"][0]),
                    ("a0", inp["rwkv_a0"][0]), ("k_k", inp["rwkv_k_k"][0]), ("k_a", inp["rwkv_k_a"][0]),
                    ("r_k", inp["rwkv_r_k"][0]), ("ln_w", inp["rwkv_ln_w"][0]), ("ln_b", inp["rwkv_ln_b"][0]),
                    ("gla_b", inp["gla_b"][0]), ("gla_norm", inp["gla_norm"][0]), ("pool_b", inp["pool_b"][0]),
                    ("pool_scale", inp["pool_scale"][0]), ("conv_w", inp["a_conv_w_2"][0]), ("conv_b", inp["a_conv_b_2"][0]),
                    ("b_r", inp["a_b_r_2"][0]), ("b_i", inp["a_b_i_2"][0]), ("lam", inp["a_lambda_2"][0])]:
        put(name, columns(a))
    put("k_norm", np.concatenate([np.asarray(inp["k_norm_2"])] * 2)[:, None])
    put("q_norm", np.concatenate([np.asarray(inp["q_norm_2"][0])] * 2)[:, None])
    put("w2a2", np.concatenate([np.asarray(inp["rwkv_w2"][0]), np.asarray(inp["rwkv_a2"][0])]))
    put("g2", np.asarray(inp["rwkv_g2"][0]))
    put("gla_w2", np.asarray(inp["gla_w2"][0]))
    pool_w = np.zeros((P, 2, P), np.float32)
    for g in range(4):
        rows_g = slice(HD * (g % 2), HD * (g % 2) + HD)
        pool_w[rows_g, g // 2, rows_g] = np.asarray(inp["pool_w"][0])[g]
    put("pool_w", pool_w)
    s, t = np.arange(P)[:, None], np.arange(P)[None, :]
    put("ident", s == t)
    put("head_ones", s // HD == t // HD)
    put("all_ones", np.ones((P, P)))
    levels = [s == t] + [(t // n == s // n + 1) & (t // n % 2 == 1) for n in (1, 2, 4, 8, 16, 32, 64)]
    put("level", np.concatenate(levels, 1))
    put("level_low", np.concatenate([m.T for m in levels[1:7]], 1))
    same = s // CHUNK == t // CHUNK
    put("strict_up", same & (s < t))
    put("incl_up", same & (s <= t))
    put("strict_low", same & (s > t))
    put("not_before", np.where(t >= s, np.float32(MASKED_OUT), np.float32(0)))
    windows = np.array([2, 4, 8, 16])[np.arange(G) // HD]
    inv = np.float32(1) / np.minimum(np.arange(SEQ)[None, :] + 1, windows[:, None]).astype(np.float32)
    put("inv_count", inv.reshape(2, P, SEQ).transpose(1, 0, 2))
    one = np.zeros((P, 8, 65), np.float32)
    one[:, :, 0] = 1
    put("scan_one", one)
    x = np.asarray(inp["x"]).reshape(TB, P, D).transpose(1, 0, 2)
    gain = np.broadcast_to(np.asarray(inp["norm_final"])[None, :], (P, D))
    assert NBLK == len(blocks)
    return {"x_in": x, "blocks": blocks, "consts": cst, "final_gain": gain}


def kernel(**inputs):
    import numpy as _np
    import concourse.bacc as _bacc
    from concourse import mybir as _mybir
    from concourse.bass_utils import run_bass_kernel_spmd as _run

    nc = _bacc.Bacc("TRN2", target_bir_lowering=False, num_devices=1)
    arrays = {name: _np.ascontiguousarray(a) for name, a in lay_out(inputs).items()}
    args = [nc.dram_tensor(name, a.shape, _mybir.dt.from_np(a.dtype), kind="ExternalInput").ap()
            for name, a in arrays.items()]
    out = nc.dram_tensor("out", (TB, P, D), _mybir.dt.float32, kind="ExternalOutput").ap()
    build(nc, *args, out)
    r = _run(nc, [arrays], core_ids=[0])
    return _np.asarray(r.results[0]["out"]).reshape(1, SEQ, D)
```

```python
import concourse.bass as bass
from concourse import mybir
from contextlib import ExitStack
import math

F32 = mybir.dt.float32
F32R = mybir.dt.float32r
U32 = mybir.dt.uint32
ALU = mybir.AluOpType
ACT = mybir.ActivationFunctionType

P = 128
SEQ = 256
D = 1024
KD = D // P
TB = SEQ // P
G = 256
FF = 2816
NFC = FF // P
HD = 64
QK_SCALE = HD ** -0.5
NORM_EPS = 1e-6
GATE_FLOOR = 1e-30
RWKV_GN_EPS = 64e-5
GLA_GATE_TAU = 16.0
CHUNK = 64
NCH = SEQ // CHUNK
LRU_C = 8.0
MASKED_OUT = -1e30

RING = 6
VERSIONS = 10
BLK = 1024


LEAD = 3
FFN_STEPS = NFC - LEAD
FIRST_STEPS = range(0, 3)
LOOP_STEPS = range(3, 7)
LOOP_TRIPS = 3
LAST_STEPS = range(3 + 4 * LOOP_TRIPS, FFN_STEPS)


def gate_block(c):
    return 2 * c if c < LEAD else 2 * LEAD + 1 + 3 * (c - LEAD)


def down_block(c):
    return 2 * LEAD + 3 * c if c < FFN_STEPS else 2 * LEAD + 3 * FFN_STEPS + c - FFN_STEPS


FFN_ORDER = sorted([(gate_block(c), 3 * c) for c in range(NFC)] + [(gate_block(c) + 1, 3 * c + 1) for c in range(NFC)]
                   + [(down_block(c), 3 * c + 2) for c in range(NFC)])


def plan_blocks():
    first, kinds = {}, []

    def add(phase, names):
        first[phase] = len(kinds)
        kinds.extend(names)

    ffn = [("gate", "up", "down")[which % 3] for _, which in FFN_ORDER]
    add("ffn_a", ffn)
    add("mix_in", ["in"] * 27)
    add("mix_out", ["rows"] * 8)
    add("ffn_b", ffn)
    add("ffn_c", ffn)
    add("lru_in", ["in"] * 16)
    add("lru_gates", ["lru"] * 4)
    add("lru_out", ["rows"] * 8)
    add("ffn_d", ffn)
    add("kv", ["in"] * 8 + ["rows"] * 8)
    add("ffn_e", ffn)
    add("q_in", ["in"] * 8)
    add("attn_out", ["rows"] * 8)
    add("ffn_f", ffn)
    return first, kinds


FIRST, KINDS = plan_blocks()
DVE_SPLITS = (1, 3)
NBLK = len(KINDS)
ORDER = list(FIRST)
LAST = dict(zip(ORDER, list(FIRST.values())[1:] + [NBLK]))

CONST_WIDTHS = [
    ("g_ffn_a", KD), ("g_mix", KD), ("g_ffn_b", KD), ("g_ffn_c", KD), ("g_lru", KD), ("g_ffn_d", KD),
    ("g_kv", KD), ("g_ffn_e", KD), ("g_attn", KD), ("g_ffn_f", KD), ("g_final", KD),
    ("norm_eps", 1), ("gn_eps", 1), ("all_ones", P),
    ("lb_logits", 2), ("hgrn_norm", 2), ("mu", 8), ("w0", 2), ("a0", 2), ("k_k", 2), ("k_a", 2), ("r_k", 2),
    ("ln_w", 2), ("ln_b", 2), ("gla_b", 2), ("gla_norm", 2), ("pool_b", 2), ("pool_scale", 2),
    ("conv_w", 4 * KD), ("conv_b", KD), ("b_r", KD), ("b_i", KD), ("lam", KD), ("k_norm", 1), ("q_norm", 1),
    ("w2a2", G), ("g2", G), ("gla_w2", G), ("pool_w", 2 * P),
    ("ident", P), ("head_ones", P),
    ("level", 8 * P), ("level_low", 6 * P), ("strict_up", P), ("incl_up", P), ("strict_low", P),
    ("not_before", P), ("inv_count", 2 * SEQ), ("scan_one", 8 * 65),
]


def const_offsets():
    at, out = 0, {}
    for name, width in CONST_WIDTHS:
        out[name] = (at, width)
        at += width
    return out, at


CONST_AT, NCONST = const_offsets()
FIRST_CONSTS = sum(CONST_AT["all_ones"])


def slot(n):
    return n % RING


def nth(n, i=0):
    return n // RING + 1 + i


class Chain:

    def __init__(self, engine, sem):
        self.engine, self.sem, self.count, self.later = engine, sem, 0, 0

    def __call__(self, ins):
        ins.then_inc(self.sem, 1)
        self.count += 1
        self.engine.wait_ge(self.sem, self.count + self.later)


def build(nc, x_in, blocks, consts, out):
    ctx = ExitStack()
    with ctx:
        def sb(name, shape, dt=F32):
            return ctx.enter_context(nc.sbuf_tensor(name, shape, dt))

        def sem(name):
            return ctx.enter_context(nc.semaphore(name))

        raw = sb("raw", [P, RING, BLK])
        w_hi = sb("w_hi", [P, RING, BLK], F32R)
        w_lo = sb("w_lo", [P, RING, BLK], F32R)
        x = sb("x", [P, KD, SEQ])
        xn_hi = sb("xn_hi", [P, KD, SEQ], F32R)
        xn_lo = sb("xn_lo", [P, KD, SEQ], F32R)
        y_hi = sb("y_hi", [P, KD, SEQ], F32R)
        y_lo = sb("y_lo", [P, KD, SEQ], F32R)
        h_hi = sb("h_hi", [P, 2, SEQ], F32R)
        h_lo = sb("h_lo", [P, 2, SEQ], F32R)
        cst = sb("cst", [P, NCONST])
        rstd = sb("rstd", [P, SEQ])
        rms = sb("rms", [P, SEQ])
        rstd_col = sb("rstd_col", [P, TB])
        table = sb("table", [1, 8])
        ARENA = 17100
        arena = sb("arena", [P, ARENA])
        ps = ctx.enter_context(nc.psum_tensor("ps", [P, 8, 512], F32))

        squares = arena[:, 0:TB * D].rearrange("p (a b) -> p a b", a=4)
        squares_sum = arena[:, TB * D:TB * D + 512]
        gate, sig = (arena[:, at:at + 2 * SEQ].rearrange("p (a b) -> p a b", a=2) for at in (2560, 3072))
        up, gs, h = (arena[:, at:at + SEQ] for at in (3584, 3840, 4096))

        def const(name, i=None, width=1):
            at, w = CONST_AT[name]
            if i is None:
                return cst[:, at:at + w]
            return cst[:, at + i * width:at + (i + 1) * width]

        arrived = [sem(f"arrived{s}") for s in range(RING)]
        hi_ready = [sem(f"hi_ready{s}") for s in range(RING)]
        lo_ready = [sem(f"lo_ready{s}") for s in range(RING)]
        used = [sem(f"used{s}") for s in range(RING)]
        x_loaded = [sem(f"x_loaded{a}") for a in range(4)]
        gains_loaded = sem("gains_loaded")
        const_loaded = sem("const_loaded")
        stored = sem("stored")
        x_ready = sem("x_ready")
        acc_done = sem("acc_done")
        sq_ready = sem("sq_ready")
        sum_ready = sem("sum_ready")
        total_ready = sem("total_ready")
        rms_ready = sem("rms_ready")
        first_rstd_ready = sem("first_rstd_ready")
        scaled_ready = sem("scaled_ready")
        rstd_ready = sem("rstd_ready")
        xn_hi_ready = sem("xn_hi_ready")
        xn_lo_ready = sem("xn_lo_ready")
        gate_ready = sem("gate_ready")
        sig_ready = sem("sig_ready")
        h_ready = sem("h_ready")
        table_ready = sem("table_ready")
        dve_chain = sem("dve_chain")
        act_chain = sem("act_chain")

        gained_squares = arena[:, 4608:4608 + TB * D].rearrange("p (a b) -> p a b", a=4)
        gained_sum = arena[:, 6656:6656 + 512]
        first_rstd, scaled = arena[:, 7168:7168 + SEQ], arena[:, 7424:7424 + SEQ]
        gain_both = sb("gain_both", [P, KD])

        def gain(name, k):
            return gain_both[:, k:k + 1] if name == "both" else const(name, k)

        def pair_of_x(a):
            return x[:, 2 * a:2 * a + 2, :].rearrange("p k t -> p (k t)")


        def carve(at, *shape):
            size = 1
            for d in shape:
                size *= d
            piece = arena[:, at:at + size]
            if len(shape) == 2:
                return piece.rearrange("p (a b) -> p a b", a=shape[0])
            if len(shape) == 3:
                return piece.rearrange("p (a b c) -> p a b c", a=shape[0], b=shape[1])
            return piece

        def over(ap, n):
            return ap.unsqueeze(1).broadcast_to([ap.shape[0], n, ap.shape[1]])

        def flat(ap):
            return ap.rearrange("p a b -> p (a b)")

        def pair(b, n=8):
            return ps[:, b:b + 2, :].rearrange("p b (m s) -> p (b m) s", m=n // 2)

        def bank(b, n=2):
            return ps[:, b, :].rearrange("p (m s) -> p m s", m=n)

        rw_raw = carve(0, 8, SEQ + 1)
        rw = carve(2056, 8, SEQ)
        gla_in = dict(q=carve(4104, 2, SEQ), k=carve(4616, 2, SEQ), v=carve(5128, 2, SEQ), gate=carve(5640, 2, SEQ))
        hgrn_in = dict(q=carve(6152, 2, SEQ), k=carve(6664, 2, SEQ), v=carve(7176, 2, SEQ), gate=carve(7688, 2, SEQ))
        PAD = 16
        pool_in = carve(8200, 2, PAD + SEQ)
        win_a = carve(8744, 2, PAD + SEQ)
        win_b = carve(9288, 2, PAD + SEQ)
        decay_to = carve(9832, 2, SEQ)
        decay_from = carve(10344, 2, SEQ)
        q_dec = [carve(10856, 2, SEQ), carve(11368, 2, SEQ)]
        k_dec = [carve(11880, 2, SEQ), carve(12392, 2, SEQ)]
        v_rows = carve(12904, 2, G)
        scores = carve(13416, 8, P)
        scores_far = carve(14440, 4, P)
        o_sb = carve(14952, 2, SEQ)
        tmp = carve(15464, 2, SEQ)
        tmp2 = carve(15976, 2, SEQ)
        norm_sb = carve(16488, 2, SEQ)
        lb = sb("lb", [P, 8])
        last_dec = sb("last_dec", [P, 8])
        ga_sb = carve(14952, SEQ)
        dec = carve(4104, 8, CHUNK + 1)
        cum = carve(4624, 8, CHUNK + 1)
        kk = carve(5144, 2, SEQ)
        iclr = carve(5656, 2, SEQ)
        k_new = carve(6168, 2, SEQ)
        inv = carve(4104, 8, P)
        inv_t = carve(5128, 8, P)
        r_dec, a_dec, b_dec, kk_dec, b_last, k_last = (carve(6680 + 512 * i, 2, SEQ) for i in range(6))
        g_r = carve(9752, 2, SEQ)
        bonus = carve(10264, 2, SEQ)
        v_tok = carve(10776, 2, G)
        a_tok = carve(2056, 2, G)
        b_tok = carve(2056 + 512, 2, G)
        k_tok = carve(2056 + 6 * SEQ, 2, G)
        l_t = carve(0, 8, P)
        lak_t = carve(1024, 8, P)
        mrb_t = carve(11288, 8, P)
        mrk_t = carve(12312, 8, P)
        y_m = carve(13336, 8, P)
        lora = carve(13336, 2, SEQ)
        sz = carve(13848, 2, SEQ)
        inv_cum = carve(11288, 2, SEQ)
        sq = carve(11800, 2, SEQ)
        lv = carve(13336, 2, G)
        w_t = carve(14360, 2, SEQ)
        u_tilde = carve(14872, 2, G)
        u = carve(15384, 2, G)
        state = [None] + [carve(15896 + 256 * i, 2, P) for i in range(3)]
        state_dec = carve(16664, 2, P)
        o_r, dev, t_r = a_dec, b_dec, kk_dec
        rms_r = carve(13336, 2, SEQ)

        ev = {name: sem(name) for name in (
            "proj_out gla_z gla_abs gla_ln gla_min gla_decay vt_done vt_out gla_qk sc_done sc_out o_done o_sq "
            "on_done on_root y_ready lb_zero lb_exp fn_done hg_ready pool_ready pool_done "
            "rw_mixed rw_lora_in rw_lora rw_iclr rw_decay rw_g rw_kk_sq rw_kk_n rw_kk_root rw_dec "
            "rw_bonus_in rw_bonus rw_tok rw_tok_act rw_tok_out rw_mat rw_mat_out rw_y rw_ym rw_z rw_z_out rw_lv rw_lv_out "
            "rw_wt rw_ut rw_wu_out rw_u rw_u_out rw_st rw_st_out rw_o rw_o_out rw_mean rw_dev rw_var rw_gn_root").split()}

        def need(engine, name, value):
            engine.wait_ge(ev[name], value)

        TAPS = 4
        rec = carve(0, KD, TAPS - 1 + SEQ)
        xc = carve(2072, KD, SEQ)
        lru_gate = carve(4120, KD, SEQ)
        gelu_z = carve(6168, KD, SEQ)
        lru_a = carve(8216, KD, SEQ)
        lru_i = carve(10264, KD, SEQ)
        lru_h = carve(12312, KD, SEQ)
        lru_t = carve(14360, KD, SEQ)
        sp = sb("sp", [P, 4, KD])

        raw_heads = carve(0, KD, SEQ)
        sq_heads = [carve(11800 + 512 * i, 2, SEQ) for i in range(2)]
        q_t = carve(2048, KD, SEQ)
        k_t = carve(13004, KD, SEQ)
        v_heads = carve(15052, TB, D)
        stick = [carve(4096 + 768 * i, 6, P) for i in range(2)]
        pass_on = [carve(5632 + 774 * i, 6, P + 1) for i in range(2)]
        left = carve(7180, 6, P + 1)
        row_end = carve(11026, 6, P + 1)
        weights = [carve(7954 + 768 * i, 6, P) for i in range(2)]
        weights_t = [carve(9490 + 768 * i, 6, P) for i in range(2)]

        for name in ("lru_abs lru_ln lru_conv lru_gate_in lru_z lru_gelu lru_gates_done lru_ri lru_sp lru_a lru_m lru_root "
                     "pad_rec heads_sq heads_n heads_root heads_ready v_out at_z at_mask at_sig at_w at_wt "
                     "at_wt_out at_o at_yhi at_sep col_done col_out").split():
            ev[name] = sem(name)
        TAKEN_BEFORE = {"mix_in": 0, "lru_in": 27, "kv": 27 + 2 * KD, "q_in": 27 + 3 * KD}
        block = ctx.enter_context(nc.Block())

        @block.sync
        def _(sp):
            sp.dma_start(cst[:, 0:FIRST_CONSTS], consts[:, 0:FIRST_CONSTS]).then_inc(gains_loaded, 16)
            for n in range(RING):
                if n == 0:
                    sp.dma_start(raw[:, n, :], blocks[n, :, :]).then_inc(arrived[n], 16)
                if n < 4:
                    sp.dma_start(x[:, 2 * n:2 * n + 2, :], x_in[:, 2 * n:2 * n + 2, :]).then_inc(x_loaded[n], 16)
                if n:
                    sp.dma_start(raw[:, n, :], blocks[n, :, :]).then_inc(arrived[n], 16)
            sp.dma_start(cst[:, FIRST_CONSTS:], consts[:, FIRST_CONSTS:]).then_inc(const_loaded, 16)
            rounds = NBLK // RING
            with sp.Fori(1, rounds) as r:
                for s in range(RING):
                    sp.wait_ge(lo_ready[s], r)
                    sp.dma_start(raw[:, s, :], blocks[bass.ds(r * RING + s, 1), :, :].rearrange("o p m -> p (o m)"))\
                        .then_inc(arrived[s], 16)
            for n in range(rounds * RING, NBLK):
                sp.wait_ge(lo_ready[slot(n)], n // RING)
                sp.dma_start(raw[:, slot(n), :], blocks[n, :, :]).then_inc(arrived[slot(n)], 16)
            for a in range(4):
                sp.wait_ge(x_ready, 4 * (VERSIONS - 1) + a + 1)
                sp.dma_start(out[:, 2 * a:2 * a + 2, :], x[:, 2 * a:2 * a + 2, :]).then_inc(stored, 16)
            sp.wait_ge(stored, 16 * 4)

        @block.gpsimd
        def _(pool):
            def lo(n, i=0):
                pool.wait_ge(hi_ready[slot(n)], nth(n, i))
                nc.gpsimd.tensor_tensor(w_lo[:, slot(n), :], raw[:, slot(n), :], w_hi[:, slot(n), :],
                                        ALU.subtract).then_inc(lo_ready[slot(n)], 1)

            for phase in ORDER:
                n0 = FIRST[phase]
                if phase.startswith("ffn"):
                    def step(k, i=0):
                        lo(n0 + gate_block(k + LEAD), 2 * i)
                        lo(n0 + gate_block(k + LEAD) + 1, 2 * i)
                    for n in range(n0, n0 + 2 * LEAD):
                        if n not in DVE_SPLITS:
                            lo(n)
                    for k in FIRST_STEPS:
                        step(k)
                    with pool.Fori(0, LOOP_TRIPS) as i:
                        for k in LOOP_STEPS:
                            step(k, i)
                    for k in LAST_STEPS:
                        step(k)
                else:
                    for n in range(n0, LAST[phase]):
                        lo(n)

        @block.scalar
        def _(act):
            chain = Chain(act, act_chain)
            state = {"next": 0, "norms": 0, "taken": 0}
            end = NBLK

            def hi(n, i=0):
                act.wait_ge(arrived[slot(n)], 16 * nth(n, i))
                if n >= RING:
                    act.wait_ge(used[slot(n)], nth(n, i) - 1)
                nc.scalar.activation(w_hi[:, slot(n), :], raw[:, slot(n), :], ACT.Copy)\
                    .then_inc(hi_ready[slot(n)], 1)

            def hi_until(n):
                while state["next"] <= min(n, end - 1):
                    hi(state["next"])
                    state["next"] += 1

            def preload(func):
                chain(nc.scalar.activation(table[:, 0:4], table[:, 4:8], func))

            def norm(version, gains, then=ACT.Sigmoid):
                for a in range(4):
                    if version:
                        act.wait_ge(x_ready, 4 * (version - 1) + a + 1)
                    else:
                        act.wait_ge(x_loaded[a], 16)
                    high_halves(gains, a)
                    if gains == "both":
                        for k in (2 * a, 2 * a + 1):
                            nc.scalar.activation(gained_squares[:, a, (k % 2) * SEQ:(k % 2 + 1) * SEQ], x[:, k, :],
                                                 ACT.Square, scale=const("g_final", k))
                    nc.scalar.activation(squares[:, a, :], pair_of_x(a), ACT.Square).then_inc(sq_ready, 1)
                    if version == 0:
                        hi_until(a + 1)
                preload(ACT.Sqrt)
                state["norms"] += 1
                act.wait_ge(total_ready, state["norms"])
                nc.scalar.activation(rms[:, :], ps[:, 3, 0:SEQ], ACT.Sqrt, scale=1.0 / D, bias=const("norm_eps"))\
                    .then_inc(rms_ready, 1)
                if gains == "both":
                    act.wait_ge(scaled_ready, 1)
                    nc.scalar.activation(rms[:, :], scaled, ACT.Sqrt, scale=1.0 / D, bias=const("norm_eps"))\
                        .then_inc(rms_ready, 1)
                if then:
                    preload(then)

            def high_halves(gains, a, dst=xn_hi):
                for k in (2 * a, 2 * a + 1):
                    nc.scalar.activation(dst[:, k, :], x[:, k, :], ACT.Copy, scale=gain(gains, k))\
                        .then_inc(xn_hi_ready, 1)

            def ffn(f, n0):
                def sigmoid(c, i=0):
                    act.wait_ge(gate_ready, NFC * f + c + 4 * i + 1)
                    nc.scalar.activation(sig[:, c % 2, :], gate[:, c % 2, :], ACT.Sigmoid).then_inc(sig_ready, 1)

                def step(k, i=0):
                    for n in range(n0 + down_block(k) + 6, n0 + down_block(k) + 9):
                        if n < end:
                            hi(n, 2 * i)
                    sigmoid(k + LEAD, i)
                hi_until(n0 + 8)
                sigmoid(0)
                hi_until(n0 + 9)
                sigmoid(1)
                hi_until(n0 + 11)
                sigmoid(2)
                for k in FIRST_STEPS:
                    step(k)
                with act.Fori(0, LOOP_TRIPS) as i:
                    for k in LOOP_STEPS:
                        step(k, i)
                for k in LAST_STEPS:
                    step(k)
                state["next"] = n0 + down_block(FFN_STEPS - 1) + 9
                hi_until(n0 + down_block(NFC - 1) + 5)

            act.wait_ge(gains_loaded, 16)
            def mixer_one():
                n0 = FIRST["mix_in"]

                def in_place(taken, ap, func):
                    need(act, "proj_out", taken)
                    nc.scalar.activation(ap, ap, func).then_inc(ev["fn_done"], 1)

                def root(k, features):
                    need(act, "on_done", k)
                    cols = slice(0, 2 if features == HD else 1)
                    nc.scalar.activation(norm_sb[:, cols, :], bank(3)[:, cols, :], ACT.Sqrt, scale=1.0 / features,
                                         bias=const("norm_eps")).then_inc(ev["on_root"], 1)

                hi_until(n0 + 8)
                need(act, "gla_abs", 1)
                chain(nc.scalar.activation(tmp2[:, :, :], tmp2[:, :, :], ACT.Exp, scale=-1.0))
                nc.scalar.activation(tmp2[:, :, :], tmp2[:, :, :], ACT.Ln, bias=1.0).then_inc(ev["gla_ln"], 1)
                hi_until(n0 + 10)
                need(act, "gla_min", 1)
                nc.scalar.activation(decay_to[:, :, :], tmp[:, :, :], ACT.Exp, scale=1.0 / GLA_GATE_TAU)\
                    .then_inc(ev["gla_decay"], 1)
                need(act, "lb_zero", 1)
                nc.scalar.activation(lb[:, 2:4], lb[:, 0:2], ACT.Exp).then_inc(ev["lb_exp"], 1)
                hi_until(n0 + 14)
                in_place(9, gla_in["gate"][:, :, :], ACT.Silu)
                hi_until(n0 + 16)
                in_place(11, hgrn_in["k"][:, :, :], ACT.Sigmoid)
                hi_until(n0 + 18)
                in_place(13, hgrn_in["q"][:, :, :], ACT.Silu)
                hi_until(n0 + 22)
                in_place(17, hgrn_in["gate"][:, :, :], ACT.Sigmoid)
                hi_until(n0 + 23)
                root(1, HD)
                hi_until(FIRST["mix_out"] + 5)
                need(act, "rw_mixed", 1)
                nc.scalar.activation(lora[0:64, 0, :], rw[0:64, 6, :], ACT.Tanh)
                nc.scalar.activation(lora[:, 1, :], rw[:, 7, :], ACT.Sigmoid).then_inc(ev["rw_lora_in"], 1)
                root(2, G)
                need(act, "rw_lora", 1)
                for c in range(2):
                    ins = nc.scalar.activation(iclr[:, c, :], bank(1)[:, c, :], ACT.Sigmoid, bias=const("a0", c))
                ins.then_inc(ev["rw_iclr"], 1)
                for c in range(2):
                    ins = nc.scalar.activation(sz[:, c, :], bank(0)[:, c, :], ACT.Sigmoid, bias=const("w0", c))
                chain(ins)
                nc.scalar.activation(dec[:, :, 1:], flat(sz).rearrange("p (a b) -> p a b", b=CHUNK), ACT.Exp,
                                     scale=-float(math.exp(-0.5))).then_inc(ev["rw_decay"], 1)
                need(act, "pool_ready", 1)
                nc.scalar.activation(g_r[:, :, :], bank(2), ACT.Copy).then_inc(ev["rw_g"], 1)
                need(act, "rw_kk_n", 1)
                nc.scalar.activation(sq[:, :, :], bank(3), ACT.Sqrt).then_inc(ev["rw_kk_root"], 1)
                need(act, "rw_tok", 2)
                nc.scalar.activation(b_tok[:, :, :], bank(5), ACT.Copy).then_inc(ev["rw_tok_act"], 1)
                need(act, "rw_tok", 3)
                nc.scalar.activation(k_tok[:, :, :], bank(6), ACT.Copy).then_inc(ev["rw_tok_act"], 1)
                need(act, "rw_var", 1)
                nc.scalar.activation(rms_r[:, :, :], bank(5), ACT.Sqrt, scale=1.0 / HD, bias=const("gn_eps")).then_inc(ev["rw_gn_root"], 1)
                hi_until(FIRST["mix_out"] + 8 + 4)


            def lru():
                n0 = FIRST["lru_in"]
                need(act, "lru_abs", 1)
                chain(nc.scalar.activation(sp[:, 1, :], sp[:, 0, :], ACT.Exp, scale=-1.0))
                nc.scalar.activation(sp[:, 1, :], sp[:, 1, :], ACT.Ln, bias=1.0).then_inc(ev["lru_ln"], 1)
                hi_until(n0 + 2 * KD + 4)
                for half in range(2):
                    need(act, "lru_z", half + 1)
                    fours = slice(4 * half, 4 * half + 4)
                    nc.scalar.activation(gelu_z[:, fours, :], gelu_z[:, fours, :], ACT.Sigmoid,
                                         scale=2 * math.sqrt(2 / math.pi)).then_inc(ev["lru_gelu"], 1)
                for i in range(KD):
                    n = FIRST["lru_gates"] + i // 2
                    if i % 2:
                        act.wait_ge(used[slot(n)], nth(n))
                    else:
                        need(act, "lru_gates_done", i // 2 + 1)
                    nc.scalar.activation(lru_a[:, i, :], bank(4 + i % 4)[:, 0, :], ACT.Sigmoid, bias=const("b_r", i))
                    nc.scalar.activation(lru_i[:, i, :], bank(4 + i % 4)[:, 1, :], ACT.Sigmoid, bias=const("b_i", i))\
                        .then_inc(ev["lru_ri"], 1)
                    hi_until(FIRST["lru_gates"] + i // 2 + 5)
                act.wait_ge(ev["lru_ri"], KD)
                need(act, "lru_sp", 1)
                for half in range(2):
                    for i in range(4 * half, 4 * half + 4):
                        ins = nc.scalar.activation(lru_t[:, i, :], lru_a[:, i, :], ACT.Tanh, scale=sp[:, 3, i:i + 1])
                    chain(ins)
                    for i in range(4 * half, 4 * half + 4):
                        ins = nc.scalar.activation(lru_a[:, i, :], lru_a[:, i, :], ACT.Exp, scale=sp[:, 2, i:i + 1])
                    ins.then_inc(ev["lru_a"], 1)
                for half in range(2):
                    fours = slice(4 * half, 4 * half + 4)
                    need(act, "lru_m", half + 1)
                    nc.scalar.activation(lru_t[:, fours, :], lru_t[:, fours, :], ACT.Sqrt).then_inc(ev["lru_root"], 1)
                hi_until(FIRST["lru_out"] + 8 + 4)

            def heads_square(k, a):
                pairs = 4 * (k - 1) + a
                need(act, "proj_out", TAKEN_BEFORE["kv" if k == 1 else "q_in"] + 2 * a + 2)
                if pairs >= 2:
                    need(act, "heads_ready", pairs - 1)
                nc.scalar.activation(sq_heads[a % 2][:, :, :], raw_heads[:, 2 * a:2 * a + 2, :], ACT.Square)\
                    .then_inc(ev["heads_sq"], 1)

            def heads_root(k, a):
                need(act, "heads_n", 4 * (k - 1) + a + 1)
                nc.scalar.activation(sq_heads[a % 2][:, :, :], bank(2 + a % 2), ACT.Sqrt, scale=1.0 / HD,
                                     bias=const("norm_eps")).then_inc(ev["heads_root"], 1)

            def heads(k, n0):
                hi_until(n0 + 8)
                heads_square(k, 0)
                hi_until(n0 + 9)
                heads_square(k, 1)
                hi_until(n0 + 10)
                heads_root(k, 0)
                heads_root(k, 1)
                hi_until(n0 + 11)
                heads_square(k, 2)
                hi_until(n0 + 12)
                heads_root(k, 2)
                hi_until(n0 + 13)
                heads_square(k, 3)
                heads_root(k, 3)

            def shared_kv():
                n0 = FIRST["kv"]
                hi_until(n0 + 7)
                for a in range(4):
                    high_halves("g_ffn_e", a, y_hi)
                heads(1, n0)
                hi_until(n0 + 2 * KD - 1)
                act.wait_ge(used[slot(n0 + 2 * KD - 1)], nth(n0 + 2 * KD - 1))
                need(act, "col_out", 1)
                for t in range(TB):
                    ins = nc.scalar.activation(v_heads[:, t, :], ps[:, 2 * t:2 * t + 2, :].rearrange("p b s -> p (b s)"),
                                               ACT.Copy, scale=rstd_col[:, t:t + 1])
                ins.then_inc(ev["v_out"], 1)
                hi_until(n0 + 2 * KD + 4)

            def attention():
                n0 = FIRST["q_in"]
                heads(2, n0)
                need(act, "at_sep", 1)
                for step in range(KD + 2):
                    if step < KD:
                        c = step
                        need(act, "at_mask", c + 1)
                        z = ps[:, 2 * (c % 2):2 * (c % 2) + 2, 0:3 * P].rearrange("p b (m s) -> p b m s", m=3)
                        if c >= 2:
                            need(act, "at_w", c - 1)
                        for out_ap, scale in ((stick[c % 2][:, :, :], QK_SCALE), (pass_on[c % 2][:, :, 0:P], -QK_SCALE)):
                            ins = nc.scalar.activation(out_ap.rearrange("p (b m) s -> p b m s", b=2), z, ACT.Sigmoid, scale=scale)
                        ins.then_inc(ev["at_sig"], 1)
                    if 0 <= step - 1 < KD:
                        c = step - 1
                        need(act, "at_wt", c + 1)
                        nc.scalar.activation(weights_t[c % 2][:, :, :].rearrange("p (b m) s -> p b (m s)", b=2),
                                             ps[:, 4:6, 0:3 * P], ACT.Copy).then_inc(ev["at_wt_out"], 1)
                    if 0 <= step - 2 < KD:
                        c = step - 2
                        need(act, "at_o", c + 1)
                        nc.scalar.activation(y_hi[:, c, :], bank(6 + c % 2)[:, 0, :], ACT.Copy).then_inc(ev["at_yhi"], 1)
                hi_until(FIRST["attn_out"] + 8 + 4)

            act.wait_ge(table_ready, 1)
            hi_until(0)
            steps = [
                lambda: norm(0, "g_ffn_a"),
                lambda: ffn(0, FIRST["ffn_a"]),
                lambda: (act.wait_ge(const_loaded, 16), norm(1, "g_mix"), mixer_one()),
                lambda: norm(2, "g_ffn_b"),
                lambda: ffn(1, FIRST["ffn_b"]),
                lambda: None,
                lambda: (norm(3, "both"), ffn(2, FIRST["ffn_c"])),
                lambda: (norm(5, "g_lru"), lru()),
                lambda: (norm(6, "g_ffn_d"), ffn(3, FIRST["ffn_d"])),
                lambda: (norm(7, "g_kv", None), shared_kv()),
                lambda: ffn(4, FIRST["ffn_e"]),
                lambda: (norm(8, "g_attn", None), attention()),
                lambda: (norm(9, "g_ffn_f"), ffn(5, FIRST["ffn_f"])),
            ]
            for step in steps:
                step()

        @block.vector
        def _(v):
            chain = Chain(v, dve_chain)
            x_tiles, xn_tiles, updates, norms, roots = [0], [0], [0], [0], [0]
            end_of_stream = [False]

            def lo(n, i=0):
                v.wait_ge(hi_ready[slot(n)], nth(n, i))
                nc.vector.tensor_tensor(w_lo[:, slot(n), :], raw[:, slot(n), :], w_hi[:, slot(n), :],
                                        ALU.subtract).then_inc(lo_ready[slot(n)], 1)

            def low_halves(gains, a, hi=xn_hi, lo=xn_lo):
                for k in (2 * a, 2 * a + 1):
                    xn_tiles[0] += 1
                    v.wait_ge(xn_hi_ready, xn_tiles[0])
                    nc.vector.scalar_tensor_tensor(lo[:, k, :], x[:, k, :], gain(gains, k), hi[:, k, :],
                                                   ALU.mult, ALU.subtract).then_inc(xn_lo_ready, 1)

            def add_squares(a, both):
                v.wait_ge(sq_ready, 4 * norms[0] + a + 1)
                sums = [(squares, squares_sum)] + ([(gained_squares, gained_sum)] if both else [])
                for of, total in sums:
                    if a == 1:
                        chain(nc.vector.tensor_tensor(total, of[:, 0, :], of[:, 1, :], ALU.add))
                    elif a > 1:
                        ins = nc.vector.tensor_tensor(total, total, of[:, a, :], ALU.add)
                        if a == 2:
                            chain(ins)
                if a == 3:
                    ins.then_inc(sum_ready, 1)

            def next_x(scale, gains=None, last_block=None):
                for a in range(5):
                    if scale is None and a < 4:
                        v.wait_ge(x_loaded[a], 16)
                        if a in DVE_SPLITS:
                            lo(a)
                    if a < 4 and scale is not None:
                        if a < 3:
                            v.wait_ge(acc_done, 3 * updates[0] + a + 1)
                        else:
                            v.wait_ge(used[slot(last_block)], nth(last_block))
                        nc.vector.scalar_tensor_tensor(pair_of_x(a), ps[:, a, :], scale, pair_of_x(a), ALU.mult, ALU.add)\
                            .then_inc(x_ready, 1)
                        x_tiles[0] += 1
                        v.wait_ge(x_ready, x_tiles[0])
                    if a:
                        if gains:
                            low_halves(gains, a - 1)
                        if not end_of_stream[0]:
                            add_squares(a - 1, gains == "both")
                if scale is not None:
                    updates[0] += 1
                if not end_of_stream[0]:
                    inverse_root(gains == "both")

            def inverse_root(both):
                norms[0] += 1

                def reciprocal(out_ap):
                    roots[0] += 1
                    v.wait_ge(rms_ready, roots[0])
                    return nc.vector.reciprocal(out_ap, rms[:, :])
                if both:
                    reciprocal(first_rstd).then_inc(first_rstd_ready, 1)
                    v.wait_ge(first_rstd_ready, 1)
                    chain(nc.vector.tensor_tensor(scaled, ps[:, 3, SEQ:], first_rstd, ALU.mult))
                    nc.vector.tensor_tensor(scaled, scaled, first_rstd, ALU.mult).then_inc(scaled_ready, 1)
                    chain(reciprocal(rstd[:, :]))
                    ins = nc.vector.tensor_tensor(rstd[:, :], rstd[:, :], first_rstd, ALU.mult)
                else:
                    ins = reciprocal(rstd[:, :])
                ins.then_inc(rstd_ready, 1)
                v.wait_ge(rstd_ready, norms[0])

            def ffn(f, n0, meanwhile=None):
                def hidden(c, i=0):
                    tile_up = n0 + gate_block(c) + 1
                    v.wait_ge(used[slot(tile_up)], nth(tile_up, 2 * i))
                    nc.vector.tensor_tensor(gate[:, c % 2, :], ps[:, 4 + c % 4, 0:SEQ], rstd[:, :], ALU.mult)\
                        .then_inc(gate_ready, 1)
                    chain(nc.vector.tensor_tensor(up[:, :], ps[:, 4 + c % 4, SEQ:], rstd[:, :], ALU.mult))
                    v.wait_ge(sig_ready, NFC * f + c + 4 * i + 1)
                    chain(nc.vector.tensor_tensor(gs[:, :], gate[:, c % 2, :], sig[:, c % 2, :], ALU.mult))
                    if c >= 2:
                        down = n0 + down_block(c - 2)
                        v.wait_ge(used[slot(down)], nth(down, 2 * i))
                    nc.vector.tensor_tensor(h_hi[:, c % 2, :], up[:, :], gs[:, :], ALU.mult)
                    chain(nc.vector.tensor_tensor(h[:, :], up[:, :], gs[:, :], ALU.mult))
                    nc.vector.tensor_tensor(h_lo[:, c % 2, :], h[:, :], h_hi[:, c % 2, :], ALU.subtract)\
                        .then_inc(h_ready, 1)
                    v.wait_ge(h_ready, NFC * f + c + 4 * i + 1)

                def step(k, i=0):
                    lo(n0 + down_block(k + 2), 2 * i)
                    if k == FFN_STEPS - 1:
                        lo(n0 + down_block(NFC - 1))
                    hidden(k + LEAD, i)
                lo(n0 + down_block(0))
                hidden(0)
                lo(n0 + down_block(1))
                hidden(1)
                hidden(2)
                if meanwhile:
                    meanwhile()
                for k in FIRST_STEPS:
                    step(k)
                count = chain.count
                with v.Fori(0, LOOP_TRIPS) as i:
                    chain.later = i * (3 * len(LOOP_STEPS))
                    for k in LOOP_STEPS:
                        step(k, i)
                assert chain.count == count + 3 * len(LOOP_STEPS)
                chain.count, chain.later = count + 3 * len(LOOP_STEPS) * LOOP_TRIPS, 0
                for k in LAST_STEPS:
                    step(k)

            def gain_x():
                for a in range(4):
                    for k in (2 * a, 2 * a + 1):
                        ins = nc.vector.scalar_tensor_tensor(x[:, k, :], x[:, k, :], const("g_final", k), first_rstd,
                                                             ALU.mult, ALU.mult)
                    ins.then_inc(x_ready, 1)
                    x_tiles[0] += 1
                    v.wait_ge(x_ready, x_tiles[0])

            def signal(ins, name):
                ins.then_inc(ev[name], 1)
                sent[name] = sent.get(name, 0) + 1
                v.wait_ge(ev[name], sent[name])

            sent = {}
            tt = nc.vector.tensor_tensor
            stt = nc.vector.scalar_tensor_tensor
            tsc = nc.vector.tensor_scalar

            def take(n0, i, dst, scale=None):
                v.wait_ge(used[slot(n0 + i)], nth(n0 + i))
                src = ps[0:dst.shape[0], 4 + i % 4, 0:SEQ]
                by = rstd[0:dst.shape[0], :]
                if scale is None:
                    ins = tt(dst, src, by, ALU.mult)
                else:
                    ins = stt(dst, src, scale, by, ALU.mult, ALU.mult)
                signal(ins, "proj_out")

            def split_y(tile, make, scratch):
                make(y_hi[:, tile, :])
                chain(make(scratch))
                signal(tt(y_lo[:, tile, :], scratch, y_hi[:, tile, :], ALU.subtract), "y_ready")

            def value_rows(k):
                need(v, "vt_done", k)
                signal(nc.vector.tensor_copy(v_rows[:, :, :], bank(2)), "vt_out")

            def decayed_attention(src, k, first_tile, meanwhile=None):
                chain(nc.vector.memset(decay_from[:, :, :], 1.0))
                chain(nc.vector.memset(scores[:, :, :], 0.0))
                for lev in range(8):
                    n = 1 << lev
                    b = lev % 2
                    if lev == 1 and meanwhile:
                        meanwhile()
                    chain(tt(q_dec[b][:, :, :], src["q"][:, :, :], decay_to[:, :, :], ALU.mult))
                    signal(tt(k_dec[b][:, :, :], src["k"][:, :, :], decay_from[:, :, :], ALU.mult), "gla_qk")
                    if n < P:
                        to, frm = (flat(a).rearrange("p (m e s) -> p m e s", e=2, s=n) for a in (decay_to, decay_from))
                        m = 2 * SEQ // (2 * n)
                        chain(tt(frm[:, :, 0, :], frm[:, :, 0, :], to[:, :, 1, n - 1:n].broadcast_to([P, m, n]), ALU.mult))
                        chain(tt(to[:, :, 1, :], to[:, :, 1, :], to[:, :, 0, n - 1:n].broadcast_to([P, m, n]), ALU.mult))
                    take_level(lev, k)
                    mix_tile(first_tile + lev)
                take_level(8, k)
                mix_tile(first_tile + 8)

            def take_level(lev, k):
                need(v, "sc_done", 9 * (k - 1) + lev + 1)
                b = 2 * (lev % 2)
                if lev < 8:
                    mask = over(const("level", lev, P), 8).bitcast(U32)
                    signal(nc.vector.copy_predicated(scores[:, :, :], mask, pair(b)), "sc_out")
                else:
                    signal(nc.vector.tensor_copy(scores_far[:, :, :].rearrange("p (j c) t -> p j (c t)", j=2),
                                                 ps[:, b:b + 2, 0:2 * P]), "sc_out")

            def attended(k):
                need(v, "o_done", k)
                chain(nc.vector.tensor_copy(o_sb[:, :, :], bank(2)))
                signal(tt(tmp[:, :, :], o_sb[:, :, :], o_sb[:, :, :], ALU.mult), "o_sq")

            def normalise(k, per_head):
                need(v, "on_root", k)
                cols = slice(0, 2 if per_head else 1)
                chain(nc.vector.reciprocal(norm_sb[:, cols, :], norm_sb[:, cols, :]))
                by = norm_sb[:, :, :] if per_head else norm_sb[:, 0:1, :].broadcast_to([P, 2, SEQ])
                chain(tt(o_sb[:, :, :], o_sb[:, :, :], by, ALU.mult))

            def pooling():
                previous = pool_in
                for step, group in ((1, 0), (2, 1), (4, 2), (8, 3)):
                    now = win_a if group % 2 == 0 else win_b
                    chain(tt(now[:, :, PAD:], previous[:, :, PAD:], previous[:, :, PAD - step:PAD + SEQ - step], ALU.add))
                    c, rows = group // 2, slice(HD * (group % 2), HD * (group % 2) + HD)
                    chain(tt(tmp[rows, c, :], now[rows, c, PAD:],
                             const("inv_count", c, SEQ)[rows, :], ALU.mult))
                    ins = tt(tmp[rows, c, :], tmp[rows, c, :], pool_in[rows, c, PAD:], ALU.subtract)
                    if group < 3:
                        chain(ins)
                    previous = now
                signal(ins, "pool_ready")

            def pooled():
                need(v, "pool_done", 1)
                for c in range(2):
                    split_y(c, lambda out: tsc(out, bank(7)[:, c, :], const("pool_b", c), const("pool_scale", c),
                                               ALU.add, ALU.mult), tmp2[:, c, :])

            def mix_tile(i):
                n0 = FIRST["mix_in"]
                places = [ga_sb[0:32, :]] + [buf[:, c, :] for buf in (
                    gla_in["q"], gla_in["k"], gla_in["v"], gla_in["gate"], hgrn_in["k"], hgrn_in["q"], hgrn_in["v"],
                    hgrn_in["gate"], pool_in[:, :, PAD:]) for c in range(2)] + [rw_raw[:, c, 1:] for c in range(8)]
                if i < len(places):
                    take(n0, i, places[i], QK_SCALE if i in (1, 2) else None)

            def mixer_one():
                v.wait_ge(const_loaded, 16)
                chain(nc.vector.memset(rw_raw[:, :, 0:1], 0.0))
                for buf in (pool_in, win_a, win_b):
                    chain(nc.vector.memset(buf[:, :, 0:PAD], 0.0))
                logits = const("lb_logits")
                signal(tt(lb[:, 0:2], logits, logits, ALU.subtract), "lb_zero")
                for i in range(4):
                    mix_tile(i)
                need(v, "gla_z", 1)
                for c in range(2):
                    chain(tsc(tmp[:, c, :], bank(3)[:, c, :], const("gla_b", c), None, ALU.add))
                signal(stt(tmp2[:, :, :], tmp[:, :, :], -1.0, tmp[:, :, :], ALU.mult, ALU.max), "gla_abs")
                mix_tile(4)
                need(v, "gla_ln", 1)
                signal(stt(tmp[:, :, :], tmp[:, :, :], 0.0, tmp2[:, :, :], ALU.min, ALU.subtract), "gla_min")
                mix_tile(5)
                mix_tile(6)
                need(v, "lb_exp", 1)
                chain(nc.vector.reciprocal(lb[:, 4:6], lb[:, 2:4]))
                chain(tt(lb[:, 4:6], lb[:, 4:6], lb[:, 2:4], ALU.mult))
                chain(tt(lb[:, 6:8], lb[:, 4:6], lb[:, 4:6], ALU.subtract))
                chain(tsc(lb[:, 0:2], lb[:, 6:8], -1.0, 1.0, ALU.mult, ALU.add))
                value_rows(1)
                mix_tile(7)
                need(v, "gla_decay", 1)
                decayed_attention(gla_in, 1, 8)
                attended(1)
                mix_tile(17)
                need(v, "on_done", 1)
                need(v, "fn_done", 3)
                for c in range(2):
                    chain(tsc(tmp[:, c, :], hgrn_in["k"][:, c, :], lb[:, c:c + 1], lb[:, 6 + c:7 + c], ALU.mult, ALU.add))
                chain(tsc(hgrn_in["k"][:, :, :], tmp[:, :, :], -1.0, 1.0, ALU.mult, ALU.add))
                chain(tsc(decay_to[:, :, :], tmp[:, :, :], GATE_FLOOR, None, ALU.max))
                mix_tile(18)
                value_rows(2)
                signal(tsc(hgrn_in["q"][:, :, :], hgrn_in["q"][:, :, :], QK_SCALE, None, ALU.mult), "hg_ready")
                mix_tile(19)

                def gla_out():
                    normalise(1, True)
                    for c in range(2):
                        split_y(6 + c, lambda out: stt(out, o_sb[:, c, :], const("gla_norm", c), gla_in["gate"][:, c, :],
                                                       ALU.mult, ALU.mult), tmp[:, c, :])
                decayed_attention(hgrn_in, 2, 20, gla_out)
                attended(2)
                shifted()
                need(v, "on_done", 2)
                pooling()
                normalise(2, False)
                for c in range(2):
                    split_y(2 + c, lambda out: stt(out, o_sb[:, c, :], const("hgrn_norm", c), hgrn_in["gate"][:, c, :],
                                                   ALU.mult, ALU.mult), tmp2[:, c, :])
                pooled()
                rwkv()

            def shifted():
                chain(tt(rw[:, :, :], rw_raw[:, :, 0:SEQ], rw_raw[:, :, 1:], ALU.subtract))
                for i in (6, 7, 0, 1, 2, 3, 4, 5):
                    ins = stt(rw[:, i, :], rw[:, i, :], const("mu", i), rw_raw[:, i, 1:], ALU.mult, ALU.add)
                    if i == 7:
                        signal(ins, "rw_mixed")
                chain(ins)
                for c in range(2):
                    chain(tsc(kk[:, c, :], rw[:, 2 + c, :], const("k_k", c), None, ALU.mult))
                signal(tt(sq[:, :, :], kk[:, :, :], kk[:, :, :], ALU.mult), "rw_kk_sq")
                chain(nc.vector.memset(dec[:, :, 0:1], 0.0))

            def rwkv():
                r_in, k_in, v_in = rw[:, 0:2, :], rw[:, 2:4, :], rw[:, 4:6, :]
                need(v, "rw_iclr", 1)
                for c in range(2):
                    chain(tsc(k_new[:, c, :], iclr[:, c, :], -1.0, const("k_a", c), ALU.add, ALU.mult))
                chain(stt(k_new[:, :, :], k_new[:, :, :], 1.0, k_in, ALU.add, ALU.mult))
                need(v, "rw_kk_root", 1)
                chain(tsc(sq[:, :, :], sq[:, :, :], 1e-12, None, ALU.max))
                chain(nc.vector.reciprocal(sq[:, :, :], sq[:, :, :]))
                chain(tt(kk[:, :, :], kk[:, :, :], sq[:, :, :], ALU.mult))
                need(v, "rw_decay", 1)
                chain(nc.vector.tensor_tensor_scan(flat(cum), flat(dec), const("scan_one"), 0.0, ALU.mult, ALU.add))

                def by_chunk(ap):
                    return ap.rearrange("p c (q s) -> p (c q) s", s=CHUNK)
                after, before = cum[:, :, 1:], cum[:, :, 0:CHUNK]
                last = cum[:, :, CHUNK:].broadcast_to([P, 8, CHUNK])
                chain(nc.vector.tensor_copy(last_dec[:, :], cum[:, :, CHUNK:].rearrange("p a b -> p (a b)")))
                chain(nc.vector.reciprocal(by_chunk(inv_cum), after))
                chain(tt(by_chunk(r_dec), by_chunk(r_in), after, ALU.mult))
                signal(tt(by_chunk(a_dec), by_chunk(kk), before, ALU.mult), "rw_dec")
                chain(tt(b_dec[:, :, :], kk[:, :, :], iclr[:, :, :], ALU.mult))
                chain(tt(b_dec[:, :, :], b_dec[:, :, :], inv_cum[:, :, :], ALU.mult))
                signal(tt(by_chunk(b_last), by_chunk(b_dec), last, ALU.mult), "rw_dec")
                chain(tt(kk_dec[:, :, :], k_new[:, :, :], inv_cum[:, :, :], ALU.mult))
                signal(tt(by_chunk(k_last), by_chunk(kk_dec), last, ALU.mult), "rw_dec")
                for c in range(2):
                    ins = stt(sq[:, c, :], r_in[:, c, :], const("r_k", c), k_new[:, c, :], ALU.mult, ALU.mult)
                signal(ins, "rw_bonus_in")
                need(v, "rw_tok", 1)
                chain(nc.vector.tensor_copy(a_tok[:, :, :], bank(4)))
                need(v, "rw_tok", 4)
                signal(nc.vector.tensor_copy(v_tok[:, :, :], bank(7)), "rw_tok_out")
                need(v, "rw_bonus", 1)
                chain(tt(bonus[:, :, :], bank(3), v_in, ALU.mult))
                need(v, "rw_mat", 1)
                signal(tt(l_t[:, :, :], pair(0), over(const("strict_up"), 8), ALU.mult), "rw_mat_out")
                need(v, "rw_mat", 2)
                signal(stt(inv[:, :, :], pair(4), -1.0, over(const("level_low", 0, P), 8), ALU.mult, ALU.mult), "rw_mat_out")
                chain(tt(inv[:, :, :], inv[:, :, :], over(const("ident"), 8), ALU.add))
                chain(stt(inv_t[:, :, :], l_t[:, :, :], -1.0, over(const("level", 1, P), 8), ALU.mult, ALU.mult))
                signal(tt(inv_t[:, :, :], inv_t[:, :, :], over(const("ident"), 8), ALU.add), "rw_z_out")
                need(v, "rw_mat", 3)
                signal(tt(lak_t[:, :, :], pair(0), over(const("strict_up"), 8), ALU.mult), "rw_mat_out")
                need(v, "rw_mat", 4)
                signal(tt(mrb_t[:, :, :], pair(2), over(const("incl_up"), 8), ALU.mult), "rw_mat_out")
                need(v, "rw_mat", 5)
                signal(tt(mrk_t[:, :, :], pair(0), over(const("incl_up"), 8), ALU.mult), "rw_mat_out")
                need(v, "rw_lv", 1)
                for lev in range(1, 6):
                    for j in range(2):
                        half = slice(4 * j, 4 * j + 4)
                        need(v, "rw_y", 2 * (lev - 1) + j + 1)
                        signal(tt(y_m[:, half, :], bank(j, 4), over(const("level_low", lev, P), 4), ALU.mult), "rw_ym")
                    for j in range(2):
                        half = slice(4 * j, 4 * j + 4)
                        need(v, "rw_z", 2 * (lev - 1) + j + 1)
                        if lev < 5:
                            chain(tt(inv[:, half, :], inv[:, half, :], bank(2 + j, 4), ALU.subtract))
                        signal(tt(inv_t[:, half, :], inv_t[:, half, :], bank(4 + j, 4), ALU.subtract), "rw_z_out")
                signal(nc.vector.tensor_copy(lv[:, :, :], bank(6)), "rw_lv_out")
                need(v, "rw_wt", 1)
                chain(nc.vector.tensor_copy(w_t[:, :, :], bank(0)))
                need(v, "rw_ut", 1)
                signal(nc.vector.tensor_copy(u_tilde[:, :, :], bank(1)), "rw_wu_out")
                for q in range(NCH):
                    rows, t = slice(CHUNK * (q % 2), CHUNK * (q % 2) + CHUNK), q // 2
                    if q == 0:
                        signal(tsc(u[rows, t, :], u_tilde[rows, t, :], -1.0, None, ALU.mult), "rw_u_out")
                    else:
                        need(v, "rw_u", q)
                        signal(stt(u[rows, t, :], ps[rows, 2 + q % 2, 0:G], -1.0, u_tilde[rows, t, :],
                                   ALU.mult, ALU.subtract), "rw_u_out")
                    if q + 1 < NCH:
                        if q:
                            for c in range(2):
                                chain(tsc(state_dec[:, c, :], state[q][:, c, :], last_dec[:, 4 * c + q:4 * c + q + 1],
                                          None, ALU.mult))
                        need(v, "rw_st", q + 1)
                        new = ps[:, 4 + q % 2, 0:2 * P].rearrange("p (c s) -> p c s", c=2)
                        ins = tt(state[q + 1][:, :, :], new, over(const("head_ones"), 2), ALU.mult)
                        if q:
                            chain(ins)
                            ins = tt(state[q + 1][:, :, :], state[q + 1][:, :, :], state_dec[:, :, :], ALU.add)
                        signal(ins, "rw_st_out")
                need(v, "rw_o", 1)
                signal(nc.vector.tensor_copy(o_r[:, :, :], bank(6)), "rw_o_out")
                need(v, "rw_mean", 1)
                chain(stt(dev[:, :, :], bank(4), -1.0 / HD, o_r[:, :, :], ALU.mult, ALU.add))
                signal(tt(t_r[:, :, :], dev[:, :, :], dev[:, :, :], ALU.mult), "rw_dev")
                need(v, "rw_gn_root", 1)
                chain(nc.vector.reciprocal(rms_r[:, :, :], rms_r[:, :, :]))
                chain(tt(dev[:, :, :], dev[:, :, :], rms_r[:, :, :], ALU.mult))
                for c in range(2):
                    chain(tsc(dev[:, c, :], dev[:, c, :], const("ln_w", c), const("ln_b", c), ALU.mult, ALU.add))
                chain(tt(dev[:, :, :], dev[:, :, :], bonus[:, :, :], ALU.add))
                need(v, "rw_g", 1)
                for c in range(2):
                    split_y(4 + c, lambda out: tt(out, dev[:, c, :], g_r[:, c, :], ALU.mult), t_r[:, c, :])

            def lru():
                n0 = FIRST["lru_in"]
                chain(nc.vector.memset(rec[:, :, 0:TAPS - 1], 0.0))
                signal(stt(sp[:, 0, :], const("lam"), -1.0, const("lam"), ALU.mult, ALU.max), "lru_abs")
                need(v, "lru_ln", 1)
                chain(tsc(sp[:, 0, :], const("lam"), -1.0, 0.0, ALU.mult, ALU.max))
                chain(tt(sp[:, 0, :], sp[:, 0, :], sp[:, 1, :], ALU.add))
                chain(tsc(sp[:, 2, :], sp[:, 0, :], -LRU_C, None, ALU.mult))
                signal(tsc(sp[:, 3, :], sp[:, 0, :], LRU_C, None, ALU.mult), "lru_sp")
                for i in range(KD):
                    take(n0, i, rec[:, i, TAPS - 1:])
                    chain(tsc(xc[:, i, :], rec[:, i, 0:SEQ], const("conv_w", i), const("conv_b", i), ALU.mult, ALU.add))
                    for k in range(1, TAPS):
                        if k == TAPS - 1:
                            chain(stt(y_hi[:, i, :], rec[:, i, k:k + SEQ], const("conv_w", k * KD + i), xc[:, i, :],
                                      ALU.mult, ALU.add))
                        chain(stt(xc[:, i, :], rec[:, i, k:k + SEQ], const("conv_w", k * KD + i), xc[:, i, :],
                                  ALU.mult, ALU.add))
                    signal(tt(y_lo[:, i, :], xc[:, i, :], y_hi[:, i, :], ALU.subtract), "lru_conv")
                for half in range(2):
                    fours = slice(4 * half, 4 * half + 4)
                    for i in range(4 * half, 4 * half + 4):
                        take(n0, KD + i, lru_gate[:, i, :])
                    g, z = lru_gate[:, fours, :], gelu_z[:, fours, :]
                    chain(tt(z, g, g, ALU.mult))
                    chain(tsc(z, z, 0.044715, 1.0, ALU.mult, ALU.add))
                    signal(tt(z, z, g, ALU.mult), "lru_z")
                for half in range(2):
                    fours = slice(4 * half, 4 * half + 4)
                    need(v, "lru_gelu", half + 1)
                    chain(tt(lru_gate[:, fours, :], lru_gate[:, fours, :], gelu_z[:, fours, :], ALU.mult))
                need(v, "lru_ri", KD)
                for half in range(2):
                    fours = slice(4 * half, 4 * half + 4)
                    chain(tt(lru_h[:, fours, :], lru_i[:, fours, :], xc[:, fours, :], ALU.mult))
                for half in range(2):
                    fours = slice(4 * half, 4 * half + 4)
                    need(v, "lru_a", half + 1)
                    chain(tt(gelu_z[:, fours, :], lru_a[:, fours, :], lru_a[:, fours, :], ALU.mult))
                    signal(stt(lru_t[:, fours, :], gelu_z[:, fours, :], 1.0, lru_t[:, fours, :], ALU.add, ALU.mult), "lru_m")
                for half in range(2):
                    fours = slice(4 * half, 4 * half + 4)
                    need(v, "lru_root", half + 1)
                    chain(tt(lru_h[:, fours, :], lru_h[:, fours, :], lru_t[:, fours, :], ALU.mult))
                    for i in range(4 * half, 4 * half + 4):
                        chain(nc.vector.tensor_tensor_scan(lru_i[:, i, :], lru_a[:, i, :], lru_h[:, i, :], 0.0,
                                                           ALU.mult, ALU.add))
                        split_y(i, lambda out: tt(out, lru_i[:, i, :], lru_gate[:, i, :], ALU.mult), gelu_z[:, i, :])

            def heads_take(n0, a):
                take(n0, 2 * a, raw_heads[:, 2 * a, :])
                take(n0, 2 * a + 1, raw_heads[:, 2 * a + 1, :])

            def heads_finish(k, a, dst, by):
                need(v, "heads_root", 4 * (k - 1) + a + 1)
                both = slice(2 * a, 2 * a + 2)
                chain(nc.vector.reciprocal(sq_heads[a % 2][:, :, :], sq_heads[a % 2][:, :, :]))
                signal(stt(dst[:, both, :], raw_heads[:, both, :], const(by), sq_heads[a % 2][:, :, :], ALU.mult, ALU.mult),
                       "heads_ready")

            def shared_kv():
                n0 = FIRST["kv"]
                heads_take(n0, 0)
                heads_take(n0, 1)
                for a in range(4):
                    low_halves("g_ffn_e", a, y_hi, y_lo)
                need(v, "col_done", 1)
                signal(nc.vector.tensor_copy(rstd_col[:, :], ps[:, 3, 0:TB]), "col_out")
                heads_finish(1, 0, k_t, "k_norm")
                heads_take(n0, 2)
                heads_finish(1, 1, k_t, "k_norm")
                heads_take(n0, 3)
                heads_finish(1, 2, k_t, "k_norm")
                heads_finish(1, 3, k_t, "k_norm")

            def attention():
                n0 = FIRST["q_in"]
                for buf in pass_on:
                    chain(nc.vector.memset(buf[:, :, P:], 0.0))
                    for j in range(2):
                        chain(nc.vector.memset(buf[:, 3 * j, P:], 1.0))
                chain(nc.vector.memset(row_end[:, :, :], 0.0))
                for j in range(2):
                    ins = nc.vector.memset(row_end[:, 3 * j + 1:3 * j + 3, P:], 1.0)
                signal(ins, "at_sep")
                heads_take(n0, 0)
                heads_take(n0, 1)
                heads_finish(2, 0, q_t, "q_norm")
                heads_take(n0, 2)
                heads_finish(2, 1, q_t, "q_norm")
                heads_take(n0, 3)
                for step in range(KD + 3):
                    if step < KD:
                        c = step
                        need(v, "at_z", c + 1)
                        z = ps[:, 2 * (c % 2):2 * (c % 2) + 2, P:3 * P].rearrange("p b (m s) -> p b m s", m=2)
                        mask = const("not_before").unsqueeze(1).unsqueeze(1).broadcast_to([P, 2, 2, P])
                        signal(tt(z, z, mask, ALU.add), "at_mask")
                        if step in (0, 1):
                            heads_finish(2, 2 + step, q_t, "q_norm")
                    if 0 <= step - 1 < KD:
                        c = step - 1
                        need(v, "at_sig", c + 1)
                        chain(nc.vector.tensor_tensor_scan(flat(left)[:, ::-1], flat(pass_on[c % 2])[:, ::-1],
                                                           flat(row_end)[:, ::-1], 1.0, ALU.mult, ALU.add))
                        if c >= 2:
                            need(v, "at_wt", c - 1)
                        signal(tt(weights[c % 2][:, :, :], stick[c % 2][:, :, :], left[:, :, 1:], ALU.mult), "at_w")
                    if 0 <= step - 3 < KD:
                        c = step - 3
                        need(v, "at_yhi", c + 1)
                        signal(tt(y_lo[:, c, :], bank(6 + c % 2)[:, 0, :], y_hi[:, c, :], ALU.subtract), "y_ready")

            nc.vector.memset(table[:, :], 1.0).then_inc(table_ready, 1)
            v.wait_ge(gains_loaded, 16)
            nc.vector.tensor_tensor(gain_both[:, :], const("g_final"), const("g_ffn_c"), ALU.mult)

            def end_sublayer(scale, phase, gains, last=False):
                end_of_stream[0] = last
                next_x(scale, None if last else gains, LAST[phase] - 1)
            E_ = VERSIONS - 1
            steps = [
                lambda: next_x(None, "g_ffn_a"),
                lambda: (ffn(0, FIRST["ffn_a"]), end_sublayer(0.5, "ffn_a", "g_mix", E_ == 0)),
                lambda: (mixer_one(), end_sublayer(1.0, "mix_out", "g_ffn_b", E_ == 1)),
                lambda: None,
                lambda: (ffn(1, FIRST["ffn_b"]), end_sublayer(0.5, "ffn_b", "both", E_ == 2)),
                lambda: None,
                lambda: (ffn(2, FIRST["ffn_c"], gain_x), end_sublayer(0.5, "ffn_c", "g_lru", E_ == 4)),
                lambda: (lru(), end_sublayer(1.0, "lru_out", "g_ffn_d", E_ == 5)),
                lambda: (ffn(3, FIRST["ffn_d"]), end_sublayer(0.5, "ffn_d", "g_kv", E_ == 6)),
                lambda: shared_kv(),
                lambda: (ffn(4, FIRST["ffn_e"]),
                         end_sublayer(0.5, "ffn_e", "g_attn", E_ == 7)),
                lambda: (attention(), end_sublayer(1.0, "attn_out", "g_ffn_f", E_ == 8)),
                lambda: (ffn(5, FIRST["ffn_f"]), end_sublayer(0.5, "ffn_f", None, True)),
            ]
            for step in steps:
                step()

        @block.tensor
        def _(pe):
            pe.wait_ge(gains_loaded, 16)

            def feature_tiles(tiles, i=0, after_norm=None, between=None, halves=(xn_hi, xn_lo)):
                x_hi, x_lo = halves
                for k in range(KD):
                    if after_norm is not None:
                        pe.wait_ge(xn_lo_ready, KD * after_norm + k + 1)
                    for n, where, opens, closes in tiles:
                        if k == 0:
                            pe.wait_ge(lo_ready[slot(n)], nth(n, i))
                        wh, wl = (w[:, slot(n), k * P:k * P + P] for w in (w_hi, w_lo))
                        nc.tensor.matmul(where, wh, x_hi[:, k, :], start=k == 0 and opens, stop=False)
                        nc.tensor.matmul(where, wh, x_lo[:, k, :], start=False, stop=False)
                        ins = nc.tensor.matmul(where, wl, x_hi[:, k, :], start=False, stop=k == KD - 1 and closes)
                        if k == KD - 1:
                            ins.then_inc(used[slot(n)], 1)
                    if between and k == between[0]:
                        between[1]()

            def feature_tile(n, where, i=0, **k):
                feature_tiles([(n, where, True, True)], i, **k)

            norms = [0]

            def total_squares(both=False):
                norms[0] += 1
                pe.wait_ge(sum_ready, norms[0])
                parts = [(squares_sum, 0)] + ([(gained_sum, SEQ)] if both else [])
                for of, at in parts:
                    for half in range(2):
                        ins = nc.tensor.matmul(ps[:, 3, at:at + SEQ], const("all_ones"), of[:, half * SEQ:half * SEQ + SEQ],
                                               start=half == 0 and at == 0, stop=half == 1 and of is parts[-1][0])
                ins.then_inc(total_ready, 1)

            def add_block(n, rhs_hi, rhs_lo, i=0, start=False, stop=False):
                pe.wait_ge(lo_ready[slot(n)], nth(n, i))
                for d in range(KD):
                    where = ps[:, d // 2, (d % 2) * SEQ:(d % 2 + 1) * SEQ]
                    wh, wl = (w[:, slot(n), d * P:d * P + P] for w in (w_hi, w_lo))
                    nc.tensor.matmul(where, wh, rhs_hi, start=start and d % 2 == 0, stop=False)
                    nc.tensor.matmul(where, wh, rhs_lo, start=False, stop=False)
                    ins = nc.tensor.matmul(where, wl, rhs_hi, start=False, stop=stop and d % 2 == 1)
                    if stop and d % 2 == 1 and d < KD - 1:
                        ins.then_inc(acc_done, 1)
                ins.then_inc(used[slot(n)], 1)

            def rows_tile(n, lhs_hi, lhs_lo, i=0, start=False, stop=False, bank=0):
                pe.wait_ge(lo_ready[slot(n)], nth(n, i))
                for t in range(TB):
                    lh, ll = (a[:, t * P:t * P + P] for a in (lhs_hi, lhs_lo))
                    for c in range(2):
                        acc = ps[:, bank + 2 * t + c, :]
                        wh, wl = (w[:, slot(n), 512 * c:512 * c + 512] for w in (w_hi, w_lo))
                        nc.tensor.matmul(acc, lh, wh, start=start, stop=False)
                        nc.tensor.matmul(acc, lh, wl, start=False, stop=False)
                        ins = nc.tensor.matmul(acc, ll, wh, start=False, stop=stop)
                ins.then_inc(used[slot(n)], 1)

            def ffn(f, g, n0, total=total_squares, **source):
                def gate_up(c, i=0):
                    feature_tile(n0 + gate_block(c), ps[:, 4 + c % 4, 0:SEQ], 2 * i, **source)
                    feature_tile(n0 + gate_block(c) + 1, ps[:, 4 + c % 4, SEQ:], 2 * i, **source)

                def down(c, i=0, **k):
                    pe.wait_ge(h_ready, NFC * f + c + 4 * i + 1)
                    add_block(n0 + down_block(c), h_hi[:, c % 2, :], h_lo[:, c % 2, :], 2 * i, **k)

                def step(k, i=0):
                    down(k, i, start=k == 0)
                    gate_up(k + LEAD, i)
                if f == 0:
                    feature_tile(n0, ps[:, 4, 0:SEQ], after_norm=g)
                    feature_tile(n0 + 1, ps[:, 4, SEQ:])
                    total()
                    feature_tile(n0 + 2, ps[:, 5, 0:SEQ])
                else:
                    feature_tiles([(n0, ps[:, 4, 0:SEQ], True, False), (n0 + 1, ps[:, 4, SEQ:], False, True),
                                   (n0 + 2, ps[:, 5, 0:SEQ], True, True)], after_norm=g,
                                  between=(6, total) if total else None, **source)
                feature_tile(n0 + 3, ps[:, 5, SEQ:], **source)
                gate_up(2)
                for k in FIRST_STEPS:
                    step(k)
                with pe.Fori(0, LOOP_TRIPS) as i:
                    for k in LOOP_STEPS:
                        step(k, i)
                for k in LAST_STEPS:
                    step(k)
                for c in range(FFN_STEPS, NFC):
                    down(c, stop=c == NFC - 1)

            mm = nc.tensor.matmul

            def attention_level(lev, src, k):
                at = 9 * (k - 1) + lev
                if lev:
                    need(pe, "gla_qk", 8 * (k - 1) + lev)
                    q_of, k_of = q_dec[(lev - 1) % 2], k_dec[(lev - 1) % 2]
                else:
                    q_of, k_of = src["q"], src["k"]
                if lev >= 2:
                    need(pe, "sc_out", at - 1)
                b = 2 * (lev % 2)
                for j in range(2):
                    rows = slice(HD * j, HD * j + HD)
                    for c in range(2):
                        if lev == 8:
                            ins = mm(ps[:, b + j, c * P:c * P + P], k_of[rows, c, 0:P], q_of[rows, c, P:], start=True, stop=True)
                            continue
                        for t in range(TB):
                            cols = slice(t * P, t * P + P)
                            ins = mm(ps[:, b + j, (2 * c + t) * P:(2 * c + t + 1) * P], k_of[rows, c, cols],
                                     q_of[rows, c, cols], start=True, stop=True)
                ins.then_inc(ev["sc_done"], 1)

            def to_rows(src, b, name):
                for t in range(TB):
                    for c in range(2):
                        ins = nc.tensor.transpose(bank(b)[:, t, c * P:c * P + P], src[:, c, t * P:t * P + P], const("ident"))
                ins.then_inc(ev[name], 1)

            def attend(k):
                need(pe, "sc_out", 9 * k)
                for c in range(2):
                    for j in range(2):
                        rows = slice(HD * j, HD * j + HD)
                        cols = slice(c * P + j * HD, c * P + j * HD + HD)
                        m = 4 * j + 2 * c
                        mm(bank(2)[rows, c, 0:P], v_rows[:, 0, cols], scores[:, m, :], start=True, stop=True)
                        mm(bank(2)[rows, c, P:], v_rows[:, 0, cols], scores_far[:, 2 * j + c, :], start=True, stop=False)
                        ins = mm(bank(2)[rows, c, P:], v_rows[:, 1, cols], scores[:, m + 1, :], start=False, stop=True)
                ins.then_inc(ev["o_done"], 1)

            def attend_norm(k, per_head):
                need(pe, "o_sq", k)
                if per_head:
                    ins = mm(ps[:, 3, :], const("head_ones"), flat(tmp), start=True, stop=True)
                else:
                    mm(bank(3)[:, 0, :], const("all_ones"), tmp[:, 0, :], start=True, stop=False)
                    ins = mm(bank(3)[:, 0, :], const("all_ones"), tmp[:, 1, :], start=False, stop=True)
                ins.then_inc(ev["on_done"], 1)

            def projections(n0, g, total):
                before = taken[0]
                taken[0] += total
                todo = iter(range(4, total))
                feature_tiles([(n0 + i, ps[:, 4 + i, 0:SEQ], True, True) for i in range(4)], after_norm=g,
                              between=(5, total_squares))

                def tile(count=1):
                    for _ in range(count):
                        i = next(todo)
                        need(pe, "proj_out", before + i - 3)
                        feature_tile(n0 + i, ps[:, 4 + i % 4, 0:SEQ])
                return tile

            taken = [0]

            def mixer_one():
                tile = projections(FIRST["mix_in"], 1, 27)
                need(pe, "proj_out", 1)
                for c in range(2):
                    ins = mm(bank(3)[:, c, :], const("gla_w2")[0:32, c * P:c * P + P], ga_sb[0:32, :], start=True, stop=True)
                ins.then_inc(ev["gla_z"], 1)
                tile(3)
                need(pe, "proj_out", 7)
                to_rows(gla_in["v"], 2, "vt_done")
                tile()
                need(pe, "gla_abs", 1)
                need(pe, "vt_out", 1)
                for lev in range(9):
                    attention_level(lev, gla_in, 1)
                    tile()
                attend(1)
                tile()
                attend_norm(1, True)
                tile()
                to_rows(hgrn_in["v"], 2, "vt_done")
                tile()
                need(pe, "hg_ready", 1)
                need(pe, "on_root", 1)
                for lev in range(9):
                    attention_level(lev, hgrn_in, 2)
                    if lev < 7:
                        tile()
                attend(2)
                attend_norm(2, False)
                rwkv()
                mix_rows(6, 8)

            def mix_rows(first, end):
                for step in range(first, end):
                    i = (0, 1, 2, 3, 6, 7, 4, 5)[step]
                    need(pe, "y_ready", 6 + max(0, step - 5))
                    add_block(FIRST["mix_out"] + step, y_hi[:, i, :], y_lo[:, i, :], start=step == 0, stop=step == 7)

            def rwkv():
                need(pe, "rw_lora_in", 1)
                for c in range(2):
                    cols = slice(c * P, c * P + P)
                    mm(bank(1)[:, c, :], const("w2a2")[64:128, cols], rw[64:128, 6, :], start=True, stop=True)
                    mm(bank(0)[:, c, :], const("w2a2")[0:64, cols], lora[0:64, 0, :], start=True, stop=True)
                    ins = mm(bank(2)[:, c, :], const("g2")[:, cols], lora[:, 1, :], start=True, stop=True)
                ins.then_inc(ev["rw_lora"], 1)
                need(pe, "rw_kk_sq", 1)
                need(pe, "on_root", 2)
                mm(ps[:, 3, :], const("head_ones"), flat(sq), start=True, stop=True).then_inc(ev["rw_kk_n"], 1)
                need(pe, "pool_ready", 1)
                for c in range(2):
                    ins = mm(bank(7)[:, c, :], const("pool_w", c, P), tmp[:, c, :], start=True, stop=True)
                ins.then_inc(ev["pool_done"], 1)
                for i, src in enumerate((a_dec, b_last, k_last)):
                    need(pe, "rw_dec", i + 1)
                    to_rows(src, 4 + i, "rw_tok")
                to_rows(rw[:, 4:6, :], 7, "rw_tok")
                need(pe, "rw_bonus_in", 1)
                mm(ps[:, 3, :], const("head_ones"), flat(sq), start=True, stop=True).then_inc(ev["rw_bonus"], 1)

                def products(b, lhs, rhs):
                    for j in range(2):
                        rows = slice(HD * j, HD * j + HD)
                        for c in range(2):
                            for t in range(TB):
                                cols = slice(t * P, t * P + P)
                                ins = mm(ps[:, b + j, (2 * c + t) * P:(2 * c + t + 1) * P], lhs[rows, c, cols],
                                         rhs[rows, c, cols], start=True, stop=True)
                    ins.then_inc(ev["rw_mat"], 1)
                need(pe, "rw_g", 1)
                products(0, b_dec, a_dec)
                need(pe, "rw_tok_out", 1)
                need(pe, "rw_tok_act", 2)
                products(4, a_dec, b_dec)
                need(pe, "rw_mat_out", 1)
                products(0, kk_dec, a_dec)
                products(2, b_dec, r_dec)
                need(pe, "rw_mat_out", 3)
                products(0, kk_dec, r_dec)
                for c in range(2):
                    for j in range(2):
                        cols = slice(c * P + j * HD, c * P + j * HD + HD)
                        for t in range(TB):
                            ins = mm(bank(6)[:, t, cols], lak_t[:, 4 * j + 2 * c + t, :], v_tok[:, t, cols],
                                     start=True, stop=True)
                ins.then_inc(ev["rw_lv"], 1)
                need(pe, "rw_mat_out", 5)
                for lev in range(1, 6):
                    for j in range(2):
                        need(pe, "rw_z_out", 1 if lev == 1 else 2 * (lev - 2) + j + 2)
                        for m in range(4):
                            ins = mm(bank(j, 4)[:, m, :], l_t[:, 4 * j + m, :], inv[:, 4 * j + m, :], start=True, stop=True)
                        ins.then_inc(ev["rw_y"], 1)
                    for j in range(2):
                        need(pe, "rw_ym", 2 * (lev - 1) + j + 1)
                        for m in range(4):
                            if lev < 5:
                                mm(bank(2 + j, 4)[:, m, :], inv_t[:, 4 * j + m, :], y_m[:, 4 * j + m, :], start=True, stop=True)
                            ins = mm(bank(4 + j, 4)[:, m, :], y_m[:, 4 * j + m, :], inv_t[:, 4 * j + m, :], start=True, stop=True)
                        ins.then_inc(ev["rw_z"], 1)
                need(pe, "rw_z_out", 11)
                for c in range(2):
                    for j in range(2):
                        cols = slice(c * P + j * HD, c * P + j * HD + HD)
                        for t in range(TB):
                            ins = mm(bank(0)[HD * j:HD * j + HD, c, t * P:t * P + P], a_tok[:, t, cols],
                                     inv_t[:, 4 * j + 2 * c + t, :], start=True, stop=True)
                ins.then_inc(ev["rw_wt"], 1)
                need(pe, "rw_lv_out", 1)
                for c in range(2):
                    for j in range(2):
                        cols = slice(c * P + j * HD, c * P + j * HD + HD)
                        for t in range(TB):
                            ins = mm(bank(1)[:, t, cols], inv_t[:, 4 * j + 2 * c + t, :], lv[:, t, cols], start=True, stop=True)
                ins.then_inc(ev["rw_ut"], 1)
                need(pe, "rw_wu_out", 1)
                for q in range(NCH):
                    rows, t = slice(CHUNK * (q % 2), CHUNK * (q % 2) + CHUNK), q // 2
                    if q:
                        need(pe, "rw_st_out", q)
                        for c in range(2):
                            ins = mm(ps[rows, 2 + q % 2, c * P:c * P + P], w_t[:, c, q * CHUNK:(q + 1) * CHUNK],
                                     state[q][:, c, :], start=True, stop=True)
                        ins.then_inc(ev["rw_u"], 1)
                    need(pe, "rw_u_out", q + 1)
                    if q + 1 < NCH:
                        for c in range(2):
                            cols = slice(c * P, c * P + P)
                            mm(ps[:, 4 + q % 2, cols], b_tok[rows, t, cols], u[rows, t, cols], start=True, stop=False)
                            ins = mm(ps[:, 4 + q % 2, cols], k_tok[rows, t, cols], v_tok[rows, t, cols], start=False, stop=True)
                        ins.then_inc(ev["rw_st"], 1)
                for c in range(2):
                    for q in range(NCH):
                        t, tok = q // 2, slice(q * CHUNK, (q + 1) * CHUNK)
                        if q:
                            mm(bank(6)[:, c, tok], state[q][:, c, :], r_dec[:, c, tok], start=True, stop=False)
                        for j in range(2):
                            rows = slice(HD * j, HD * j + HD)
                            cols = slice(c * P + j * HD, c * P + j * HD + HD)
                            m, own = 4 * j + 2 * c + t, slice((q % 2) * CHUNK, (q % 2) * CHUNK + CHUNK)
                            mm(bank(6)[rows, c, tok], u[:, t, cols], mrb_t[:, m, own], start=q == 0, stop=False)
                            ins = mm(bank(6)[rows, c, tok], v_tok[:, t, cols], mrk_t[:, m, own], start=False, stop=True)
                ins.then_inc(ev["rw_o"], 1)
                mix_rows(0, 1)
                need(pe, "rw_o_out", 1)
                mm(ps[:, 4, :], const("head_ones"), flat(o_r), start=True, stop=True).then_inc(ev["rw_mean"], 1)
                mix_rows(1, 2)
                need(pe, "rw_dev", 1)
                mm(ps[:, 5, :], const("head_ones"), flat(t_r), start=True, stop=True).then_inc(ev["rw_var"], 1)
                mix_rows(2, 6)

            def lru():
                before = taken[0]
                projections(FIRST["lru_in"], 4, 2 * KD)(2 * KD - 4)
                n0 = FIRST["lru_gates"]
                for b in range(4):
                    n = n0 + b
                    need(pe, "lru_conv", 2 * b + 2)
                    pe.wait_ge(lo_ready[slot(n)], nth(n))
                    for half in range(2):
                        i = 2 * b + half
                        need(pe, *(("proj_out", before + 2 * KD - 3 + i) if i < 4 else ("lru_ri", i - 3)))
                        for gate in range(2):
                            where = bank(4 + i % 4)[:, gate, :]
                            for k in range(2):
                                at = ((half * 2 + gate) * 2 + k) * P
                                wh, wl = (w[:, slot(n), at:at + P] for w in (w_hi, w_lo))
                                mm(where, wh, y_hi[:, 2 * b + k, :], start=k == 0, stop=False)
                                mm(where, wh, y_lo[:, 2 * b + k, :], start=False, stop=False)
                                ins = mm(where, wl, y_hi[:, 2 * b + k, :], start=False, stop=k == 1)
                        ins.then_inc(used[slot(n)] if half else ev["lru_gates_done"], 1)
                for i in range(KD):
                    n = FIRST["lru_out"] + i
                    need(pe, "y_ready", 8 + i + 1)
                    add_block(n, y_hi[:, i, :], y_lo[:, i, :], start=i == 0, stop=i == KD - 1)

            def heads_squares(k, a):
                need(pe, "heads_sq", 4 * (k - 1) + a + 1)
                if a >= 2:
                    need(pe, "heads_root", 4 * (k - 1) + a - 1)
                mm(ps[:, 2 + a % 2, :], const("head_ones"), flat(sq_heads[a % 2]), start=True, stop=True)\
                    .then_inc(ev["heads_n"], 1)

            def shared_kv():
                n0 = FIRST["kv"]
                tile = projections(n0, 6, KD)
                tile()
                pe.wait_ge(rstd_ready, norms[0])
                for t in range(TB):
                    ins = mm(ps[:, 3, t:t + 1], rstd[0:1, t * P:t * P + P], const("all_ones")[0:1, 0:1], start=True, stop=True)
                ins.then_inc(ev["col_done"], 1)
                heads_squares(1, 0)
                tile()
                need(pe, "col_out", 1)
                heads_squares(1, 1)
                tile()
                heads_squares(1, 2)
                tile()
                heads_squares(1, 3)
                need(pe, "heads_root", 4)
                for k in range(KD):
                    rows_tile(n0 + KD + k, xn_hi[:, k, :], xn_lo[:, k, :], start=k == 0, stop=k == KD - 1)
                need(pe, "v_out", 1)

            def attention():
                n0 = FIRST["q_in"]
                tile = projections(n0, 8, KD)
                tile(2)
                heads_squares(2, 0)
                heads_squares(2, 1)
                tile(2)
                heads_squares(2, 2)
                heads_squares(2, 3)

                def logits(c):
                    need(pe, "heads_ready", 4 + c // 2 + 1)
                    if c == 1:
                        need(pe, "heads_root", 8)
                    if c >= 2:
                        need(pe, "at_sig", c - 1)
                    for j in range(2):
                        rows, b = slice(HD * j, HD * j + HD), 2 * (c % 2) + j
                        mm(ps[:, b, 0:2 * P], q_t[rows, c, P:], k_t[rows, c, :], start=True, stop=True)
                        ins = mm(ps[:, b, 2 * P:3 * P], q_t[rows, c, 0:P], k_t[rows, c, 0:P], start=True, stop=True)
                    ins.then_inc(ev["at_z"], 1)
                logits(0)
                logits(1)
                for c in range(KD):
                    need(pe, "at_w", c + 1)
                    if c:
                        need(pe, "at_wt_out", c)
                    for j in range(2):
                        for m in range(3):
                            ins = nc.tensor.transpose(ps[:, 4 + j, m * P:m * P + P], weights[c % 2][:, 3 * j + m, :], const("ident"))
                    ins.then_inc(ev["at_wt"], 1)
                    if c + 2 < KD:
                        logits(c + 2)
                    need(pe, "at_wt_out", c + 1)
                    if c >= 2:
                        need(pe, "y_ready", 16 + c - 1)
                    for j in range(2):
                        rows, cols = slice(HD * j, HD * j + HD), slice(c * P + HD * j, c * P + HD * j + HD)
                        o, w = bank(6 + c % 2)[rows, 0, :], weights_t[c % 2]
                        mm(o[:, P:], v_heads[:, 0, cols], w[:, 3 * j, :], start=True, stop=False)
                        mm(o[:, P:], v_heads[:, 1, cols], w[:, 3 * j + 1, :], start=False, stop=True)
                        ins = mm(o[:, 0:P], v_heads[:, 0, cols], w[:, 3 * j + 2, :], start=True, stop=True)
                    ins.then_inc(ev["at_o"], 1)
                for i in range(KD):
                    need(pe, "y_ready", 16 + i + 1)
                    add_block(FIRST["attn_out"] + i, y_hi[:, i, :], y_lo[:, i, :], start=i == 0, stop=i == KD - 1)

            steps = [
                lambda: None,
                lambda: ffn(0, 0, FIRST["ffn_a"]),
                lambda: (pe.wait_ge(const_loaded, 16), mixer_one()),
                lambda: None,
                lambda: ffn(1, 2, FIRST["ffn_b"]),
                lambda: None,
                lambda: ffn(2, 3, FIRST["ffn_c"], lambda: total_squares(True)),
                lambda: lru(),
                lambda: ffn(3, 5, FIRST["ffn_d"]),
                lambda: shared_kv(),
                lambda: ffn(4, 7, FIRST["ffn_e"], None, halves=(y_hi, y_lo)),
                lambda: attention(),
                lambda: ffn(5, 9, FIRST["ffn_f"]),
            ]
            for step in steps:
                step()


def lay_out(inp):
    import numpy as np

    def features(w, cols=None):
        w = np.asarray(w)
        m = w.shape[1] // P
        return w.reshape(KD, P, m, P).transpose(2, 1, 0, 3).reshape(m, P, BLK)

    def rows(w):
        return np.asarray(w).reshape(-1, P, BLK)

    def ffn(w_in, w_out):
        w_in, w_out = np.asarray(w_in), np.asarray(w_out)
        gate, up, down = features(w_in[:, :FF]), features(w_in[:, FF:]), rows(w_out)
        return np.stack([gate, up, down], 1).reshape(-1, P, BLK)[[which for _, which in FFN_ORDER]]

    w_in, w_out = np.asarray(inp["w_in"][0]), np.asarray(inp["w_out"][0])
    pool, hg, rw, gl = w_in[:, :G], w_in[:, G:5 * G], w_in[:, 5 * G:9 * G], w_in[:, 9 * G:]
    ga = np.zeros((D, P), np.float32)
    ga[:, :16] = gl[:, 4 * G:]
    mix_in = np.concatenate([ga, gl[:, :4 * G], hg[:, G:2 * G], hg[:, :G], hg[:, 2 * G:], pool, rw], 1)
    wr = np.asarray(inp["a_w_r_2"][0])
    wi = np.asarray(inp["a_w_i_2"][0])
    lru = np.stack([wr, wi], 1).reshape(4, 2, 2, P, 2, P).transpose(0, 3, 4, 1, 2, 5).reshape(4, P, BLK)
    a_in = np.asarray(inp["a_w_in_2"][0])
    a_in = np.concatenate([a_in[:, D:], a_in[:, :D]], 1)
    w_kv = np.asarray(inp["w_kv_2"])
    w13, w2 = inp["ffn1_w13_2"], inp["ffn1_w2_2"]
    v13, v2 = inp["ffn2_w13_2"], inp["ffn2_w2_2"]
    blocks = np.concatenate([
        ffn(inp["ffn1_w_in"][0], inp["ffn1_w_out"][0]), features(mix_in), rows(w_out)[[0, 1, 2, 3, 6, 7, 4, 5]],
        ffn(inp["ffn2_w_in"][0], inp["ffn2_w_out"][0]), ffn(w13[0], w2[0]),
        features(a_in), lru, rows(inp["a_w_out_2"][0]), ffn(v13[0], v2[0]),
        features(w_kv[:, :D]), rows(w_kv[:, D:]), ffn(w13[1], w2[1]),
        features(inp["b_w_q_2"][0]), rows(inp["b_w_o_2"][0]), ffn(v13[1], v2[1])])
    assert blocks.shape == (NBLK, P, BLK)

    cst = np.zeros((P, NCONST), np.float32)

    def put(name, a):
        at, w = CONST_AT[name]
        a = np.asarray(a)
        cst[:a.shape[0], at:at + w] = a.reshape(a.shape[0], w)

    def columns(a):
        return np.asarray(a).reshape(-1, P).T

    for name, a in [("g_ffn_a", inp["norm_ffn1"][0]), ("g_mix", inp["norm_mix"][0]), ("g_ffn_b", inp["norm_ffn2"][0]),
                    ("g_ffn_c", inp["ffn1_norm_2"][0]), ("g_lru", inp["mix_norm_2"][0]), ("g_ffn_d", inp["ffn2_norm_2"][0]),
                    ("g_kv", inp["kv_norm_2"]), ("g_ffn_e", inp["ffn1_norm_2"][1]), ("g_attn", inp["mix_norm_2"][1]),
                    ("g_ffn_f", inp["ffn2_norm_2"][1]),
                    ("g_final", inp["norm_final"]), ("lb_logits", inp["hgrn_lb_logits"][0]),
                    ("hgrn_norm", inp["hgrn_norm"][0]), ("mu", inp["rwkv_mu"][0]), ("w0", inp["rwkv_w0"][0]),
                    ("a0", inp["rwkv_a0"][0]), ("k_k", inp["rwkv_k_k"][0]), ("k_a", inp["rwkv_k_a"][0]),
                    ("r_k", inp["rwkv_r_k"][0]), ("ln_w", inp["rwkv_ln_w"][0]), ("ln_b", inp["rwkv_ln_b"][0]),
                    ("gla_b", inp["gla_b"][0]), ("gla_norm", inp["gla_norm"][0]), ("pool_b", inp["pool_b"][0]),
                    ("pool_scale", inp["pool_scale"][0]), ("conv_w", inp["a_conv_w_2"][0]), ("conv_b", inp["a_conv_b_2"][0]),
                    ("b_r", inp["a_b_r_2"][0]), ("b_i", inp["a_b_i_2"][0]), ("lam", inp["a_lambda_2"][0])]:
        put(name, columns(a))
    put("k_norm", np.concatenate([np.asarray(inp["k_norm_2"])] * 2)[:, None])
    put("q_norm", np.concatenate([np.asarray(inp["q_norm_2"][0])] * 2)[:, None])
    put("w2a2", np.concatenate([np.asarray(inp["rwkv_w2"][0]), np.asarray(inp["rwkv_a2"][0])]))
    put("g2", np.asarray(inp["rwkv_g2"][0]))
    put("gla_w2", np.asarray(inp["gla_w2"][0]))
    pool_w = np.zeros((P, 2, P), np.float32)
    for g in range(4):
        rows_g = slice(HD * (g % 2), HD * (g % 2) + HD)
        pool_w[rows_g, g // 2, rows_g] = np.asarray(inp["pool_w"][0])[g]
    put("pool_w", pool_w)
    s, t = np.arange(P)[:, None], np.arange(P)[None, :]
    put("ident", s == t)
    put("head_ones", s // HD == t // HD)
    put("all_ones", np.ones((P, P)))
    put("norm_eps", np.full((P, 1), NORM_EPS))
    put("gn_eps", np.full((P, 1), RWKV_GN_EPS))
    levels = [s == t] + [(t // n == s // n + 1) & (t // n % 2 == 1) for n in (1, 2, 4, 8, 16, 32, 64)]
    put("level", np.concatenate(levels, 1))
    put("level_low", np.concatenate([m.T for m in levels[1:7]], 1))
    same = s // CHUNK == t // CHUNK
    put("strict_up", same & (s < t))
    put("incl_up", same & (s <= t))
    put("strict_low", same & (s > t))
    put("not_before", np.where(t >= s, np.float32(MASKED_OUT), np.float32(0)))
    windows = np.array([2, 4, 8, 16])[np.arange(G) // HD]
    inv = np.float32(1) / np.minimum(np.arange(SEQ)[None, :] + 1, windows[:, None]).astype(np.float32)
    put("inv_count", inv.reshape(2, P, SEQ).transpose(1, 0, 2))
    one = np.zeros((P, 8, 65), np.float32)
    one[:, :, 0] = 1
    put("scan_one", one)
    x = np.asarray(inp["x"]).reshape(SEQ, KD, P).transpose(2, 1, 0)
    assert NBLK == len(blocks)
    return {"x_in": x, "blocks": blocks, "consts": cst}


def kernel(**inputs):
    import numpy as _np
    import concourse.bacc as _bacc
    from concourse import mybir as _mybir
    from concourse.bass_utils import run_bass_kernel_spmd as _run

    nc = _bacc.Bacc("TRN2", target_bir_lowering=False, num_devices=1)
    arrays = {name: _np.ascontiguousarray(a) for name, a in lay_out(inputs).items()}
    args = [nc.dram_tensor(name, a.shape, _mybir.dt.from_np(a.dtype), kind="ExternalInput").ap()
            for name, a in arrays.items()]
    out = nc.dram_tensor("out", (P, KD, SEQ), _mybir.dt.float32, kind="ExternalOutput").ap()
    build(nc, *args, out)
    r = _run(nc, [arrays], core_ids=[0])
    return _np.ascontiguousarray(_np.asarray(r.results[0]["out"]).transpose(2, 1, 0)).reshape(1, SEQ, D)
```

```python
import concourse.bass as bass
from concourse import mybir
from contextlib import ExitStack
import math

F32 = mybir.dt.float32
F32R = mybir.dt.float32r
U32 = mybir.dt.uint32
ALU = mybir.AluOpType
ACT = mybir.ActivationFunctionType

P = 128
SEQ = 256
D = 1024
KD = D // P
TB = SEQ // P
G = 256
FF = 2816
NFC = FF // P
HD = 64
QK_SCALE = HD ** -0.5
NORM_EPS = 1e-6
GATE_FLOOR = 1e-30
RWKV_GN_EPS = 64e-5
GLA_GATE_TAU = 16.0
CHUNK = 64
NCH = SEQ // CHUNK
LRU_C = 8.0
MASKED_OUT = -1e30

RING = 6
VERSIONS = 10
BLK = 1024


LEAD = 3
FFN_STEPS = NFC - LEAD
FIRST_STEPS = range(0, 3)
LOOP_STEPS = range(3, 7)
LOOP_TRIPS = 3
LAST_STEPS = range(3 + 4 * LOOP_TRIPS, FFN_STEPS)


def gate_block(c):
    return 2 * c if c < LEAD else 2 * LEAD + 1 + 3 * (c - LEAD)


def down_block(c):
    return 2 * LEAD + 3 * c if c < FFN_STEPS else 2 * LEAD + 3 * FFN_STEPS + c - FFN_STEPS


FFN_ORDER = sorted([(gate_block(c), 3 * c) for c in range(NFC)] + [(gate_block(c) + 1, 3 * c + 1) for c in range(NFC)]
                   + [(down_block(c), 3 * c + 2) for c in range(NFC)])


def plan_blocks():
    first, kinds = {}, []

    def add(phase, names):
        first[phase] = len(kinds)
        kinds.extend(names)

    ffn = [("gate", "up", "down")[which % 3] for _, which in FFN_ORDER]
    add("ffn_a", ffn)
    add("mix_in", ["in"] * 27)
    add("mix_out", ["rows"] * 8)
    add("ffn_b", ffn)
    add("ffn_c", ffn)
    add("lru_in", ["in"] * 8)
    add("lru_gates", ["lru"] * 4)
    add("lru_branch", ["in"] * 8)
    add("lru_out", ["rows"] * 8)
    add("ffn_d", ffn)
    add("kv", ["in"] * 8 + ["rows"] * 8)
    add("ffn_e", ffn)
    add("q_in", ["in"] * 8)
    add("attn_out", ["rows"] * 8)
    add("ffn_f", ffn)
    return first, kinds


FIRST, KINDS = plan_blocks()
DVE_SPLITS = (1, 3)
NBLK = len(KINDS)
ORDER = list(FIRST)
LAST = dict(zip(ORDER, list(FIRST.values())[1:] + [NBLK]))

CONST_WIDTHS = [
    ("g_ffn_a", KD), ("g_mix", KD), ("g_ffn_b", KD), ("g_ffn_c", KD), ("g_lru", KD), ("g_ffn_d", KD),
    ("g_kv", KD), ("g_ffn_e", KD), ("g_attn", KD), ("g_ffn_f", KD), ("g_final", KD),
    ("norm_eps", 1), ("gn_eps", 1), ("all_ones", P),
    ("lb_logits", 2), ("hgrn_norm", 2), ("mu", 8), ("w0", 2), ("a0", 2), ("k_k", 2), ("k_a", 2), ("r_k", 2),
    ("ln_w", 2), ("ln_b", 2), ("gla_b", 2), ("gla_norm", 2), ("pool_b", 2), ("pool_scale", 2),
    ("conv_w", 4 * KD), ("conv_b", KD), ("b_r", KD), ("b_i", KD), ("lam", KD), ("k_norm", 1), ("q_norm", 1),
    ("w2a2", G), ("g2", G), ("gla_w2", G), ("pool_w", 2 * P),
    ("ident", P), ("head_ones", P),
    ("level", 8 * P), ("level_low", 6 * P), ("strict_up", P), ("incl_up", P), ("strict_low", P),
    ("not_before", P), ("inv_count", 2 * SEQ), ("scan_one", 8 * 65),
]


def const_offsets():
    at, out = 0, {}
    for name, width in CONST_WIDTHS:
        out[name] = (at, width)
        at += width
    return out, at


CONST_AT, NCONST = const_offsets()
FIRST_CONSTS = sum(CONST_AT["all_ones"])


def tile_bank(i, spare):
    if i < 4:
        return 4 + i
    return i - 4 if i < 4 + spare else 4 + (i - 4 - spare) % 4


def tile_before(i, spare):
    return 0 if i < 4 + spare else i - 3 - (spare if i < 8 + spare else 0)


MIX_SPARE, LRU_SPARE, HEADS_SPARE = 3, 4, 2


def slot(n):
    return n % RING


def nth(n, i=0):
    return n // RING + 1 + i


class Chain:

    def __init__(self, engine, sem):
        self.engine, self.sem, self.count, self.later = engine, sem, 0, 0

    def __call__(self, ins):
        ins.then_inc(self.sem, 1)
        self.count += 1
        self.engine.wait_ge(self.sem, self.count + self.later)


def build(nc, x_in, blocks, consts, out):
    ctx = ExitStack()
    with ctx:
        def sb(name, shape, dt=F32):
            return ctx.enter_context(nc.sbuf_tensor(name, shape, dt))

        def sem(name):
            return ctx.enter_context(nc.semaphore(name))

        raw = sb("raw", [P, RING, BLK])
        w_hi = sb("w_hi", [P, RING, BLK], F32R)
        w_lo = sb("w_lo", [P, RING, BLK], F32R)
        x = sb("x", [P, KD, SEQ])
        xn_hi = sb("xn_hi", [P, KD, SEQ], F32R)
        xn_lo = sb("xn_lo", [P, KD, SEQ], F32R)
        y_hi = sb("y_hi", [P, KD, SEQ], F32R)
        y_lo = sb("y_lo", [P, KD, SEQ], F32R)
        h_hi = sb("h_hi", [P, 2, SEQ], F32R)
        h_lo = sb("h_lo", [P, 2, SEQ], F32R)
        cst = sb("cst", [P, NCONST])
        rstd = sb("rstd", [P, SEQ])
        rms = sb("rms", [P, SEQ])
        rstd_col = sb("rstd_col", [P, TB])
        table = sb("table", [1, 8])
        ARENA = 17100
        arena = sb("arena", [P, ARENA])
        ps = ctx.enter_context(nc.psum_tensor("ps", [P, 8, 512], F32))

        squares = arena[:, 0:TB * D].rearrange("p (a b) -> p a b", a=4)
        squares_sum = arena[:, TB * D:TB * D + 512]
        gate, sig = (arena[:, at:at + 2 * SEQ].rearrange("p (a b) -> p a b", a=2) for at in (2560, 3072))
        up, gs, h = (arena[:, at:at + SEQ] for at in (3584, 3840, 4096))

        def const(name, i=None, width=1):
            at, w = CONST_AT[name]
            if i is None:
                return cst[:, at:at + w]
            return cst[:, at + i * width:at + (i + 1) * width]

        arrived = [sem(f"arrived{s}") for s in range(RING)]
        hi_ready = [sem(f"hi_ready{s}") for s in range(RING)]
        lo_ready = [sem(f"lo_ready{s}") for s in range(RING)]
        used = [sem(f"used{s}") for s in range(RING)]
        x_loaded = [sem(f"x_loaded{a}") for a in range(4)]
        gains_loaded = sem("gains_loaded")
        const_loaded = sem("const_loaded")
        stored = sem("stored")
        x_ready = sem("x_ready")
        acc_done = sem("acc_done")
        sq_ready = sem("sq_ready")
        sum_ready = sem("sum_ready")
        total_ready = sem("total_ready")
        rms_ready = sem("rms_ready")
        first_rstd_ready = sem("first_rstd_ready")
        scaled_ready = sem("scaled_ready")
        rstd_ready = sem("rstd_ready")
        xn_hi_ready = sem("xn_hi_ready")
        xn_lo_ready = sem("xn_lo_ready")
        gate_ready = sem("gate_ready")
        sig_ready = sem("sig_ready")
        h_ready = sem("h_ready")
        table_ready = sem("table_ready")
        dve_chain = sem("dve_chain")
        act_chain = sem("act_chain")
        pool_chain = sem("pool_chain")

        gained_squares = arena[:, 4608:4608 + TB * D].rearrange("p (a b) -> p a b", a=4)
        gained_sum = arena[:, 6656:6656 + 512]
        first_rstd, scaled = arena[:, 7168:7168 + SEQ], arena[:, 7424:7424 + SEQ]
        gain_both = sb("gain_both", [P, KD])

        def gain(name, k):
            return gain_both[:, k:k + 1] if name == "both" else const(name, k)

        def pair_of_x(a):
            return x[:, 2 * a:2 * a + 2, :].rearrange("p k t -> p (k t)")


        def carve(at, *shape):
            size = 1
            for d in shape:
                size *= d
            piece = arena[:, at:at + size]
            if len(shape) == 2:
                return piece.rearrange("p (a b) -> p a b", a=shape[0])
            if len(shape) == 3:
                return piece.rearrange("p (a b c) -> p a b c", a=shape[0], b=shape[1])
            return piece

        def over(ap, n):
            return ap.unsqueeze(1).broadcast_to([ap.shape[0], n, ap.shape[1]])

        def flat(ap):
            return ap.rearrange("p a b -> p (a b)")

        def pair(b, n=8):
            return ps[:, b:b + 2, :].rearrange("p b (m s) -> p (b m) s", m=n // 2)

        def bank(b, n=2):
            return ps[:, b, :].rearrange("p (m s) -> p m s", m=n)

        rw_raw = carve(0, 8, SEQ + 1)
        rw = carve(2056, 8, SEQ)
        gla_in = dict(q=carve(4104, 2, SEQ), k=carve(4616, 2, SEQ), v=carve(5128, 2, SEQ), gate=carve(5640, 2, SEQ))
        hgrn_in = dict(q=carve(6152, 2, SEQ), k=carve(6664, 2, SEQ), v=carve(7176, 2, SEQ), gate=carve(7688, 2, SEQ))
        PAD = 16
        pool_in = carve(8200, 2, PAD + SEQ)
        win_a = carve(8744, 2, PAD + SEQ)
        win_b = carve(9288, 2, PAD + SEQ)
        decay_to = carve(9832, 2, SEQ)
        decay_from = carve(10344, 2, SEQ)
        q_dec = [carve(10856, 2, SEQ), carve(11368, 2, SEQ)]
        k_dec = [carve(11880, 2, SEQ), carve(12392, 2, SEQ)]
        v_rows = carve(12904, 2, G)
        scores = carve(13416, 8, P)
        scores_far = carve(14440, 4, P)
        o_sb = carve(14952, 2, SEQ)
        tmp = carve(15464, 2, SEQ)
        tmp2 = carve(15976, 2, SEQ)
        norm_sb = carve(16488, 2, SEQ)
        lb = sb("lb", [P, 8])
        last_dec = sb("last_dec", [P, 8])
        ga_sb = carve(14952, SEQ)
        dec, cum = (carve(520 * i, 8, CHUNK + 1) for i in range(2))
        inv_cum = carve(4104, 2, SEQ)
        kk, iclr, k_new = (carve(4624 + 512 * i, 2, SEQ) for i in range(3))
        inv = carve(4104, 8, P)
        inv_t = carve(5128, 8, P)
        r_dec, a_dec, b_dec, kk_dec, b_last, k_last = (carve(9832 + 512 * i, 2, SEQ) for i in range(6))
        g_r = carve(6160, 2, SEQ)
        bonus = carve(6672, 2, SEQ)
        v_tok = carve(13928, 2, G)
        a_tok = carve(2056, 2, G)
        b_tok = carve(2056 + 512, 2, G)
        k_tok = carve(2056 + 6 * SEQ, 2, G)
        l_t = carve(0, 8, P)
        lak_t = carve(1024, 8, P)
        mrb_t = carve(12904, 8, P)
        mrk_t = carve(8200, 8, P)
        y_m = carve(15464, 8, P)
        out_scratch = carve(9224, 2, SEQ)
        lora = carve(12904, 2, SEQ)
        sz = carve(13416, 2, SEQ)
        sq = carve(14440, 2, SEQ)
        lv = carve(7688, 2, G)
        w_t = carve(14440, 2, SEQ)
        u_tilde = carve(14952, 2, G)
        u = carve(15464, 2, G)
        state = [None] + [carve(15976 + 256 * i, 2, P) for i in range(3)]
        state_dec = carve(16744, 2, P)
        o_r, dev, t_r = a_dec, b_dec, kk_dec
        rms_r = carve(9224, 2, SEQ)

        ev = {name: sem(name) for name in (
            "proj_out gla_z gla_abs gla_ln gla_min gla_decay vt_done vt_out gla_qk sc_done sc_out o_done o_sq "
            "on_done on_root y_ready lb_zero lb_exp fn_done hg_ready pool_ready pool_done "
            "rw_mixed rw_lora_in rw_lora rw_iclr rw_decay rw_g rw_kk_sq rw_kk_n rw_kk_root rw_dec "
            "rw_bonus_in rw_bonus rw_tok rw_tok_act rw_tok_out rw_mat rw_mat_out rw_y rw_ym rw_z rw_z_out rw_lv rw_lv_out "
            "rw_wt rw_ut rw_wu_out rw_u rw_u_out rw_st rw_st_out rw_o rw_o_out rw_mean rw_dev rw_var rw_gn_root").split()}

        def need(engine, name, value):
            engine.wait_ge(ev[name], value)

        TAPS = 4
        rec = carve(0, KD, TAPS - 1 + SEQ)
        xc = carve(2072, KD, SEQ)
        lru_gate = carve(4120, KD, SEQ)
        gelu_z = carve(6168, KD, SEQ)
        lru_a = carve(8216, KD, SEQ)
        lru_i = carve(10264, KD, SEQ)
        lru_h = carve(12312, KD, SEQ)
        lru_t = carve(14360, KD, SEQ)
        sp = sb("sp", [P, 4, KD])

        raw_heads = carve(0, KD, SEQ)
        sq_heads = [carve(at, 2, SEQ) for at in (9490, 10258, 11800, 12312)]
        q_t = carve(2048, KD, SEQ)
        k_t = carve(13004, KD, SEQ)
        v_heads = carve(15052, TB, D)
        stick = [carve(4096 + 768 * i, 6, P) for i in range(2)]
        pass_on = [carve(5632 + 774 * i, 6, P + 1) for i in range(2)]
        left = carve(7180, 6, P + 1)
        row_end = carve(11026, 6, P + 1)
        weights = [carve(7954 + 768 * i, 6, P) for i in range(2)]
        weights_t = [carve(9490 + 768 * i, 6, P) for i in range(2)]

        for name in ("lru_abs lru_ln lru_xc lru_xc_hi lru_conv lru_gate_in lru_z lru_gelu lru_gates_done lru_ri lru_sp lru_a lru_m lru_root "
                     "pad_rec heads_sq heads_n heads_root heads_ready v_out at_z at_mask at_sig at_w at_wt "
                     "at_wt_out at_o at_yhi at_sep col_done col_out").split():
            ev[name] = sem(name)
        TAKEN_BEFORE = {"mix_in": 0, "lru_in": 27, "kv": 27 + 2 * KD, "q_in": 27 + 3 * KD}
        block = ctx.enter_context(nc.Block())

        @block.sync
        def _(sp):
            sp.dma_start(cst[:, 0:FIRST_CONSTS], consts[:, 0:FIRST_CONSTS]).then_inc(gains_loaded, 16)
            for n in range(RING):
                if n == 0:
                    sp.dma_start(raw[:, n, :], blocks[n, :, :]).then_inc(arrived[n], 16)
                if n < 4:
                    sp.dma_start(x[:, 2 * n:2 * n + 2, :], x_in[:, 2 * n:2 * n + 2, :]).then_inc(x_loaded[n], 16)
                if n:
                    sp.dma_start(raw[:, n, :], blocks[n, :, :]).then_inc(arrived[n], 16)
            sp.dma_start(cst[:, FIRST_CONSTS:], consts[:, FIRST_CONSTS:]).then_inc(const_loaded, 16)
            rounds = NBLK // RING
            with sp.Fori(1, rounds) as r:
                for s in range(RING):
                    sp.wait_ge(lo_ready[s], r)
                    sp.dma_start(raw[:, s, :], blocks[bass.ds(r * RING + s, 1), :, :].rearrange("o p m -> p (o m)"))\
                        .then_inc(arrived[s], 16)
            for n in range(rounds * RING, NBLK):
                sp.wait_ge(lo_ready[slot(n)], n // RING)
                sp.dma_start(raw[:, slot(n), :], blocks[n, :, :]).then_inc(arrived[slot(n)], 16)
            for a in range(4):
                sp.wait_ge(x_ready, 4 * (VERSIONS - 1) + a + 1)
                sp.dma_start(out[:, 2 * a:2 * a + 2, :], x[:, 2 * a:2 * a + 2, :]).then_inc(stored, 16)
            sp.wait_ge(stored, 16 * 4)

        @block.gpsimd
        def _(pool):
            def lo(n, i=0):
                pool.wait_ge(hi_ready[slot(n)], nth(n, i))
                nc.gpsimd.tensor_tensor(w_lo[:, slot(n), :], raw[:, slot(n), :], w_hi[:, slot(n), :],
                                        ALU.subtract).then_inc(lo_ready[slot(n)], 1)

            chain = Chain(pool, pool_chain)

            def pooling():
                add = nc.gpsimd.tensor_tensor
                need(pool, "proj_out", 19)
                need(pool, "y_ready", 2)
                previous = pool_in
                for step, group in ((1, 0), (2, 1), (4, 2), (8, 3)):
                    now = win_a if group % 2 == 0 else win_b
                    chain(add(now[:, :, PAD:], previous[:, :, PAD:], previous[:, :, PAD - step:PAD + SEQ - step], ALU.add))
                    c, rows = group // 2, slice(HD * (group % 2), HD * (group % 2) + HD)
                    chain(add(tmp[rows, c, :], now[rows, c, PAD:], const("inv_count", c, SEQ)[rows, :], ALU.mult))
                    ins = add(tmp[rows, c, :], tmp[rows, c, :], pool_in[rows, c, PAD:], ALU.subtract)
                    if group < 3:
                        chain(ins)
                    previous = now
                ins.then_inc(ev["pool_ready"], 1)
                need(pool, "pool_ready", 1)

            for phase in ORDER:
                n0 = FIRST[phase]
                if phase == "mix_out":
                    pooling()
                if phase.startswith("ffn"):
                    def step(k, i=0):
                        lo(n0 + gate_block(k + LEAD), 2 * i)
                        lo(n0 + gate_block(k + LEAD) + 1, 2 * i)
                    for n in range(n0, n0 + 2 * LEAD):
                        if n not in DVE_SPLITS:
                            lo(n)
                    for k in FIRST_STEPS:
                        step(k)
                    with pool.Fori(0, LOOP_TRIPS) as i:
                        for k in LOOP_STEPS:
                            step(k, i)
                    for k in LAST_STEPS:
                        step(k)
                else:
                    for n in range(n0, LAST[phase]):
                        lo(n)

        @block.scalar
        def _(act):
            chain = Chain(act, act_chain)
            state = {"next": 0, "norms": 0, "taken": 0}
            end = NBLK

            def hi(n, i=0):
                act.wait_ge(arrived[slot(n)], 16 * nth(n, i))
                if n >= RING:
                    act.wait_ge(used[slot(n)], nth(n, i) - 1)
                nc.scalar.activation(w_hi[:, slot(n), :], raw[:, slot(n), :], ACT.Copy)\
                    .then_inc(hi_ready[slot(n)], 1)

            def hi_until(n):
                while state["next"] <= min(n, end - 1):
                    hi(state["next"])
                    state["next"] += 1

            def preload(func):
                chain(nc.scalar.activation(table[:, 0:4], table[:, 4:8], func))

            def norm(version, gains, then=ACT.Sigmoid):
                for a in range(4):
                    if version:
                        act.wait_ge(x_ready, 4 * (version - 1) + a + 1)
                    else:
                        act.wait_ge(x_loaded[a], 16)
                    high_halves(gains, a)
                    if gains == "both":
                        for k in (2 * a, 2 * a + 1):
                            nc.scalar.activation(gained_squares[:, a, (k % 2) * SEQ:(k % 2 + 1) * SEQ], x[:, k, :],
                                                 ACT.Square, scale=const("g_final", k))
                    nc.scalar.activation(squares[:, a, :], pair_of_x(a), ACT.Square).then_inc(sq_ready, 1)
                    if version == 0:
                        hi_until(a + 1)
                preload(ACT.Sqrt)
                state["norms"] += 1
                act.wait_ge(total_ready, state["norms"])
                nc.scalar.activation(rms[:, :], ps[:, 3, 0:SEQ], ACT.Sqrt, scale=1.0 / D, bias=const("norm_eps"))\
                    .then_inc(rms_ready, 1)
                if gains == "both":
                    act.wait_ge(scaled_ready, 1)
                    nc.scalar.activation(rms[:, :], scaled, ACT.Sqrt, scale=1.0 / D, bias=const("norm_eps"))\
                        .then_inc(rms_ready, 1)
                if then:
                    preload(then)

            def high_halves(gains, a, dst=xn_hi):
                for k in (2 * a, 2 * a + 1):
                    nc.scalar.activation(dst[:, k, :], x[:, k, :], ACT.Copy, scale=gain(gains, k))\
                        .then_inc(xn_hi_ready, 1)

            def ffn(f, n0):
                def sigmoid(c, i=0):
                    act.wait_ge(gate_ready, NFC * f + c + 4 * i + 1)
                    nc.scalar.activation(sig[:, c % 2, :], gate[:, c % 2, :], ACT.Sigmoid).then_inc(sig_ready, 1)

                def step(k, i=0):
                    for n in range(n0 + down_block(k) + 6, n0 + down_block(k) + 9):
                        if n < end:
                            hi(n, 2 * i)
                    sigmoid(k + LEAD, i)
                hi_until(n0 + 8)
                sigmoid(0)
                hi_until(n0 + 9)
                sigmoid(1)
                hi_until(n0 + 11)
                sigmoid(2)
                for k in FIRST_STEPS:
                    step(k)
                with act.Fori(0, LOOP_TRIPS) as i:
                    for k in LOOP_STEPS:
                        step(k, i)
                for k in LAST_STEPS:
                    step(k)
                state["next"] = n0 + down_block(FFN_STEPS - 1) + 9
                hi_until(n0 + down_block(NFC - 1) + 5)

            act.wait_ge(gains_loaded, 16)
            def mixer_one():
                n0 = FIRST["mix_in"]

                def in_place(taken, ap, func):
                    need(act, "proj_out", taken)
                    nc.scalar.activation(ap, ap, func).then_inc(ev["fn_done"], 1)

                def root(k, features):
                    need(act, "on_done", k)
                    cols = slice(0, 2 if features == HD else 1)
                    nc.scalar.activation(norm_sb[:, cols, :], bank(3)[:, cols, :], ACT.Sqrt, scale=1.0 / features,
                                         bias=const("norm_eps")).then_inc(ev["on_root"], 1)

                hi_until(n0 + 8)
                need(act, "gla_abs", 1)
                chain(nc.scalar.activation(tmp2[:, :, :], tmp2[:, :, :], ACT.Exp, scale=-1.0))
                nc.scalar.activation(tmp2[:, :, :], tmp2[:, :, :], ACT.Ln, bias=1.0).then_inc(ev["gla_ln"], 1)
                hi_until(n0 + 10)
                need(act, "gla_min", 1)
                nc.scalar.activation(decay_to[:, :, :], tmp[:, :, :], ACT.Exp, scale=1.0 / GLA_GATE_TAU)\
                    .then_inc(ev["gla_decay"], 1)
                need(act, "lb_zero", 1)
                nc.scalar.activation(lb[:, 2:4], lb[:, 0:2], ACT.Exp).then_inc(ev["lb_exp"], 1)
                hi_until(n0 + 14)
                in_place(9, gla_in["gate"][:, :, :], ACT.Silu)
                hi_until(n0 + 16)
                in_place(11, hgrn_in["k"][:, :, :], ACT.Sigmoid)
                hi_until(n0 + 18)
                in_place(13, hgrn_in["q"][:, :, :], ACT.Silu)
                hi_until(n0 + 22)
                in_place(17, hgrn_in["gate"][:, :, :], ACT.Sigmoid)
                hi_until(n0 + 23)
                root(1, HD)
                hi_until(FIRST["mix_out"] + 5)
                need(act, "rw_mixed", 1)
                nc.scalar.activation(lora[0:64, 0, :], rw[0:64, 6, :], ACT.Tanh)
                nc.scalar.activation(lora[:, 1, :], rw[:, 7, :], ACT.Sigmoid).then_inc(ev["rw_lora_in"], 1)
                root(2, G)
                need(act, "rw_kk_n", 1)
                nc.scalar.activation(sq[:, :, :], bank(4), ACT.Sqrt).then_inc(ev["rw_kk_root"], 1)
                need(act, "rw_lora", 1)
                for c in range(2):
                    ins = nc.scalar.activation(iclr[:, c, :], bank(1)[:, c, :], ACT.Sigmoid, bias=const("a0", c))
                ins.then_inc(ev["rw_iclr"], 1)
                for c in range(2):
                    ins = nc.scalar.activation(sz[:, c, :], bank(0)[:, c, :], ACT.Sigmoid, bias=const("w0", c))
                chain(ins)
                need(act, "rw_kk_sq", 1)
                nc.scalar.activation(dec[:, :, 1:], flat(sz).rearrange("p (a b) -> p a b", b=CHUNK), ACT.Exp,
                                     scale=-float(math.exp(-0.5))).then_inc(ev["rw_decay"], 1)
                nc.scalar.activation(g_r[:, :, :], bank(2), ACT.Copy).then_inc(ev["rw_g"], 1)
                need(act, "rw_tok", 2)
                need(act, "rw_dec", 3)
                nc.scalar.activation(b_tok[:, :, :], bank(5), ACT.Copy).then_inc(ev["rw_tok_act"], 1)
                need(act, "rw_tok", 3)
                nc.scalar.activation(k_tok[:, :, :], bank(6), ACT.Copy).then_inc(ev["rw_tok_act"], 1)
                need(act, "rw_var", 1)
                nc.scalar.activation(rms_r[:, :, :], bank(5), ACT.Sqrt, scale=1.0 / HD, bias=const("gn_eps")).then_inc(ev["rw_gn_root"], 1)
                hi_until(FIRST["mix_out"] + 8 + 4)


            def lru():
                n0 = FIRST["lru_in"]

                def round_xc(i):
                    need(act, "lru_xc", i + 1)
                    nc.scalar.activation(y_hi[:, i, :], xc[:, i, :], ACT.Copy).then_inc(ev["lru_xc_hi"], 1)

                def gates(i):
                    n = FIRST["lru_gates"] + i // 2
                    if i % 2:
                        act.wait_ge(used[slot(n)], nth(n))
                    else:
                        need(act, "lru_gates_done", i // 2 + 1)
                    nc.scalar.activation(lru_a[:, i, :], bank(4 + i % 4)[:, 0, :], ACT.Sigmoid, bias=const("b_r", i))
                    nc.scalar.activation(lru_i[:, i, :], bank(4 + i % 4)[:, 1, :], ACT.Sigmoid, bias=const("b_i", i))\
                        .then_inc(ev["lru_ri"], 1)

                for i in range(6):
                    hi_until(n0 + 6 + i)
                    round_xc(i)
                hi_until(n0 + 12)
                gates(0)
                gates(1)
                round_xc(6)
                hi_until(n0 + 14)
                round_xc(7)
                gates(2)
                gates(3)
                hi_until(n0 + 15)
                for i in range(4, KD):
                    gates(i)
                hi_until(n0 + 17)
                need(act, "lru_abs", 1)
                chain(nc.scalar.activation(sp[:, 1, :], sp[:, 0, :], ACT.Exp, scale=-1.0))
                nc.scalar.activation(sp[:, 1, :], sp[:, 1, :], ACT.Ln, bias=1.0).then_inc(ev["lru_ln"], 1)
                n0 = FIRST["lru_branch"]
                hi_until(n0 + 5)
                act.wait_ge(ev["lru_ri"], KD)
                need(act, "lru_sp", 1)
                for half in range(2):
                    for i in range(4 * half, 4 * half + 4):
                        ins = nc.scalar.activation(lru_t[:, i, :], lru_a[:, i, :], ACT.Tanh, scale=sp[:, 3, i:i + 1])
                    chain(ins)
                    for i in range(4 * half, 4 * half + 4):
                        ins = nc.scalar.activation(lru_a[:, i, :], lru_a[:, i, :], ACT.Exp, scale=sp[:, 2, i:i + 1])
                    ins.then_inc(ev["lru_a"], 1)
                    hi_until(n0 + 7 + half)
                for half in range(2):
                    fours = slice(4 * half, 4 * half + 4)
                    need(act, "lru_m", half + 1)
                    nc.scalar.activation(lru_t[:, fours, :], lru_t[:, fours, :], ACT.Sqrt).then_inc(ev["lru_root"], 1)
                    hi_until(n0 + 9 + half)
                for half in range(2):
                    need(act, "lru_z", half + 1)
                    fours = slice(4 * half, 4 * half + 4)
                    nc.scalar.activation(gelu_z[:, fours, :], gelu_z[:, fours, :], ACT.Sigmoid,
                                         scale=2 * math.sqrt(2 / math.pi)).then_inc(ev["lru_gelu"], 1)
                    hi_until(n0 + (11, 13)[half])
                hi_until(FIRST["lru_out"] + 8 + 4)

            def heads_square(k, a):
                need(act, "proj_out", TAKEN_BEFORE["kv" if k == 1 else "q_in"] + 2 * a + 2)
                nc.scalar.activation(sq_heads[a][:, :, :], raw_heads[:, 2 * a:2 * a + 2, :], ACT.Square)\
                    .then_inc(ev["heads_sq"], 1)

            def heads_root(k, a):
                need(act, "heads_n", 4 * (k - 1) + a + 1)
                nc.scalar.activation(sq_heads[a][:, :, :], bank(4 + a if k == 1 else 2 + a % 2), ACT.Sqrt, scale=1.0 / HD,
                                     bias=const("norm_eps")).then_inc(ev["heads_root"], 1)

            def shared_kv():
                n0 = FIRST["kv"]
                hi_until(n0 + 7)
                for a in range(4):
                    high_halves("g_ffn_e", a, y_hi)
                for a in range(4):
                    hi_until(n0 + 8 + 2 * a)
                    heads_square(1, a)
                for a in range(4):
                    hi_until(n0 + 15 + a)
                    heads_root(1, a)
                hi_until(n0 + 2 * KD + 4)
                act.wait_ge(used[slot(n0 + 2 * KD - 1)], nth(n0 + 2 * KD - 1))
                need(act, "col_out", 1)
                for t in range(TB):
                    ins = nc.scalar.activation(v_heads[:, t, :], ps[:, 2 * t:2 * t + 2, :].rearrange("p b s -> p (b s)"),
                                               ACT.Copy, scale=rstd_col[:, t:t + 1])
                ins.then_inc(ev["v_out"], 1)

            def attention():
                n0 = FIRST["q_in"]
                for a in range(3):
                    hi_until(n0 + 8 + 2 * a)
                    heads_square(2, a)
                    if a:
                        heads_root(2, a - 1)
                hi_until(n0 + 13)
                heads_square(2, 3)
                heads_root(2, 2)
                heads_root(2, 3)
                preload(ACT.Sigmoid)
                need(act, "at_sep", 1)
                for step in range(KD + 2):
                    if step < KD:
                        c = step
                        need(act, "at_mask", c + 1)
                        z = ps[:, 2 * (c % 2):2 * (c % 2) + 2, 0:3 * P].rearrange("p b (m s) -> p b m s", m=3)
                        if c >= 2:
                            need(act, "at_w", c - 1)
                        for out_ap, scale in ((stick[c % 2][:, :, :], QK_SCALE), (pass_on[c % 2][:, :, 0:P], -QK_SCALE)):
                            ins = nc.scalar.activation(out_ap.rearrange("p (b m) s -> p b m s", b=2), z, ACT.Sigmoid, scale=scale)
                        ins.then_inc(ev["at_sig"], 1)
                    if 0 <= step - 1 < KD:
                        c = step - 1
                        need(act, "at_wt", c + 1)
                        nc.scalar.activation(weights_t[c % 2][:, :, :].rearrange("p (b m) s -> p b (m s)", b=2),
                                             ps[:, 4:6, 0:3 * P], ACT.Copy).then_inc(ev["at_wt_out"], 1)
                    if 0 <= step - 2 < KD:
                        c = step - 2
                        need(act, "at_o", c + 1)
                        nc.scalar.activation(y_hi[:, c, :], bank(6 + c % 2)[:, 0, :], ACT.Copy).then_inc(ev["at_yhi"], 1)
                hi_until(FIRST["attn_out"] + 8 + 4)

            act.wait_ge(table_ready, 1)
            hi_until(0)
            steps = [
                lambda: norm(0, "g_ffn_a"),
                lambda: ffn(0, FIRST["ffn_a"]),
                lambda: (act.wait_ge(const_loaded, 16), norm(1, "g_mix"), mixer_one()),
                lambda: norm(2, "g_ffn_b"),
                lambda: ffn(1, FIRST["ffn_b"]),
                lambda: None,
                lambda: (norm(3, "both"), ffn(2, FIRST["ffn_c"])),
                lambda: (norm(5, "g_lru"), lru()),
                lambda: (norm(6, "g_ffn_d"), ffn(3, FIRST["ffn_d"])),
                lambda: (norm(7, "g_kv", None), shared_kv()),
                lambda: ffn(4, FIRST["ffn_e"]),
                lambda: (norm(8, "g_attn", None), attention()),
                lambda: (norm(9, "g_ffn_f"), ffn(5, FIRST["ffn_f"])),
            ]
            for step in steps:
                step()

        @block.vector
        def _(v):
            chain = Chain(v, dve_chain)
            x_tiles, xn_tiles, updates, norms, roots = [0], [0], [0], [0], [0]
            end_of_stream = [False]

            def lo(n, i=0):
                v.wait_ge(hi_ready[slot(n)], nth(n, i))
                nc.vector.tensor_tensor(w_lo[:, slot(n), :], raw[:, slot(n), :], w_hi[:, slot(n), :],
                                        ALU.subtract).then_inc(lo_ready[slot(n)], 1)

            def low_halves(gains, a, hi=xn_hi, lo=xn_lo):
                for k in (2 * a, 2 * a + 1):
                    xn_tiles[0] += 1
                    v.wait_ge(xn_hi_ready, xn_tiles[0])
                    nc.vector.scalar_tensor_tensor(lo[:, k, :], x[:, k, :], gain(gains, k), hi[:, k, :],
                                                   ALU.mult, ALU.subtract).then_inc(xn_lo_ready, 1)

            def add_squares(a, both):
                v.wait_ge(sq_ready, 4 * norms[0] + a + 1)
                sums = [(squares, squares_sum)] + ([(gained_squares, gained_sum)] if both else [])
                for of, total in sums:
                    if a == 1:
                        chain(nc.vector.tensor_tensor(total, of[:, 0, :], of[:, 1, :], ALU.add))
                    elif a > 1:
                        ins = nc.vector.tensor_tensor(total, total, of[:, a, :], ALU.add)
                        if a == 2:
                            chain(ins)
                if a == 3:
                    ins.then_inc(sum_ready, 1)

            def next_x(scale, gains=None, last_block=None):
                for a in range(5):
                    if scale is None and a < 4:
                        v.wait_ge(x_loaded[a], 16)
                        if a in DVE_SPLITS:
                            lo(a)
                    if a < 4 and scale is not None:
                        if a < 3:
                            v.wait_ge(acc_done, 3 * updates[0] + a + 1)
                        else:
                            v.wait_ge(used[slot(last_block)], nth(last_block))
                        nc.vector.scalar_tensor_tensor(pair_of_x(a), ps[:, a, :], scale, pair_of_x(a), ALU.mult, ALU.add)\
                            .then_inc(x_ready, 1)
                        x_tiles[0] += 1
                        v.wait_ge(x_ready, x_tiles[0])
                    if a:
                        if gains:
                            low_halves(gains, a - 1)
                        if not end_of_stream[0]:
                            add_squares(a - 1, gains == "both")
                if scale is not None:
                    updates[0] += 1
                if not end_of_stream[0]:
                    inverse_root(gains == "both")

            def inverse_root(both):
                norms[0] += 1

                def reciprocal(out_ap):
                    roots[0] += 1
                    v.wait_ge(rms_ready, roots[0])
                    return nc.vector.reciprocal(out_ap, rms[:, :])
                if both:
                    reciprocal(first_rstd).then_inc(first_rstd_ready, 1)
                    v.wait_ge(first_rstd_ready, 1)
                    chain(nc.vector.tensor_tensor(scaled, ps[:, 3, SEQ:], first_rstd, ALU.mult))
                    nc.vector.tensor_tensor(scaled, scaled, first_rstd, ALU.mult).then_inc(scaled_ready, 1)
                    chain(reciprocal(rstd[:, :]))
                    ins = nc.vector.tensor_tensor(rstd[:, :], rstd[:, :], first_rstd, ALU.mult)
                else:
                    ins = reciprocal(rstd[:, :])
                ins.then_inc(rstd_ready, 1)
                v.wait_ge(rstd_ready, norms[0])

            def ffn(f, n0, meanwhile=None):
                def hidden(c, i=0):
                    tile_up = n0 + gate_block(c) + 1
                    v.wait_ge(used[slot(tile_up)], nth(tile_up, 2 * i))
                    nc.vector.tensor_tensor(gate[:, c % 2, :], ps[:, 4 + c % 4, 0:SEQ], rstd[:, :], ALU.mult)\
                        .then_inc(gate_ready, 1)
                    chain(nc.vector.tensor_tensor(up[:, :], ps[:, 4 + c % 4, SEQ:], rstd[:, :], ALU.mult))
                    v.wait_ge(sig_ready, NFC * f + c + 4 * i + 1)
                    chain(nc.vector.tensor_tensor(gs[:, :], gate[:, c % 2, :], sig[:, c % 2, :], ALU.mult))
                    if c >= 2:
                        down = n0 + down_block(c - 2)
                        v.wait_ge(used[slot(down)], nth(down, 2 * i))
                    nc.vector.tensor_tensor(h_hi[:, c % 2, :], up[:, :], gs[:, :], ALU.mult)
                    chain(nc.vector.tensor_tensor(h[:, :], up[:, :], gs[:, :], ALU.mult))
                    nc.vector.tensor_tensor(h_lo[:, c % 2, :], h[:, :], h_hi[:, c % 2, :], ALU.subtract)\
                        .then_inc(h_ready, 1)
                    v.wait_ge(h_ready, NFC * f + c + 4 * i + 1)

                def step(k, i=0):
                    lo(n0 + down_block(k + 2), 2 * i)
                    if k == FFN_STEPS - 1:
                        lo(n0 + down_block(NFC - 1))
                    hidden(k + LEAD, i)
                lo(n0 + down_block(0))
                hidden(0)
                lo(n0 + down_block(1))
                hidden(1)
                hidden(2)
                if meanwhile:
                    meanwhile()
                for k in FIRST_STEPS:
                    step(k)
                count = chain.count
                with v.Fori(0, LOOP_TRIPS) as i:
                    chain.later = i * (3 * len(LOOP_STEPS))
                    for k in LOOP_STEPS:
                        step(k, i)
                assert chain.count == count + 3 * len(LOOP_STEPS)
                chain.count, chain.later = count + 3 * len(LOOP_STEPS) * LOOP_TRIPS, 0
                for k in LAST_STEPS:
                    step(k)

            def gain_x():
                for a in range(4):
                    for k in (2 * a, 2 * a + 1):
                        ins = nc.vector.scalar_tensor_tensor(x[:, k, :], x[:, k, :], const("g_final", k), first_rstd,
                                                             ALU.mult, ALU.mult)
                    ins.then_inc(x_ready, 1)
                    x_tiles[0] += 1
                    v.wait_ge(x_ready, x_tiles[0])

            def signal(ins, name):
                ins.then_inc(ev[name], 1)
                sent[name] = sent.get(name, 0) + 1
                v.wait_ge(ev[name], sent[name])

            sent = {}
            tt = nc.vector.tensor_tensor
            stt = nc.vector.scalar_tensor_tensor
            tsc = nc.vector.tensor_scalar

            def take(n, b, dst, scale=None):
                v.wait_ge(used[slot(n)], nth(n))
                src = ps[0:dst.shape[0], b, 0:SEQ]
                by = rstd[0:dst.shape[0], :]
                if scale is None:
                    ins = tt(dst, src, by, ALU.mult)
                else:
                    ins = stt(dst, src, scale, by, ALU.mult, ALU.mult)
                signal(ins, "proj_out")

            def split_y(tile, make, scratch):
                make(y_hi[:, tile, :])
                chain(make(scratch))
                signal(tt(y_lo[:, tile, :], scratch, y_hi[:, tile, :], ALU.subtract), "y_ready")

            def value_rows(k):
                need(v, "vt_done", k)
                signal(nc.vector.tensor_copy(v_rows[:, :, :], bank(2)), "vt_out")

            def decayed_attention(src, k, first_tile, meanwhile=()):
                chain(nc.vector.memset(decay_from[:, :, :], 1.0))
                chain(nc.vector.memset(scores[:, :, :], 0.0))
                for lev in range(8):
                    n = 1 << lev
                    b = lev % 2
                    if lev and lev <= len(meanwhile):
                        meanwhile[lev - 1]()
                    chain(tt(q_dec[b][:, :, :], src["q"][:, :, :], decay_to[:, :, :], ALU.mult))
                    signal(tt(k_dec[b][:, :, :], src["k"][:, :, :], decay_from[:, :, :], ALU.mult), "gla_qk")
                    if n < P:
                        to, frm = (flat(a).rearrange("p (m e s) -> p m e s", e=2, s=n) for a in (decay_to, decay_from))
                        m = 2 * SEQ // (2 * n)
                        chain(tt(frm[:, :, 0, :], frm[:, :, 0, :], to[:, :, 1, n - 1:n].broadcast_to([P, m, n]), ALU.mult))
                        chain(tt(to[:, :, 1, :], to[:, :, 1, :], to[:, :, 0, n - 1:n].broadcast_to([P, m, n]), ALU.mult))
                    take_level(lev, k)
                    mix_tile(first_tile + lev)
                take_level(8, k)
                mix_tile(first_tile + 8)

            def take_level(lev, k):
                need(v, "sc_done", 9 * (k - 1) + lev + 1)
                b = 2 * (lev % 2)
                if lev < 8:
                    mask = over(const("level", lev, P), 8).bitcast(U32)
                    signal(nc.vector.copy_predicated(scores[:, :, :], mask, pair(b)), "sc_out")
                else:
                    signal(nc.vector.tensor_copy(scores_far[:, :, :].rearrange("p (j c) t -> p j (c t)", j=2),
                                                 ps[:, b:b + 2, 0:2 * P]), "sc_out")

            def attended(k):
                need(v, "o_done", k)
                chain(nc.vector.tensor_copy(o_sb[:, :, :], bank(2)))
                signal(tt((tmp, tmp2)[k - 1][:, :, :], o_sb[:, :, :], o_sb[:, :, :], ALU.mult), "o_sq")

            def inverse_norm(k, c):
                need(v, "on_root", k)
                chain(nc.vector.reciprocal(norm_sb[:, c, :], norm_sb[:, c, :]))

            def normalise(per_head):
                by = norm_sb[:, :, :] if per_head else norm_sb[:, 0:1, :].broadcast_to([P, 2, SEQ])
                chain(tt(o_sb[:, :, :], o_sb[:, :, :], by, ALU.mult))

            def pooled(c):
                split_y(c, lambda out: tsc(out, bank(7)[:, c, :], const("pool_b", c), const("pool_scale", c),
                                           ALU.add, ALU.mult), out_scratch[:, c, :])

            def mix_tile(i):
                n0 = FIRST["mix_in"]
                places = [ga_sb[0:32, :]] + [buf[:, c, :] for buf in (
                    gla_in["q"], gla_in["k"], gla_in["v"], gla_in["gate"], hgrn_in["k"], hgrn_in["q"], hgrn_in["v"],
                    hgrn_in["gate"], pool_in[:, :, PAD:]) for c in range(2)] + [rw_raw[:, c, 1:] for c in range(8)]
                if i < len(places):
                    take(n0 + i, tile_bank(i, MIX_SPARE), places[i], QK_SCALE if i in (1, 2) else None)

            def mixer_one():
                v.wait_ge(const_loaded, 16)
                chain(nc.vector.memset(rw_raw[:, :, 0:1], 0.0))
                for buf in (pool_in, win_a, win_b):
                    chain(nc.vector.memset(buf[:, :, 0:PAD], 0.0))
                logits = const("lb_logits")
                signal(tt(lb[:, 0:2], logits, logits, ALU.subtract), "lb_zero")
                for i in range(4):
                    mix_tile(i)
                need(v, "gla_z", 1)
                for c in range(2):
                    chain(tsc(tmp[:, c, :], bank(3)[:, c, :], const("gla_b", c), None, ALU.add))
                signal(stt(tmp2[:, :, :], tmp[:, :, :], -1.0, tmp[:, :, :], ALU.mult, ALU.max), "gla_abs")
                mix_tile(4)
                need(v, "gla_ln", 1)
                signal(stt(tmp[:, :, :], tmp[:, :, :], 0.0, tmp2[:, :, :], ALU.min, ALU.subtract), "gla_min")
                mix_tile(5)
                mix_tile(6)
                need(v, "lb_exp", 1)
                chain(nc.vector.reciprocal(lb[:, 4:6], lb[:, 2:4]))
                chain(tt(lb[:, 4:6], lb[:, 4:6], lb[:, 2:4], ALU.mult))
                chain(tt(lb[:, 6:8], lb[:, 4:6], lb[:, 4:6], ALU.subtract))
                chain(tsc(lb[:, 0:2], lb[:, 6:8], -1.0, 1.0, ALU.mult, ALU.add))
                value_rows(1)
                mix_tile(7)
                need(v, "gla_decay", 1)
                decayed_attention(gla_in, 1, 8)
                attended(1)
                mix_tile(17)
                need(v, "on_done", 1)
                need(v, "fn_done", 3)
                for c in range(2):
                    chain(tsc(tmp[:, c, :], hgrn_in["k"][:, c, :], lb[:, c:c + 1], lb[:, 6 + c:7 + c], ALU.mult, ALU.add))
                chain(tsc(hgrn_in["k"][:, :, :], tmp[:, :, :], -1.0, 1.0, ALU.mult, ALU.add))
                chain(tsc(decay_to[:, :, :], tmp[:, :, :], GATE_FLOOR, None, ALU.max))
                mix_tile(18)
                value_rows(2)
                signal(tsc(hgrn_in["q"][:, :, :], hgrn_in["q"][:, :, :], QK_SCALE, None, ALU.mult), "hg_ready")
                mix_tile(19)

                def gla_out(c):
                    if c == 0:
                        normalise(True)
                    split_y(6 + c, lambda out: stt(out, o_sb[:, c, :], const("gla_norm", c), gla_in["gate"][:, c, :],
                                                   ALU.mult, ALU.mult), tmp[:, c, :])
                decayed_attention(hgrn_in, 2, 20, [lambda: inverse_norm(1, 0), lambda: inverse_norm(1, 1),
                                                   lambda: gla_out(0), lambda: gla_out(1)])
                attended(2)
                shifted()

                def hgrn_out(c):
                    split_y(2 + c, lambda out: stt(out, o_sb[:, c, :], const("hgrn_norm", c), hgrn_in["gate"][:, c, :],
                                                   ALU.mult, ALU.mult), out_scratch[:, c, :])
                rwkv([lambda: hgrn_out(0), lambda: hgrn_out(1), lambda: pooled(0), lambda: pooled(1)])

            def shifted():
                chain(tt(rw[:, :, :], rw_raw[:, :, 0:SEQ], rw_raw[:, :, 1:], ALU.subtract))
                for i in (6, 7, 0, 1, 4, 5, 2, 3):
                    ins = stt(rw[:, i, :], rw[:, i, :], const("mu", i), rw_raw[:, i, 1:], ALU.mult, ALU.add)
                    if i == 7:
                        signal(ins, "rw_mixed")
                chain(ins)
                for c in range(2):
                    chain(tsc(kk[:, c, :], rw[:, 2 + c, :], const("k_k", c), None, ALU.mult))
                signal(tt(sq[:, :, :], kk[:, :, :], kk[:, :, :], ALU.mult), "rw_kk_sq")
                chain(nc.vector.memset(dec[:, :, 0:1], 0.0))

            def rwkv(others):
                r_in, k_in, v_in = rw[:, 0:2, :], rw[:, 2:4, :], rw[:, 4:6, :]
                need(v, "rw_kk_root", 1)
                chain(tsc(sq[:, :, :], sq[:, :, :], 1e-12, None, ALU.max))
                chain(nc.vector.reciprocal(sq[:, :, :], sq[:, :, :]))
                chain(tt(kk[:, :, :], kk[:, :, :], sq[:, :, :], ALU.mult))
                inverse_norm(2, 0)

                def by_chunk(ap):
                    return ap.rearrange("p c (q s) -> p (c q) s", s=CHUNK)
                after, before = cum[:, :, 1:], cum[:, :, 0:CHUNK]
                last = cum[:, :, CHUNK:].broadcast_to([P, 8, CHUNK])
                need(v, "rw_iclr", 1)
                chain(tt(b_dec[:, :, :], kk[:, :, :], iclr[:, :, :], ALU.mult))
                need(v, "rw_decay", 1)
                chain(nc.vector.tensor_tensor_scan(flat(cum), flat(dec), const("scan_one"), 0.0, ALU.mult, ALU.add))
                signal(tt(by_chunk(a_dec), by_chunk(kk), before, ALU.mult), "rw_dec")
                chain(nc.vector.reciprocal(by_chunk(inv_cum), after))
                chain(tt(b_dec[:, :, :], b_dec[:, :, :], inv_cum[:, :, :], ALU.mult))
                signal(tt(by_chunk(b_last), by_chunk(b_dec), last, ALU.mult), "rw_dec")
                for c in range(2):
                    chain(tsc(k_new[:, c, :], iclr[:, c, :], -1.0, const("k_a", c), ALU.add, ALU.mult))
                chain(stt(k_new[:, :, :], k_new[:, :, :], 1.0, k_in, ALU.add, ALU.mult))
                chain(tt(kk_dec[:, :, :], k_new[:, :, :], inv_cum[:, :, :], ALU.mult))
                signal(tt(by_chunk(k_last), by_chunk(kk_dec), last, ALU.mult), "rw_dec")
                chain(tt(by_chunk(r_dec), by_chunk(r_in), after, ALU.mult))
                chain(nc.vector.tensor_copy(last_dec[:, :], cum[:, :, CHUNK:].rearrange("p a b -> p (a b)")))
                for c in range(2):
                    ins = stt(sq[:, c, :], r_in[:, c, :], const("r_k", c), k_new[:, c, :], ALU.mult, ALU.mult)
                signal(ins, "rw_bonus_in")
                need(v, "rw_tok", 1)
                chain(nc.vector.tensor_copy(a_tok[:, :, :], bank(4)))
                normalise(False)
                need(v, "rw_tok", 4)
                signal(nc.vector.tensor_copy(v_tok[:, :, :], bank(7)), "rw_tok_out")
                need(v, "rw_bonus", 1)
                chain(tt(bonus[:, :, :], bank(3), v_in, ALU.mult))
                need(v, "rw_mat", 1)
                signal(tt(l_t[:, :, :], pair(0), over(const("strict_up"), 8), ALU.mult), "rw_mat_out")
                need(v, "rw_mat", 2)
                signal(stt(inv[:, :, :], pair(4), -1.0, over(const("level_low", 0, P), 8), ALU.mult, ALU.mult), "rw_mat_out")
                chain(tt(inv[:, :, :], inv[:, :, :], over(const("ident"), 8), ALU.add))
                chain(stt(inv_t[:, :, :], l_t[:, :, :], -1.0, over(const("level", 1, P), 8), ALU.mult, ALU.mult))
                signal(tt(inv_t[:, :, :], inv_t[:, :, :], over(const("ident"), 8), ALU.add), "rw_z_out")
                need(v, "rw_mat", 3)
                signal(tt(lak_t[:, :, :], pair(0), over(const("strict_up"), 8), ALU.mult), "rw_mat_out")
                need(v, "rw_mat", 4)
                signal(tt(mrb_t[:, :, :], pair(2), over(const("incl_up"), 8), ALU.mult), "rw_mat_out")
                need(v, "rw_mat", 5)
                signal(tt(mrk_t[:, :, :], pair(0), over(const("incl_up"), 8), ALU.mult), "rw_mat_out")
                need(v, "rw_lv", 1)
                need(v, "pool_done", 1)
                for lev in range(1, 6):
                    for j in range(2):
                        half = slice(4 * j, 4 * j + 4)
                        need(v, "rw_y", 2 * (lev - 1) + j + 1)
                        signal(tt(y_m[:, half, :], bank(j, 4), over(const("level_low", lev, P), 4), ALU.mult), "rw_ym")
                    for j in range(2):
                        half = slice(4 * j, 4 * j + 4)
                        need(v, "rw_z", 2 * (lev - 1) + j + 1)
                        if lev < 5:
                            chain(tt(inv[:, half, :], inv[:, half, :], bank(2 + j, 4), ALU.subtract))
                        signal(tt(inv_t[:, half, :], inv_t[:, half, :], bank(4 + j, 4), ALU.subtract), "rw_z_out")
                    if lev < 5:
                        others[lev - 1]()
                signal(nc.vector.tensor_copy(lv[:, :, :], bank(6)), "rw_lv_out")
                need(v, "rw_wt", 1)
                chain(nc.vector.tensor_copy(w_t[:, :, :], bank(0)))
                need(v, "rw_ut", 1)
                signal(nc.vector.tensor_copy(u_tilde[:, :, :], bank(1)), "rw_wu_out")
                for q in range(NCH):
                    rows, t = slice(CHUNK * (q % 2), CHUNK * (q % 2) + CHUNK), q // 2
                    if q == 0:
                        signal(tsc(u[rows, t, :], u_tilde[rows, t, :], -1.0, None, ALU.mult), "rw_u_out")
                    else:
                        need(v, "rw_u", q)
                        signal(stt(u[rows, t, :], ps[rows, 2 + q % 2, 0:G], -1.0, u_tilde[rows, t, :],
                                   ALU.mult, ALU.subtract), "rw_u_out")
                    if q + 1 < NCH:
                        if q:
                            for c in range(2):
                                chain(tsc(state_dec[:, c, :], state[q][:, c, :], last_dec[:, 4 * c + q:4 * c + q + 1],
                                          None, ALU.mult))
                        need(v, "rw_st", q + 1)
                        new = ps[:, 4 + q % 2, 0:2 * P].rearrange("p (c s) -> p c s", c=2)
                        ins = tt(state[q + 1][:, :, :], new, over(const("head_ones"), 2), ALU.mult)
                        if q:
                            chain(ins)
                            ins = tt(state[q + 1][:, :, :], state[q + 1][:, :, :], state_dec[:, :, :], ALU.add)
                        signal(ins, "rw_st_out")
                need(v, "rw_o", 1)
                signal(nc.vector.tensor_copy(o_r[:, :, :], bank(6)), "rw_o_out")
                need(v, "rw_mean", 1)
                chain(stt(dev[:, :, :], bank(4), -1.0 / HD, o_r[:, :, :], ALU.mult, ALU.add))
                signal(tt(t_r[:, :, :], dev[:, :, :], dev[:, :, :], ALU.mult), "rw_dev")
                need(v, "rw_gn_root", 1)
                chain(nc.vector.reciprocal(rms_r[:, :, :], rms_r[:, :, :]))
                chain(tt(dev[:, :, :], dev[:, :, :], rms_r[:, :, :], ALU.mult))
                for c in range(2):
                    chain(tsc(dev[:, c, :], dev[:, c, :], const("ln_w", c), const("ln_b", c), ALU.mult, ALU.add))
                chain(tt(dev[:, :, :], dev[:, :, :], bonus[:, :, :], ALU.add))
                need(v, "rw_g", 1)
                for c in range(2):
                    split_y(4 + c, lambda out: tt(out, dev[:, c, :], g_r[:, c, :], ALU.mult), t_r[:, c, :])

            def lru():
                n0 = FIRST["lru_in"]
                chain(nc.vector.memset(rec[:, :, 0:TAPS - 1], 0.0))
                signal(stt(sp[:, 0, :], const("lam"), -1.0, const("lam"), ALU.mult, ALU.max), "lru_abs")

                def low_half(i):
                    need(v, "lru_xc_hi", i + 1)
                    signal(tt(y_lo[:, i, :], xc[:, i, :], y_hi[:, i, :], ALU.subtract), "lru_conv")
                for i in range(KD):
                    take(n0 + i, tile_bank(i, LRU_SPARE), rec[:, i, TAPS - 1:])
                    chain(tsc(xc[:, i, :], rec[:, i, 0:SEQ], const("conv_w", i), const("conv_b", i), ALU.mult, ALU.add))
                    for k in range(1, TAPS):
                        ins = stt(xc[:, i, :], rec[:, i, k:k + SEQ], const("conv_w", k * KD + i), xc[:, i, :],
                                  ALU.mult, ALU.add)
                        if k < TAPS - 1:
                            chain(ins)
                        else:
                            signal(ins, "lru_xc")
                    if i:
                        low_half(i - 1)
                low_half(KD - 1)
                n0 = FIRST["lru_branch"]
                halves = [slice(0, 4), slice(4, 8)]

                def branch(first):
                    for i in (first, first + 1):
                        take(n0 + i, i % 4, lru_gate[:, i, :])

                def decayed(half):
                    fours = halves[half]
                    need(v, "lru_a", half + 1)
                    chain(tt(gelu_z[:, fours, :], lru_a[:, fours, :], lru_a[:, fours, :], ALU.mult))
                    signal(stt(lru_t[:, fours, :], gelu_z[:, fours, :], 1.0, lru_t[:, fours, :], ALU.add, ALU.mult), "lru_m")

                def cubic(half):
                    g, z = lru_gate[:, halves[half], :], gelu_z[:, halves[half], :]
                    chain(tt(z, g, g, ALU.mult))
                    chain(tsc(z, z, 0.044715, 1.0, ALU.mult, ALU.add))
                    signal(tt(z, z, g, ALU.mult), "lru_z")

                for half in range(2):
                    need(v, "lru_ri", 4 * half + 4)
                    chain(tt(lru_h[:, halves[half], :], lru_i[:, halves[half], :], xc[:, halves[half], :], ALU.mult))
                need(v, "lru_ln", 1)
                chain(tsc(sp[:, 0, :], const("lam"), -1.0, 0.0, ALU.mult, ALU.max))
                chain(tt(sp[:, 0, :], sp[:, 0, :], sp[:, 1, :], ALU.add))
                chain(tsc(sp[:, 2, :], sp[:, 0, :], -LRU_C, None, ALU.mult))
                signal(tsc(sp[:, 3, :], sp[:, 0, :], LRU_C, None, ALU.mult), "lru_sp")
                branch(0)
                decayed(0)
                branch(2)
                decayed(1)
                cubic(0)
                branch(4)

                def scan_inputs(half):
                    fours = halves[half]
                    need(v, "lru_root", half + 1)
                    chain(tt(lru_h[:, fours, :], lru_h[:, fours, :], lru_t[:, fours, :], ALU.mult))
                    need(v, "lru_gelu", half + 1)
                    chain(tt(lru_gate[:, fours, :], lru_gate[:, fours, :], gelu_z[:, fours, :], ALU.mult))

                def scan(i):
                    chain(nc.vector.tensor_tensor_scan(lru_i[:, i, :], lru_a[:, i, :], lru_h[:, i, :], 0.0,
                                                       ALU.mult, ALU.add))
                    split_y(i, lambda out: tt(out, lru_i[:, i, :], lru_gate[:, i, :], ALU.mult), gelu_z[:, i, :])

                scan_inputs(0)
                branch(6)
                for i in range(3):
                    scan(i)
                cubic(1)
                scan(3)
                scan_inputs(1)
                for i in range(4, 8):
                    scan(i)

            def heads_take(n0, a):
                for i in (2 * a, 2 * a + 1):
                    take(n0 + i, tile_bank(i, HEADS_SPARE), raw_heads[:, i, :])

            def heads_finish(k, a, dst, by):
                need(v, "heads_root", 4 * (k - 1) + a + 1)
                both = slice(2 * a, 2 * a + 2)
                chain(nc.vector.reciprocal(sq_heads[a][:, :, :], sq_heads[a][:, :, :]))
                signal(stt(dst[:, both, :], raw_heads[:, both, :], const(by), sq_heads[a][:, :, :], ALU.mult, ALU.mult),
                       "heads_ready")

            def shared_kv():
                n0 = FIRST["kv"]
                heads_take(n0, 0)
                heads_take(n0, 1)
                for a in range(4):
                    low_halves("g_ffn_e", a, y_hi, y_lo)
                need(v, "col_done", 1)
                signal(nc.vector.tensor_copy(rstd_col[:, :], ps[:, 3, 0:TB]), "col_out")
                heads_take(n0, 2)
                heads_take(n0, 3)
                for a in range(4):
                    heads_finish(1, a, k_t, "k_norm")

            def attention():
                n0 = FIRST["q_in"]
                for buf in pass_on:
                    chain(nc.vector.memset(buf[:, :, P:], 0.0))
                    for j in range(2):
                        chain(nc.vector.memset(buf[:, 3 * j, P:], 1.0))
                chain(nc.vector.memset(row_end[:, :, :], 0.0))
                for j in range(2):
                    ins = nc.vector.memset(row_end[:, 3 * j + 1:3 * j + 3, P:], 1.0)
                signal(ins, "at_sep")
                heads_take(n0, 0)
                heads_take(n0, 1)
                heads_take(n0, 2)
                heads_finish(2, 0, q_t, "q_norm")
                heads_take(n0, 3)
                heads_finish(2, 1, q_t, "q_norm")

                def masked(c):
                    need(v, "at_z", c + 1)
                    z = ps[:, 2 * (c % 2):2 * (c % 2) + 2, P:3 * P].rearrange("p b (m s) -> p b m s", m=2)
                    mask = const("not_before").unsqueeze(1).unsqueeze(1).broadcast_to([P, 2, 2, P])
                    signal(tt(z, z, mask, ALU.add), "at_mask")

                masked(0)
                masked(1)
                for step in range(1, KD + 3):
                    if 0 <= step - 1 < KD:
                        c = step - 1
                        need(v, "at_sig", c + 1)
                        chain(nc.vector.tensor_tensor_scan(flat(left)[:, ::-1], flat(pass_on[c % 2])[:, ::-1],
                                                           flat(row_end)[:, ::-1], 1.0, ALU.mult, ALU.add))
                        if c >= 2:
                            need(v, "at_wt", c - 1)
                        signal(tt(weights[c % 2][:, :, :], stick[c % 2][:, :, :], left[:, :, 1:], ALU.mult), "at_w")
                        if c in (0, 2):
                            heads_finish(2, 2 + c // 2, q_t, "q_norm")
                    if 2 <= step < KD:
                        masked(step)
                    if 0 <= step - 3 < KD:
                        c = step - 3
                        need(v, "at_yhi", c + 1)
                        signal(tt(y_lo[:, c, :], bank(6 + c % 2)[:, 0, :], y_hi[:, c, :], ALU.subtract), "y_ready")

            nc.vector.memset(table[:, :], 1.0).then_inc(table_ready, 1)
            v.wait_ge(gains_loaded, 16)
            nc.vector.tensor_tensor(gain_both[:, :], const("g_final"), const("g_ffn_c"), ALU.mult)

            def end_sublayer(scale, phase, gains, last=False):
                end_of_stream[0] = last
                next_x(scale, None if last else gains, LAST[phase] - 1)
            E_ = VERSIONS - 1
            steps = [
                lambda: next_x(None, "g_ffn_a"),
                lambda: (ffn(0, FIRST["ffn_a"]), end_sublayer(0.5, "ffn_a", "g_mix", E_ == 0)),
                lambda: (mixer_one(), end_sublayer(1.0, "mix_out", "g_ffn_b", E_ == 1)),
                lambda: None,
                lambda: (ffn(1, FIRST["ffn_b"]), end_sublayer(0.5, "ffn_b", "both", E_ == 2)),
                lambda: None,
                lambda: (ffn(2, FIRST["ffn_c"], gain_x), end_sublayer(0.5, "ffn_c", "g_lru", E_ == 4)),
                lambda: (lru(), end_sublayer(1.0, "lru_out", "g_ffn_d", E_ == 5)),
                lambda: (ffn(3, FIRST["ffn_d"]), end_sublayer(0.5, "ffn_d", "g_kv", E_ == 6)),
                lambda: shared_kv(),
                lambda: (ffn(4, FIRST["ffn_e"]),
                         end_sublayer(0.5, "ffn_e", "g_attn", E_ == 7)),
                lambda: (attention(), end_sublayer(1.0, "attn_out", "g_ffn_f", E_ == 8)),
                lambda: (ffn(5, FIRST["ffn_f"]), end_sublayer(0.5, "ffn_f", None, True)),
            ]
            for step in steps:
                step()

        @block.tensor
        def _(pe):
            pe.wait_ge(gains_loaded, 16)

            def feature_tiles(tiles, i=0, after_norm=None, between=None, halves=(xn_hi, xn_lo)):
                x_hi, x_lo = halves
                for k in range(KD):
                    if after_norm is not None:
                        pe.wait_ge(xn_lo_ready, KD * after_norm + k + 1)
                    for n, where, opens, closes in tiles:
                        if k == 0:
                            pe.wait_ge(lo_ready[slot(n)], nth(n, i))
                        wh, wl = (w[:, slot(n), k * P:k * P + P] for w in (w_hi, w_lo))
                        nc.tensor.matmul(where, wh, x_hi[:, k, :], start=k == 0 and opens, stop=False)
                        nc.tensor.matmul(where, wh, x_lo[:, k, :], start=False, stop=False)
                        ins = nc.tensor.matmul(where, wl, x_hi[:, k, :], start=False, stop=k == KD - 1 and closes)
                        if k == KD - 1:
                            ins.then_inc(used[slot(n)], 1)
                    if between and k == between[0]:
                        between[1]()

            def feature_tile(n, where, i=0, **k):
                feature_tiles([(n, where, True, True)], i, **k)

            norms = [0]

            def total_squares(both=False):
                norms[0] += 1
                pe.wait_ge(sum_ready, norms[0])
                parts = [(squares_sum, 0)] + ([(gained_sum, SEQ)] if both else [])
                for of, at in parts:
                    for half in range(2):
                        ins = nc.tensor.matmul(ps[:, 3, at:at + SEQ], const("all_ones"), of[:, half * SEQ:half * SEQ + SEQ],
                                               start=half == 0 and at == 0, stop=half == 1 and of is parts[-1][0])
                ins.then_inc(total_ready, 1)

            def add_block(n, rhs_hi, rhs_lo, i=0, start=False, stop=False):
                pe.wait_ge(lo_ready[slot(n)], nth(n, i))
                for d in range(KD):
                    where = ps[:, d // 2, (d % 2) * SEQ:(d % 2 + 1) * SEQ]
                    wh, wl = (w[:, slot(n), d * P:d * P + P] for w in (w_hi, w_lo))
                    nc.tensor.matmul(where, wh, rhs_hi, start=start and d % 2 == 0, stop=False)
                    nc.tensor.matmul(where, wh, rhs_lo, start=False, stop=False)
                    ins = nc.tensor.matmul(where, wl, rhs_hi, start=False, stop=stop and d % 2 == 1)
                    if stop and d % 2 == 1 and d < KD - 1:
                        ins.then_inc(acc_done, 1)
                ins.then_inc(used[slot(n)], 1)

            def rows_tile(n, lhs_hi, lhs_lo, i=0, start=False, stop=False, bank=0):
                pe.wait_ge(lo_ready[slot(n)], nth(n, i))
                for t in range(TB):
                    lh, ll = (a[:, t * P:t * P + P] for a in (lhs_hi, lhs_lo))
                    for c in range(2):
                        acc = ps[:, bank + 2 * t + c, :]
                        wh, wl = (w[:, slot(n), 512 * c:512 * c + 512] for w in (w_hi, w_lo))
                        nc.tensor.matmul(acc, lh, wh, start=start, stop=False)
                        nc.tensor.matmul(acc, lh, wl, start=False, stop=False)
                        ins = nc.tensor.matmul(acc, ll, wh, start=False, stop=stop)
                ins.then_inc(used[slot(n)], 1)

            def ffn(f, g, n0, total=total_squares, **source):
                def gate_up(c, i=0):
                    feature_tile(n0 + gate_block(c), ps[:, 4 + c % 4, 0:SEQ], 2 * i, **source)
                    feature_tile(n0 + gate_block(c) + 1, ps[:, 4 + c % 4, SEQ:], 2 * i, **source)

                def down(c, i=0, **k):
                    pe.wait_ge(h_ready, NFC * f + c + 4 * i + 1)
                    add_block(n0 + down_block(c), h_hi[:, c % 2, :], h_lo[:, c % 2, :], 2 * i, **k)

                def step(k, i=0):
                    down(k, i, start=k == 0)
                    gate_up(k + LEAD, i)
                if f == 0:
                    feature_tile(n0, ps[:, 4, 0:SEQ], after_norm=g)
                    feature_tile(n0 + 1, ps[:, 4, SEQ:])
                    total()
                    feature_tile(n0 + 2, ps[:, 5, 0:SEQ])
                else:
                    feature_tiles([(n0, ps[:, 4, 0:SEQ], True, False), (n0 + 1, ps[:, 4, SEQ:], False, True),
                                   (n0 + 2, ps[:, 5, 0:SEQ], True, True)], after_norm=g,
                                  between=(6, total), **source)
                feature_tile(n0 + 3, ps[:, 5, SEQ:], **source)
                gate_up(2)
                for k in FIRST_STEPS:
                    step(k)
                with pe.Fori(0, LOOP_TRIPS) as i:
                    for k in LOOP_STEPS:
                        step(k, i)
                for k in LAST_STEPS:
                    step(k)
                for c in range(FFN_STEPS, NFC):
                    down(c, stop=c == NFC - 1)

            mm = nc.tensor.matmul

            def attention_level(lev, src, k):
                at = 9 * (k - 1) + lev
                if lev:
                    need(pe, "gla_qk", 8 * (k - 1) + lev)
                    q_of, k_of = q_dec[(lev - 1) % 2], k_dec[(lev - 1) % 2]
                else:
                    q_of, k_of = src["q"], src["k"]
                if lev >= 2:
                    need(pe, "sc_out", at - 1)
                b = 2 * (lev % 2)
                for j in range(2):
                    rows = slice(HD * j, HD * j + HD)
                    for c in range(2):
                        if lev == 8:
                            ins = mm(ps[:, b + j, c * P:c * P + P], k_of[rows, c, 0:P], q_of[rows, c, P:], start=True, stop=True)
                            continue
                        for t in range(TB):
                            cols = slice(t * P, t * P + P)
                            ins = mm(ps[:, b + j, (2 * c + t) * P:(2 * c + t + 1) * P], k_of[rows, c, cols],
                                     q_of[rows, c, cols], start=True, stop=True)
                ins.then_inc(ev["sc_done"], 1)

            def to_rows(src, b, name):
                for t in range(TB):
                    for c in range(2):
                        ins = nc.tensor.transpose(bank(b)[:, t, c * P:c * P + P], src[:, c, t * P:t * P + P], const("ident"))
                ins.then_inc(ev[name], 1)

            def attend(k):
                need(pe, "sc_out", 9 * k)
                for c in range(2):
                    for j in range(2):
                        rows = slice(HD * j, HD * j + HD)
                        cols = slice(c * P + j * HD, c * P + j * HD + HD)
                        m = 4 * j + 2 * c
                        mm(bank(2)[rows, c, 0:P], v_rows[:, 0, cols], scores[:, m, :], start=True, stop=True)
                        mm(bank(2)[rows, c, P:], v_rows[:, 0, cols], scores_far[:, 2 * j + c, :], start=True, stop=False)
                        ins = mm(bank(2)[rows, c, P:], v_rows[:, 1, cols], scores[:, m + 1, :], start=False, stop=True)
                ins.then_inc(ev["o_done"], 1)

            def attend_norm(k, per_head):
                need(pe, "o_sq", k)
                if per_head:
                    ins = mm(ps[:, 3, :], const("head_ones"), flat(tmp), start=True, stop=True)
                else:
                    mm(bank(3)[:, 0, :], const("all_ones"), tmp2[:, 0, :], start=True, stop=False)
                    ins = mm(bank(3)[:, 0, :], const("all_ones"), tmp2[:, 1, :], start=False, stop=True)
                ins.then_inc(ev["on_done"], 1)

            def projections(n0, g, total, spare):
                before = taken[0]
                taken[0] += total
                todo = iter(range(4, total))
                feature_tiles([(n0 + i, ps[:, 4 + i, 0:SEQ], True, True) for i in range(4)], after_norm=g,
                              between=(5, total_squares))

                def tile(count=1):
                    for _ in range(count):
                        i = next(todo)
                        if tile_before(i, spare):
                            need(pe, "proj_out", before + tile_before(i, spare))
                        feature_tile(n0 + i, ps[:, tile_bank(i, spare), 0:SEQ])
                return tile

            taken = [0]

            def mixer_one():
                tile = projections(FIRST["mix_in"], 1, 27, MIX_SPARE)
                tile()
                need(pe, "proj_out", 1)
                for c in range(2):
                    ins = mm(bank(3)[:, c, :], const("gla_w2")[0:32, c * P:c * P + P], ga_sb[0:32, :], start=True, stop=True)
                ins.then_inc(ev["gla_z"], 1)
                tile(3)
                need(pe, "proj_out", 7)
                to_rows(gla_in["v"], 2, "vt_done")
                need(pe, "gla_abs", 1)
                need(pe, "vt_out", 1)
                for lev in range(9):
                    attention_level(lev, gla_in, 1)
                    tile()
                attend(1)
                tile()
                attend_norm(1, True)
                tile()
                to_rows(hgrn_in["v"], 2, "vt_done")
                tile()
                need(pe, "hg_ready", 1)
                need(pe, "on_root", 1)
                for lev in range(9):
                    attention_level(lev, hgrn_in, 2)
                    if lev < 7:
                        tile()
                attend(2)
                attend_norm(2, False)
                rwkv()
                mix_rows(6, 8)

            def mix_rows(first, end):
                for step in range(first, end):
                    i = (0, 1, 2, 3, 6, 7, 4, 5)[step]
                    need(pe, "y_ready", 6 + max(0, step - 5))
                    add_block(FIRST["mix_out"] + step, y_hi[:, i, :], y_lo[:, i, :], start=step == 0, stop=step == 7)

            def rwkv():
                need(pe, "proj_out", 27)
                need(pe, "rw_kk_sq", 1)
                mm(ps[:, 4, :], const("head_ones"), flat(sq), start=True, stop=True).then_inc(ev["rw_kk_n"], 1)
                need(pe, "rw_lora_in", 1)
                for c in range(2):
                    cols = slice(c * P, c * P + P)
                    mm(bank(1)[:, c, :], const("w2a2")[64:128, cols], rw[64:128, 6, :], start=True, stop=True)
                    mm(bank(0)[:, c, :], const("w2a2")[0:64, cols], lora[0:64, 0, :], start=True, stop=True)
                    ins = mm(bank(2)[:, c, :], const("g2")[:, cols], lora[:, 1, :], start=True, stop=True)
                ins.then_inc(ev["rw_lora"], 1)
                for i, src in enumerate((a_dec, b_last, k_last)):
                    need(pe, "rw_dec", i + 1)
                    if i == 0:
                        need(pe, "rw_kk_root", 1)
                    to_rows(src, 4 + i, "rw_tok")
                to_rows(rw[:, 4:6, :], 7, "rw_tok")
                need(pe, "rw_bonus_in", 1)
                need(pe, "on_root", 2)
                mm(ps[:, 3, :], const("head_ones"), flat(sq), start=True, stop=True).then_inc(ev["rw_bonus"], 1)

                def products(b, lhs, rhs):
                    for j in range(2):
                        rows = slice(HD * j, HD * j + HD)
                        for c in range(2):
                            for t in range(TB):
                                cols = slice(t * P, t * P + P)
                                ins = mm(ps[:, b + j, (2 * c + t) * P:(2 * c + t + 1) * P], lhs[rows, c, cols],
                                         rhs[rows, c, cols], start=True, stop=True)
                    ins.then_inc(ev["rw_mat"], 1)
                need(pe, "rw_g", 1)
                products(0, b_dec, a_dec)
                need(pe, "rw_tok_out", 1)
                need(pe, "rw_tok_act", 2)
                need(pe, "pool_ready", 1)
                for c in range(2):
                    ins = mm(bank(7)[:, c, :], const("pool_w", c, P), tmp[:, c, :], start=True, stop=True)
                ins.then_inc(ev["pool_done"], 1)
                products(4, a_dec, b_dec)
                need(pe, "rw_mat_out", 1)
                products(0, kk_dec, a_dec)
                products(2, b_dec, r_dec)
                need(pe, "rw_mat_out", 3)
                products(0, kk_dec, r_dec)
                for c in range(2):
                    for j in range(2):
                        cols = slice(c * P + j * HD, c * P + j * HD + HD)
                        for t in range(TB):
                            ins = mm(bank(6)[:, t, cols], lak_t[:, 4 * j + 2 * c + t, :], v_tok[:, t, cols],
                                     start=True, stop=True)
                ins.then_inc(ev["rw_lv"], 1)
                need(pe, "rw_mat_out", 5)
                for lev in range(1, 6):
                    for j in range(2):
                        need(pe, "rw_z_out", 1 if lev == 1 else 2 * (lev - 2) + j + 2)
                        for m in range(4):
                            ins = mm(bank(j, 4)[:, m, :], l_t[:, 4 * j + m, :], inv[:, 4 * j + m, :], start=True, stop=True)
                        ins.then_inc(ev["rw_y"], 1)
                    for j in range(2):
                        need(pe, "rw_ym", 2 * (lev - 1) + j + 1)
                        for m in range(4):
                            if lev < 5:
                                mm(bank(2 + j, 4)[:, m, :], inv_t[:, 4 * j + m, :], y_m[:, 4 * j + m, :], start=True, stop=True)
                            ins = mm(bank(4 + j, 4)[:, m, :], y_m[:, 4 * j + m, :], inv_t[:, 4 * j + m, :], start=True, stop=True)
                        ins.then_inc(ev["rw_z"], 1)
                need(pe, "rw_z_out", 11)
                for c in range(2):
                    for j in range(2):
                        cols = slice(c * P + j * HD, c * P + j * HD + HD)
                        for t in range(TB):
                            ins = mm(bank(0)[HD * j:HD * j + HD, c, t * P:t * P + P], a_tok[:, t, cols],
                                     inv_t[:, 4 * j + 2 * c + t, :], start=True, stop=True)
                ins.then_inc(ev["rw_wt"], 1)
                need(pe, "rw_lv_out", 1)
                for c in range(2):
                    for j in range(2):
                        cols = slice(c * P + j * HD, c * P + j * HD + HD)
                        for t in range(TB):
                            ins = mm(bank(1)[:, t, cols], inv_t[:, 4 * j + 2 * c + t, :], lv[:, t, cols], start=True, stop=True)
                ins.then_inc(ev["rw_ut"], 1)
                need(pe, "rw_wu_out", 1)
                for q in range(NCH):
                    rows, t = slice(CHUNK * (q % 2), CHUNK * (q % 2) + CHUNK), q // 2
                    if q:
                        need(pe, "rw_st_out", q)
                        for c in range(2):
                            ins = mm(ps[rows, 2 + q % 2, c * P:c * P + P], w_t[:, c, q * CHUNK:(q + 1) * CHUNK],
                                     state[q][:, c, :], start=True, stop=True)
                        ins.then_inc(ev["rw_u"], 1)
                    need(pe, "rw_u_out", q + 1)
                    if q + 1 < NCH:
                        for c in range(2):
                            cols = slice(c * P, c * P + P)
                            mm(ps[:, 4 + q % 2, cols], b_tok[rows, t, cols], u[rows, t, cols], start=True, stop=False)
                            ins = mm(ps[:, 4 + q % 2, cols], k_tok[rows, t, cols], v_tok[rows, t, cols], start=False, stop=True)
                        ins.then_inc(ev["rw_st"], 1)
                for c in range(2):
                    for q in range(NCH):
                        t, tok = q // 2, slice(q * CHUNK, (q + 1) * CHUNK)
                        if q:
                            mm(bank(6)[:, c, tok], state[q][:, c, :], r_dec[:, c, tok], start=True, stop=False)
                        for j in range(2):
                            rows = slice(HD * j, HD * j + HD)
                            cols = slice(c * P + j * HD, c * P + j * HD + HD)
                            m, own = 4 * j + 2 * c + t, slice((q % 2) * CHUNK, (q % 2) * CHUNK + CHUNK)
                            mm(bank(6)[rows, c, tok], u[:, t, cols], mrb_t[:, m, own], start=q == 0, stop=False)
                            ins = mm(bank(6)[rows, c, tok], v_tok[:, t, cols], mrk_t[:, m, own], start=False, stop=True)
                ins.then_inc(ev["rw_o"], 1)
                mix_rows(0, 1)
                need(pe, "rw_o_out", 1)
                mm(ps[:, 4, :], const("head_ones"), flat(o_r), start=True, stop=True).then_inc(ev["rw_mean"], 1)
                mix_rows(1, 2)
                need(pe, "rw_dev", 1)
                mm(ps[:, 5, :], const("head_ones"), flat(t_r), start=True, stop=True).then_inc(ev["rw_var"], 1)
                mix_rows(2, 6)

            def lru():
                before = taken[0]
                projections(FIRST["lru_in"], 4, KD, LRU_SPARE)(KD - 4)
                n0 = FIRST["lru_gates"]
                for b in range(4):
                    n = n0 + b
                    need(pe, "lru_conv", 2 * b + 2)
                    pe.wait_ge(lo_ready[slot(n)], nth(n))
                    for half in range(2):
                        i = 2 * b + half
                        need(pe, *(("proj_out", before + i + 1) if i < 4 else ("lru_ri", i - 3)))
                        for gate in range(2):
                            where = bank(4 + i % 4)[:, gate, :]
                            for k in range(2):
                                at = ((half * 2 + gate) * 2 + k) * P
                                wh, wl = (w[:, slot(n), at:at + P] for w in (w_hi, w_lo))
                                mm(where, wh, y_hi[:, 2 * b + k, :], start=k == 0, stop=False)
                                mm(where, wh, y_lo[:, 2 * b + k, :], start=False, stop=False)
                                ins = mm(where, wl, y_hi[:, 2 * b + k, :], start=False, stop=k == 1)
                        ins.then_inc(used[slot(n)] if half else ev["lru_gates_done"], 1)
                taken[0] += KD
                for i in range(KD):
                    need(pe, "proj_out", before + 4 + i + 1)
                    feature_tile(FIRST["lru_branch"] + i, ps[:, i % 4, 0:SEQ])
                need(pe, "proj_out", before + 2 * KD)
                for i in range(KD):
                    n = FIRST["lru_out"] + i
                    need(pe, "y_ready", 8 + i + 1)
                    add_block(n, y_hi[:, i, :], y_lo[:, i, :], start=i == 0, stop=i == KD - 1)

            def heads_squares(k, a):
                need(pe, "heads_sq", 4 * (k - 1) + a + 1)
                if a >= 2 and k == 2:
                    need(pe, "heads_root", 4 + a - 1)
                mm(ps[:, 4 + a if k == 1 else 2 + a % 2, :], const("head_ones"), flat(sq_heads[a]), start=True, stop=True)\
                    .then_inc(ev["heads_n"], 1)

            def shared_kv():
                n0 = FIRST["kv"]
                before = taken[0]
                tile = projections(n0, 6, KD, HEADS_SPARE)
                tile(2)
                pe.wait_ge(rstd_ready, norms[0])
                for t in range(TB):
                    ins = mm(ps[:, 3, t:t + 1], rstd[0:1, t * P:t * P + P], const("all_ones")[0:1, 0:1], start=True, stop=True)
                ins.then_inc(ev["col_done"], 1)
                tile(2)
                need(pe, "col_out", 1)
                need(pe, "proj_out", before + 6)
                for k in range(KD):
                    rows_tile(n0 + KD + k, xn_hi[:, k, :], xn_lo[:, k, :], start=k == 0, stop=k == KD - 1)
                    if 1 <= k < 5:
                        need(pe, "proj_out", before + KD)
                        heads_squares(1, k - 1)

            def attention():
                n0 = FIRST["q_in"]
                tile = projections(n0, 8, KD, HEADS_SPARE)
                tile(2)
                heads_squares(2, 0)
                tile()
                heads_squares(2, 1)
                tile()
                heads_squares(2, 2)
                heads_squares(2, 3)

                def logits(c):
                    need(pe, "heads_ready", 4 + c // 2 + 1)
                    if c == 1:
                        need(pe, "heads_root", 8)
                    if c >= 2:
                        need(pe, "at_sig", c - 1)
                    for j in range(2):
                        rows, b = slice(HD * j, HD * j + HD), 2 * (c % 2) + j
                        mm(ps[:, b, 0:2 * P], q_t[rows, c, P:], k_t[rows, c, :], start=True, stop=True)
                        ins = mm(ps[:, b, 2 * P:3 * P], q_t[rows, c, 0:P], k_t[rows, c, 0:P], start=True, stop=True)
                    ins.then_inc(ev["at_z"], 1)
                logits(0)
                logits(1)
                for c in range(KD):
                    need(pe, "at_w", c + 1)
                    if c:
                        need(pe, "at_wt_out", c)
                    for j in range(2):
                        for m in range(3):
                            ins = nc.tensor.transpose(ps[:, 4 + j, m * P:m * P + P], weights[c % 2][:, 3 * j + m, :], const("ident"))
                    ins.then_inc(ev["at_wt"], 1)
                    if c + 2 < KD:
                        logits(c + 2)
                    need(pe, "at_wt_out", c + 1)
                    if c >= 2:
                        need(pe, "y_ready", 16 + c - 1)
                    for j in range(2):
                        rows, cols = slice(HD * j, HD * j + HD), slice(c * P + HD * j, c * P + HD * j + HD)
                        o, w = bank(6 + c % 2)[rows, 0, :], weights_t[c % 2]
                        mm(o[:, P:], v_heads[:, 0, cols], w[:, 3 * j, :], start=True, stop=False)
                        mm(o[:, P:], v_heads[:, 1, cols], w[:, 3 * j + 1, :], start=False, stop=True)
                        ins = mm(o[:, 0:P], v_heads[:, 0, cols], w[:, 3 * j + 2, :], start=True, stop=True)
                    ins.then_inc(ev["at_o"], 1)
                for i in range(KD):
                    need(pe, "y_ready", 16 + i + 1)
                    add_block(FIRST["attn_out"] + i, y_hi[:, i, :], y_lo[:, i, :], start=i == 0, stop=i == KD - 1)

            steps = [
                lambda: None,
                lambda: ffn(0, 0, FIRST["ffn_a"]),
                lambda: (pe.wait_ge(const_loaded, 16), mixer_one()),
                lambda: None,
                lambda: ffn(1, 2, FIRST["ffn_b"]),
                lambda: None,
                lambda: ffn(2, 3, FIRST["ffn_c"], lambda: total_squares(True)),
                lambda: lru(),
                lambda: ffn(3, 5, FIRST["ffn_d"]),
                lambda: shared_kv(),
                lambda: ffn(4, 7, FIRST["ffn_e"], lambda: need(pe, "v_out", 1), halves=(y_hi, y_lo)),
                lambda: attention(),
                lambda: ffn(5, 9, FIRST["ffn_f"]),
            ]
            for step in steps:
                step()


def lay_out(inp):
    import numpy as np

    def features(w, cols=None):
        w = np.asarray(w)
        m = w.shape[1] // P
        return w.reshape(KD, P, m, P).transpose(2, 1, 0, 3).reshape(m, P, BLK)

    def rows(w):
        return np.asarray(w).reshape(-1, P, BLK)

    def ffn(w_in, w_out):
        w_in, w_out = np.asarray(w_in), np.asarray(w_out)
        gate, up, down = features(w_in[:, :FF]), features(w_in[:, FF:]), rows(w_out)
        return np.stack([gate, up, down], 1).reshape(-1, P, BLK)[[which for _, which in FFN_ORDER]]

    w_in, w_out = np.asarray(inp["w_in"][0]), np.asarray(inp["w_out"][0])
    pool, hg, rw, gl = w_in[:, :G], w_in[:, G:5 * G], w_in[:, 5 * G:9 * G], w_in[:, 9 * G:]
    ga = np.zeros((D, P), np.float32)
    ga[:, :16] = gl[:, 4 * G:]
    mix_in = np.concatenate([ga, gl[:, :4 * G], hg[:, G:2 * G], hg[:, :G], hg[:, 2 * G:], pool, rw], 1)
    wr = np.asarray(inp["a_w_r_2"][0])
    wi = np.asarray(inp["a_w_i_2"][0])
    lru = np.stack([wr, wi], 1).reshape(4, 2, 2, P, 2, P).transpose(0, 3, 4, 1, 2, 5).reshape(4, P, BLK)
    a_in = np.asarray(inp["a_w_in_2"][0])
    a_in = np.concatenate([a_in[:, D:], a_in[:, :D]], 1)
    w_kv = np.asarray(inp["w_kv_2"])
    w13, w2 = inp["ffn1_w13_2"], inp["ffn1_w2_2"]
    v13, v2 = inp["ffn2_w13_2"], inp["ffn2_w2_2"]
    blocks = np.concatenate([
        ffn(inp["ffn1_w_in"][0], inp["ffn1_w_out"][0]), features(mix_in), rows(w_out)[[0, 1, 2, 3, 6, 7, 4, 5]],
        ffn(inp["ffn2_w_in"][0], inp["ffn2_w_out"][0]), ffn(w13[0], w2[0]),
        features(a_in[:, :D]), lru, features(a_in[:, D:]), rows(inp["a_w_out_2"][0]), ffn(v13[0], v2[0]),
        features(w_kv[:, :D]), rows(w_kv[:, D:]), ffn(w13[1], w2[1]),
        features(inp["b_w_q_2"][0]), rows(inp["b_w_o_2"][0]), ffn(v13[1], v2[1])])
    assert blocks.shape == (NBLK, P, BLK)

    cst = np.zeros((P, NCONST), np.float32)

    def put(name, a):
        at, w = CONST_AT[name]
        a = np.asarray(a)
        cst[:a.shape[0], at:at + w] = a.reshape(a.shape[0], w)

    def columns(a):
        return np.asarray(a).reshape(-1, P).T

    for name, a in [("g_ffn_a", inp["norm_ffn1"][0]), ("g_mix", inp["norm_mix"][0]), ("g_ffn_b", inp["norm_ffn2"][0]),
                    ("g_ffn_c", inp["ffn1_norm_2"][0]), ("g_lru", inp["mix_norm_2"][0]), ("g_ffn_d", inp["ffn2_norm_2"][0]),
                    ("g_kv", inp["kv_norm_2"]), ("g_ffn_e", inp["ffn1_norm_2"][1]), ("g_attn", inp["mix_norm_2"][1]),
                    ("g_ffn_f", inp["ffn2_norm_2"][1]),
                    ("g_final", inp["norm_final"]), ("lb_logits", inp["hgrn_lb_logits"][0]),
                    ("hgrn_norm", inp["hgrn_norm"][0]), ("mu", inp["rwkv_mu"][0]), ("w0", inp["rwkv_w0"][0]),
                    ("a0", inp["rwkv_a0"][0]), ("k_k", inp["rwkv_k_k"][0]), ("k_a", inp["rwkv_k_a"][0]),
                    ("r_k", inp["rwkv_r_k"][0]), ("ln_w", inp["rwkv_ln_w"][0]), ("ln_b", inp["rwkv_ln_b"][0]),
                    ("gla_b", inp["gla_b"][0]), ("gla_norm", inp["gla_norm"][0]), ("pool_b", inp["pool_b"][0]),
                    ("pool_scale", inp["pool_scale"][0]), ("conv_w", inp["a_conv_w_2"][0]), ("conv_b", inp["a_conv_b_2"][0]),
                    ("b_r", inp["a_b_r_2"][0]), ("b_i", inp["a_b_i_2"][0]), ("lam", inp["a_lambda_2"][0])]:
        put(name, columns(a))
    put("k_norm", np.concatenate([np.asarray(inp["k_norm_2"])] * 2)[:, None])
    put("q_norm", np.concatenate([np.asarray(inp["q_norm_2"][0])] * 2)[:, None])
    put("w2a2", np.concatenate([np.asarray(inp["rwkv_w2"][0]), np.asarray(inp["rwkv_a2"][0])]))
    put("g2", np.asarray(inp["rwkv_g2"][0]))
    put("gla_w2", np.asarray(inp["gla_w2"][0]))
    pool_w = np.zeros((P, 2, P), np.float32)
    for g in range(4):
        rows_g = slice(HD * (g % 2), HD * (g % 2) + HD)
        pool_w[rows_g, g // 2, rows_g] = np.asarray(inp["pool_w"][0])[g]
    put("pool_w", pool_w)
    s, t = np.arange(P)[:, None], np.arange(P)[None, :]
    put("ident", s == t)
    put("head_ones", s // HD == t // HD)
    put("all_ones", np.ones((P, P)))
    put("norm_eps", np.full((P, 1), NORM_EPS))
    put("gn_eps", np.full((P, 1), RWKV_GN_EPS))
    levels = [s == t] + [(t // n == s // n + 1) & (t // n % 2 == 1) for n in (1, 2, 4, 8, 16, 32, 64)]
    put("level", np.concatenate(levels, 1))
    put("level_low", np.concatenate([m.T for m in levels[1:7]], 1))
    same = s // CHUNK == t // CHUNK
    put("strict_up", same & (s < t))
    put("incl_up", same & (s <= t))
    put("strict_low", same & (s > t))
    put("not_before", np.where(t >= s, np.float32(MASKED_OUT), np.float32(0)))
    windows = np.array([2, 4, 8, 16])[np.arange(G) // HD]
    inv = np.float32(1) / np.minimum(np.arange(SEQ)[None, :] + 1, windows[:, None]).astype(np.float32)
    put("inv_count", inv.reshape(2, P, SEQ).transpose(1, 0, 2))
    one = np.zeros((P, 8, 65), np.float32)
    one[:, :, 0] = 1
    put("scan_one", one)
    x = np.asarray(inp["x"]).reshape(SEQ, KD, P).transpose(2, 1, 0)
    assert NBLK == len(blocks)
    return {"x_in": x, "blocks": blocks, "consts": cst}


def kernel(**inputs):
    import numpy as _np
    import concourse.bacc as _bacc
    from concourse import mybir as _mybir
    from concourse.bass_utils import run_bass_kernel_spmd as _run

    nc = _bacc.Bacc("TRN2", target_bir_lowering=False, num_devices=1)
    arrays = {name: _np.ascontiguousarray(a) for name, a in lay_out(inputs).items()}
    args = [nc.dram_tensor(name, a.shape, _mybir.dt.from_np(a.dtype), kind="ExternalInput").ap()
            for name, a in arrays.items()]
    out = nc.dram_tensor("out", (P, KD, SEQ), _mybir.dt.float32, kind="ExternalOutput").ap()
    build(nc, *args, out)
    r = _run(nc, [arrays], core_ids=[0])
    return _np.ascontiguousarray(_np.asarray(r.results[0]["out"]).transpose(2, 1, 0)).reshape(1, SEQ, D)
```
